# Optimizing a Trainium2 kernel written in Bass

```python
import math
import jax, jax.numpy as jnp
from jax import lax
import numpy as np

D_MODEL = 1024
BATCH = 1
SEQ = 256
DEPTH = 2

CHUNK = 64
Q_BLOCK = 128
MEM_LEN = 256
D_MIX = D_MODEL
DIFF_HEADS = 4
DIFF_HEAD_DIM = 64
DIFF_V_DIM = 2 * DIFF_HEAD_DIM
D_DIFF_QK = DIFF_HEADS * 2 * DIFF_HEAD_DIM
D_DIFF = DIFF_HEADS * DIFF_V_DIM
MLSTM_HEADS = 4
MLSTM_HEAD_DIM = 64
D_MLSTM = MLSTM_HEADS * MLSTM_HEAD_DIM
CONV_WIDTH = 4
S5_GROUP = 16
D_S5 = D_MIX - D_DIFF - D_MLSTM
S5_GROUPS = D_S5 // S5_GROUP
S5_STATE = 64
XATTN_HEADS = 4
D_FF = 2816
ROPE_THETA = 10000.0
LN_EPS = 1e-5
DN_ALPHA = (2 * DEPTH) ** 0.25
DN_BETA = (8 * DEPTH) ** -0.25
IN_WIDTHS = (D_DIFF_QK, D_DIFF_QK, D_DIFF,
             D_MLSTM, D_MLSTM, D_MLSTM, D_MLSTM,
             MLSTM_HEADS, MLSTM_HEADS,
             D_S5)
D_IN = sum(IN_WIDTHS)

kernel_name = "hybrid_diffattn_mlstm_s5_streaming_encoder"

def split_columns(t, widths):
    out, start = [], 0
    for w in widths:
        out.append(t[..., start:start + w])
        start += w
    return out

def layer_norm(x, g, b):
    xf = x.astype(jnp.float32)
    mu = jnp.mean(xf, -1, keepdims=True)
    var = jnp.mean(jnp.square(xf - mu), -1, keepdims=True)
    y = (xf - mu) * lax.rsqrt(var + LN_EPS)
    return (y * g.astype(jnp.float32) + b.astype(jnp.float32)).astype(x.dtype)

def rms_norm(x, g):
    xf = x.astype(jnp.float32)
    y = xf * lax.rsqrt(jnp.mean(xf * xf, -1, keepdims=True) + LN_EPS)
    return (y * g.astype(jnp.float32)).astype(x.dtype)

def swiglu(x, w_gate, w_up, w_down):
    return (jax.nn.silu(x @ w_gate) * (x @ w_up)) @ w_down

def rope_tables(seq):
    pos = jnp.arange(seq, dtype=jnp.float32)
    inv = ROPE_THETA ** (-jnp.arange(0, DIFF_HEAD_DIM, 2, dtype=jnp.float32) / DIFF_HEAD_DIM)
    ang = pos[:, None] * inv[None, :]
    return jnp.cos(ang), jnp.sin(ang)

def apply_rope(t, cos, sin):
    t1, t2 = jnp.split(t, 2, axis=-1)
    c = cos[None, :, None, None, :]
    s = sin[None, :, None, None, :]
    return jnp.concatenate([t1 * c - t2 * s, t2 * c + t1 * s], -1).astype(t.dtype)

def diff_attention(q, k, v, lam):
    b_, s_ = q.shape[:2]
    nqb = s_ // Q_BLOCK
    scale = DIFF_HEAD_DIM ** -0.5
    k_chunk = jnp.arange(s_) // CHUNK
    qb = jnp.moveaxis(q.reshape(b_, nqb, Q_BLOCK, DIFF_HEADS, 2, DIFF_HEAD_DIM), 1, 0)

    def block(args):
        j, qj = args
        q_chunk = (j * Q_BLOCK + jnp.arange(Q_BLOCK)) // CHUNK
        allowed = k_chunk[None, :] <= q_chunk[:, None]
        s = jnp.einsum('bqhmd,bkhmd->bhmqk', qj, k).astype(jnp.float32) * scale
        s = jnp.where(allowed, s, -jnp.inf)
        p = jax.nn.softmax(s, axis=-1)
        a = p[:, :, 0] - lam * p[:, :, 1]
        return jnp.einsum('bhqk,bkhe->bqhe', a.astype(v.dtype), v)

    out = lax.map(block, (jnp.arange(nqb), qb))
    return jnp.moveaxis(out, 0, 1).reshape(b_, s_, DIFF_HEADS, DIFF_V_DIM)

def causal_conv(x, w, b):
    kw = w.shape[0]
    s_ = x.shape[1]
    xp = jnp.pad(x, ((0, 0), (kw - 1, 0), (0, 0)))
    y = xp[:, 0:s_] * w[0]
    for j in range(1, kw):
        y = y + xp[:, j:j + s_] * w[j]
    return y + b

def mlstm_chunkwise(q, k, v, ig, lf):
    b_, s_, h_, d_ = q.shape
    nc = s_ // CHUNK
    tril = jnp.tril(jnp.ones((CHUNK, CHUNK), bool))

    def to_chunks(t):
        return jnp.moveaxis(t.reshape((b_, nc, CHUNK) + t.shape[2:]), 1, 0)

    def step(carry, xs):
        c_st, n_st, m_st = carry
        qc, kc, vc, ic, fc = xs
        bcum = jnp.cumsum(fc, axis=1)
        b_last = bcum[:, -1]
        log_d = bcum[:, :, None, :] - bcum[:, None, :, :] + ic[:, None, :, :]
        log_d = jnp.where(tril[None, :, :, None], log_d, -jnp.inf)
        log_inter = bcum + m_st[:, None, :]
        m_t = jnp.maximum(log_inter, jnp.max(log_d, axis=2))
        dmat = jnp.exp(log_d - m_t[:, :, None, :])
        scores = jnp.einsum('bthd,bshd->btsh', qc, kc) * dmat
        inter = jnp.exp(log_inter - m_t)
        num = (jnp.einsum('btsh,bshd->bthd', scores, vc)
               + inter[..., None] * jnp.einsum('bhvk,bthk->bthv', c_st, qc))
        den = jnp.sum(scores, axis=2) + inter * jnp.einsum('bhk,bthk->bth', n_st, qc)
        den = jnp.maximum(jnp.abs(den), jnp.exp(-m_t))
        h = num / den[..., None]
        m_new = jnp.maximum(b_last + m_st, jnp.max(b_last[:, None] - bcum + ic, axis=1))
        w = jnp.exp(b_last[:, None] - bcum + ic - m_new[:, None])
        decay = jnp.exp(b_last + m_st - m_new)
        c_new = decay[..., None, None] * c_st + jnp.einsum('bshv,bshk->bhvk', vc * w[..., None], kc)
        n_new = decay[..., None] * n_st + jnp.einsum('bsh,bshk->bhk', w, kc)
        return (c_new, n_new, m_new), h

    init = (jnp.zeros((b_, h_, d_, d_), jnp.float32),
            jnp.zeros((b_, h_, d_), jnp.float32),
            jnp.zeros((b_, h_), jnp.float32))
    _, h = lax.scan(step, init, tuple(to_chunks(t) for t in (q, k, v, ig, lf)))
    return jnp.moveaxis(h, 0, 1).reshape(b_, s_, h_, d_)

def s5_layer(u, a_re, a_im, log_step, b_re, b_im, c_re, c_im, d_skip, glu_w, glu_b):
    b_, s_, _ = u.shape
    f32 = jnp.float32
    uf = u.astype(f32).reshape(b_, s_, S5_GROUPS, S5_GROUP)
    lam = lax.complex(a_re.astype(f32), a_im.astype(f32))
    step = jnp.exp(log_step.astype(f32))[:, None]
    lam_bar = jnp.exp(lam * step)
    b_mat = lax.complex(b_re.astype(f32), b_im.astype(f32))
    b_bar = ((lam_bar - 1.0) / lam)[..., None] * b_mat
    bu = jnp.einsum('bsgc,gpc->bsgp', uf.astype(jnp.complex64), b_bar)

    def combine(left, right):
        a_l, x_l = left
        a_r, x_r = right
        return a_r * a_l, a_r * x_l + x_r

    a_seq = jnp.broadcast_to(lam_bar, (s_,) + lam_bar.shape)[None]
    _, states = lax.associative_scan(combine, (a_seq, bu), axis=1)
    c_mat = lax.complex(c_re.astype(f32), c_im.astype(f32))
    y = (jnp.einsum('bsgp,gcp->bsgc', states, c_mat).real
         + d_skip.astype(f32).reshape(S5_GROUPS, S5_GROUP) * uf)
    y = jax.nn.gelu(y.reshape(b_, s_, D_S5))
    y = y * jax.nn.sigmoid(y @ glu_w.astype(f32) + glu_b.astype(f32))
    return y.astype(u.dtype)

def hybrid_mix(x, cos, sin, lambda_init, w_in, conv_w, conv_b, mlstm_gate_b, mlstm_norm_g,
               diff_lambda, diff_norm_g, s5_a_re, s5_a_im, s5_log_step, s5_b_re, s5_b_im,
               s5_c_re, s5_c_im, s5_d, s5_glu_w, s5_glu_b, w_out):
    b_, s_, _ = x.shape
    f32 = jnp.float32
    proj = x @ w_in
    dq, dk, dv, mq, mk, mv, mo, mi, mf, su = split_columns(proj, IN_WIDTHS)

    dq = apply_rope(dq.reshape(b_, s_, DIFF_HEADS, 2, DIFF_HEAD_DIM), cos, sin)
    dk = apply_rope(dk.reshape(b_, s_, DIFF_HEADS, 2, DIFF_HEAD_DIM), cos, sin)
    dv = dv.reshape(b_, s_, DIFF_HEADS, DIFF_V_DIM)
    lq1, lk1, lq2, lk2 = [diff_lambda[i].astype(f32) for i in range(4)]
    lam = jnp.exp(jnp.sum(lq1 * lk1)) - jnp.exp(jnp.sum(lq2 * lk2)) + lambda_init
    a_out = diff_attention(dq, dk, dv, lam)
    a_out = rms_norm(a_out, diff_norm_g) * (1.0 - lambda_init)
    a_out = a_out.reshape(b_, s_, D_DIFF).astype(x.dtype)

    qk = jax.nn.silu(causal_conv(jnp.concatenate([mq, mk], -1), conv_w, conv_b))
    mq, mk = qk[..., :D_MLSTM], qk[..., D_MLSTM:]
    shp = (b_, s_, MLSTM_HEADS, MLSTM_HEAD_DIM)
    q = mq.reshape(shp).astype(f32)
    k = mk.reshape(shp).astype(f32) * (MLSTM_HEAD_DIM ** -0.5)
    v = mv.reshape(shp).astype(f32)
    gb = mlstm_gate_b.astype(f32)
    ig = mi.astype(f32) + gb[:MLSTM_HEADS]
    lf = jax.nn.log_sigmoid(mf.astype(f32) + gb[MLSTM_HEADS:])
    h = mlstm_chunkwise(q, k, v, ig, lf)
    h = rms_norm(h, mlstm_norm_g.reshape(MLSTM_HEADS, MLSTM_HEAD_DIM))
    b_out = (jax.nn.sigmoid(mo.astype(f32)) * h.reshape(b_, s_, D_MLSTM)).astype(x.dtype)

    c_out = s5_layer(su, s5_a_re, s5_a_im, s5_log_step, s5_b_re, s5_b_im,
                     s5_c_re, s5_c_im, s5_d, s5_glu_w, s5_glu_b)

    return jnp.concatenate([a_out, b_out, c_out.astype(x.dtype)], -1) @ w_out

def memory_cross_attention(x, mem, wq, wkv, wo):
    b_, s_, _ = x.shape
    m_ = mem.shape[1]
    hd = D_MODEL // XATTN_HEADS
    q = (x @ wq).reshape(b_, s_, XATTN_HEADS, hd)
    kv = mem @ wkv
    k = kv[..., :D_MODEL].reshape(b_, m_, XATTN_HEADS, hd)
    v = kv[..., D_MODEL:].reshape(b_, m_, XATTN_HEADS, hd)
    s = jnp.einsum('bqhd,bmhd->bhqm', q, k).astype(jnp.float32) * (hd ** -0.5)
    p = jax.nn.softmax(s, axis=-1).astype(v.dtype)
    o = jnp.einsum('bhqm,bmhd->bqhd', p, v).reshape(b_, s_, D_MODEL)
    return o @ wo

def setup_inputs(seed: int = 0) -> dict:
    key = jax.random.key(seed)
    ks = iter(jax.random.split(key, 40))
    f32 = jnp.float32

    def normal(shape, scale):
        return scale * jax.random.normal(next(ks), shape, f32)

    x = normal((BATCH, SEQ, D_MODEL), 1.0)
    mem = normal((BATCH, MEM_LEN, D_MODEL), 1.0)
    ffn_w_gate = normal((DEPTH, 2, D_MODEL, D_FF), D_MODEL ** -0.5)
    ffn_w_up = normal((DEPTH, 2, D_MODEL, D_FF), D_MODEL ** -0.5)
    ffn_w_down = normal((DEPTH, 2, D_FF, D_MODEL), DN_BETA * D_FF ** -0.5)
    ln_g = 1.0 + normal((DEPTH, 4, D_MODEL), 0.02)
    ln_b = normal((DEPTH, 4, D_MODEL), 0.02)
    w_in = normal((DEPTH, D_MODEL, D_IN), D_MODEL ** -0.5)
    conv_w = normal((DEPTH, CONV_WIDTH, 2 * D_MLSTM), CONV_WIDTH ** -0.5)
    conv_b = normal((DEPTH, 2 * D_MLSTM), 0.02)
    f_bias = jnp.linspace(3.0, 6.0, MLSTM_HEADS, dtype=f32)
    mlstm_gate_b = jnp.concatenate([normal((DEPTH, MLSTM_HEADS), 0.1),
                                    f_bias + normal((DEPTH, MLSTM_HEADS), 0.1)], -1)
    mlstm_norm_g = 1.0 + normal((DEPTH, D_MLSTM), 0.02)
    diff_lambda = normal((DEPTH, 4, DIFF_HEAD_DIM), 0.1)
    diff_norm_g = 1.0 + normal((DEPTH, DIFF_V_DIM), 0.02)
    n_idx = jnp.arange(S5_STATE, dtype=f32)
    s5_a_re = -0.5 + normal((DEPTH, S5_GROUPS, S5_STATE), 0.01)
    s5_a_im = jnp.pi * n_idx + normal((DEPTH, S5_GROUPS, S5_STATE), 0.01)
    s5_log_step = jax.random.uniform(next(ks), (DEPTH, S5_GROUPS), f32,
                                     math.log(1e-3), math.log(1e-1))
    s5_b_re = normal((DEPTH, S5_GROUPS, S5_STATE, S5_GROUP), (2 * S5_GROUP) ** -0.5)
    s5_b_im = normal((DEPTH, S5_GROUPS, S5_STATE, S5_GROUP), (2 * S5_GROUP) ** -0.5)
    s5_c_re = normal((DEPTH, S5_GROUPS, S5_GROUP, S5_STATE), (2 * S5_STATE) ** -0.5)
    s5_c_im = normal((DEPTH, S5_GROUPS, S5_GROUP, S5_STATE), (2 * S5_STATE) ** -0.5)
    s5_d = normal((DEPTH, D_S5), 1.0)
    s5_glu_w = normal((DEPTH, D_S5, D_S5), D_S5 ** -0.5)
    s5_glu_b = normal((DEPTH, D_S5), 0.02)
    w_out = normal((DEPTH, D_MIX, D_MODEL), DN_BETA * D_MIX ** -0.5)
    xattn_wq = normal((DEPTH, D_MODEL, D_MODEL), D_MODEL ** -0.5)
    xattn_wkv = normal((DEPTH, D_MODEL, 2 * D_MODEL), D_MODEL ** -0.5)
    xattn_wo = normal((DEPTH, D_MODEL, D_MODEL), DN_BETA * D_MODEL ** -0.5)
    return {"x": x, "mem": mem, "ffn_w_gate": ffn_w_gate, "ffn_w_up": ffn_w_up,
            "ffn_w_down": ffn_w_down, "ln_g": ln_g, "ln_b": ln_b, "w_in": w_in,
            "conv_w": conv_w, "conv_b": conv_b, "mlstm_gate_b": mlstm_gate_b,
            "mlstm_norm_g": mlstm_norm_g, "diff_lambda": diff_lambda,
            "diff_norm_g": diff_norm_g, "s5_a_re": s5_a_re, "s5_a_im": s5_a_im,
            "s5_log_step": s5_log_step, "s5_b_re": s5_b_re, "s5_b_im": s5_b_im,
            "s5_c_re": s5_c_re, "s5_c_im": s5_c_im, "s5_d": s5_d, "s5_glu_w": s5_glu_w,
            "s5_glu_b": s5_glu_b, "w_out": w_out, "xattn_wq": xattn_wq,
            "xattn_wkv": xattn_wkv, "xattn_wo": xattn_wo}

def reference(x, mem, ffn_w_gate, ffn_w_up, ffn_w_down, ln_g, ln_b, w_in, conv_w, conv_b,
              mlstm_gate_b, mlstm_norm_g, diff_lambda, diff_norm_g, s5_a_re, s5_a_im,
              s5_log_step, s5_b_re, s5_b_im, s5_c_re, s5_c_im, s5_d, s5_glu_w, s5_glu_b,
              w_out, xattn_wq, xattn_wkv, xattn_wo):
    cos, sin = rope_tables(x.shape[1])
    for l in range(DEPTH):
        lambda_init = 0.8 - 0.6 * math.exp(-0.3 * l)
        h = swiglu(x, ffn_w_gate[l, 0], ffn_w_up[l, 0], ffn_w_down[l, 0])
        x = layer_norm(DN_ALPHA * x + 0.5 * h, ln_g[l, 0], ln_b[l, 0])
        h = hybrid_mix(x, cos, sin, lambda_init, w_in[l], conv_w[l], conv_b[l],
                       mlstm_gate_b[l], mlstm_norm_g[l], diff_lambda[l], diff_norm_g[l],
                       s5_a_re[l], s5_a_im[l], s5_log_step[l], s5_b_re[l], s5_b_im[l],
                       s5_c_re[l], s5_c_im[l], s5_d[l], s5_glu_w[l], s5_glu_b[l], w_out[l])
        x = layer_norm(DN_ALPHA * x + h, ln_g[l, 1], ln_b[l, 1])
        h = memory_cross_attention(x, mem, xattn_wq[l], xattn_wkv[l], xattn_wo[l])
        x = layer_norm(DN_ALPHA * x + h, ln_g[l, 2], ln_b[l, 2])
        h = swiglu(x, ffn_w_gate[l, 1], ffn_w_up[l, 1], ffn_w_down[l, 1])
        x = layer_norm(DN_ALPHA * x + 0.5 * h, ln_g[l, 3], ln_b[l, 3])
    return x


_drawn_inputs = setup_inputs


def setup_inputs(seed=0):
    import zlib

    import numpy as np

    out = dict(_drawn_inputs(seed))
    spreads = {}
    factors = {'conv_b': 8.0,
     'mlstm_norm_g': 32.564,
     'diff_lambda': 4.32,
     'diff_norm_g': 21.35,
     's5_a_re': 64.0,
     's5_a_im': 64.0,
     's5_log_step': 64.0,
     's5_b_re': 64.0,
     's5_b_im': 64.0,
     's5_c_re': 64.0,
     's5_c_im': 64.0,
     's5_glu_b': 200.0,
     's5_glu_w': 10.333}
    for name, (base, spread) in spreads.items():
        noise = np.random.default_rng([zlib.crc32(name.encode()), seed]).standard_normal(out[name].shape)
        drawn = base * np.exp(spread * noise) if base else spread * noise
        out[name] = __import__('jax').numpy.asarray(drawn.astype(out[name].dtype))
    for name, factor in factors.items():
        out[name] = (out[name] * factor).astype(out[name].dtype)
    return out
```

```python
import math
from contextlib import ExitStack

import numpy as np

import concourse.bass as bass
from concourse import mybir

F32 = mybir.dt.float32
F32R = mybir.dt.float32r
I32 = mybir.dt.int32
ACT = mybir.ActivationFunctionType
ALU = mybir.AluOpType
AX = mybir.AxisListType.X

D = 1024
SEQ = 256
DEPTH = 2
FF = 2816
P = 128
KC = D // P
TT = SEQ // P
FB = 256
BLOCKS = FF // FB
HEADS = 4
CHUNK = 64
GROUPS = 16
TILES = GROUPS * 64 // P
ALPHA = (2 * DEPTH) ** 0.25
EPS = 1e-5
LAMBDA_INIT = [0.8 - 0.6 * math.exp(-0.3 * l) for l in range(DEPTH)]

U_FFN = (0, 66)
U_SU, U_MQ, U_MK, U_DQ, U_DK, U_DV, U_MM = 33, 34, 35, 36, 38, 40, 42
U_K, U_V, U_WOUT, U_WQ, U_WO = 44, 48, 52, 57, 61
UNITS = 99
RING = 3
PER_SLOT = UNITS // RING

C_DQ, C_DK, C_DV, C_MQ, C_MK, C_MV, C_SU = 0, 512, 1024, 1536, 1792, 2048, 2568

K_ID, K_CM, K_TRI, K_COS, K_SIN, K_IOTA, K_LAM, K_SEL, K_END = 0, 128, 512, 896, 960, 1024, 1280, 1284, 1796

P_B, P_C, P_GLU, P_GLUB, P_D, P_CW, P_CB, P_GB, P_GW, P_DG, P_MG, P_END = (
    0, 512, 1024, 1536, 1538, 1540, 1556, 1560, 1562, 1626, 1754, 2010)

R_RAD, R_PHI, R_PLO, R_FRE, R_FIM, R_NLAM, R_OML, R_END = 0, 8, 16, 24, 32, 40, 41, 44

MAGIC = 12582912.0
MAGIC12 = 3072.0
TWO_PI = 6.2831850

DVE_LINKS, POOL_LINKS = 158, 107


def build(nc, x_in, mem_in, wg, wu, wd, ln_g, ln_b, w_in, w_out, wq, wkv, wo, par, setup, const, out):
    wg_v = wg.rearrange("l s (c p) f -> (l s) p c f", p=P)
    wu_v = wu.rearrange("l s (c p) f -> (l s) p c f", p=P)
    wd_v = wd.rearrange("l s (c p) n -> (l s) c p n", p=P)
    win_v = w_in.rearrange("l (c p) n -> l p c n", p=P)
    wout_v = w_out.rearrange("l (c p) n -> l c p n", p=P)
    wq_v = wq.rearrange("l (c p) n -> l p c n", p=P)
    wkv_v = wkv.rearrange("l (c p) n -> l p c n", p=P)
    wo_v = wo.rearrange("l (c p) n -> l c p n", p=P)
    lng_v = ln_g.rearrange("l n d -> (l n) d")
    lnb_v = ln_b.rearrange("l n d -> (l n) d")

    ctx = ExitStack()
    with ctx:
        top = [(nc.sbuf_base + 31) // 32 * 32]

        def place(name, shape, dt, at=None):
            size = 4 * int(np.prod(shape[1:]))
            if at is None:
                at = top[0]
                top[0] += (size + 31) // 32 * 32
            return nc.alloc_sbuf_tensor_at(name, shape, dt, offset=at), at

        def sb(name, shape, dt=F32, at=None):
            return place(name, shape, dt, at)[0]

        kst = sb("kst", [P, K_END])
        X = sb("X", [P, TT, D])
        XH, xh_at = place("XH", [P, KC, SEQ], F32R)
        XL, xl_at = place("XL", [P, KC, SEQ], F32R)
        MH = sb("MH", [P, KC, SEQ], F32R)
        ML = sb("ML", [P, KC, SEQ], F32R)
        RAW = [sb(f"RAW{s}", [P, 2048]) for s in range(RING)]
        WH = [sb(f"WH{s}", [P, 2048], F32R) for s in range(RING)]
        WL = [sb(f"WL{s}", [P, 2048], F32R) for s in range(RING)]
        LNGB, gb_at = place("LNGB", [P, 2, D], F32)
        F8, f8_at = place("F8", [P, 2048], F32)
        KT = sb("KT", [P, KC, SEQ])
        V, v_at = place("V", [P, TT, D], F32)
        CH, ch_at = place("CH", [P, KC, SEQ], F32R)
        CL, cl_at = place("CL", [P, KC, SEQ], F32R)
        RQ, rq_at = place("RQ", [P, 2048], F32)
        DV = sb("DV", [P, TT, 512])
        VA = sb("VA", [P, TT, HEADS, 65])
        SIGO = sb("SIGO", [P, TT, 256])
        CIN, cin_at = place("CIN", [P, 4, SEQ + 3], F32)
        COUT, cout_at = place("COUT", [P, 4, SEQ], F32)
        UT = sb("UT", [P, 2, SEQ])
        PAR = sb("PAR", [P, P_END])
        REC = sb("REC", [P, DEPTH, R_END])
        CUR = sb("CUR", [P, R_END])
        GWH = sb("GWH", [P, KC, 8], F32R)
        GWL = sb("GWL", [P, KC, 8], F32R)
        CP = sb("CP", [P, 2, TILES, 32])
        SM = sb("SM", [P, 224])
        ones_c = sb("ones_c", [P, 1])

        HB = sb("HB", [P, TT, FB], F32, f8_at)
        SG = sb("SG", [P, TT, FB], F32, f8_at + 2048)
        HH = sb("HH", [P, 2, SEQ], F32R, f8_at + 4096)
        HL = sb("HL", [P, 2, SEQ], F32R, f8_at + 6144)
        QK = sb("QK", [P, TT, 1024], F32, f8_at)
        RO = sb("RO", [P, TT, 1024], F32, rq_at)
        CAT = sb("CAT", [P, TT, 768], F32, rq_at)
        QX = sb("QX", [P, KC, SEQ], F32, rq_at)
        MEMX = sb("MEMX", [P, TT, D], F32, rq_at)
        DQT = sb("DQT", [P, HEADS, SEQ], F32, xh_at)
        DKT = sb("DKT", [P, HEADS, SEQ], F32, xh_at + 4096)
        ES = sb("ES", [P, 2, 384], F32, xl_at)
        PR = sb("PR", [P, 2, 384], F32, xl_at + 3072)
        AT = sb("AT", [P, 384], F32, xl_at + 6144)
        AQ = sb("AQ", [P, P], F32, xl_at + 3072)
        XP = sb("XP", [P, 2, 256], F32, xl_at)
        XPT = sb("XPT", [P, 2, 2, 256], F32, xl_at + 2048)
        ZW = sb("ZW", [P, 2, SEQ], F32, gb_at)
        ZT = sb("ZT", [P, 2, SEQ], F32, gb_at + 2048)
        ZS = sb("ZS", [P, 2, 2, SEQ], F32, gb_at + 4096)
        EC = sb("EC", [P, TILES, SEQ], F32, ch_at)
        ESN = sb("ESN", [P, TILES, SEQ], F32, cl_at)
        EF = sb("EF", [P, SEQ], F32, rq_at)
        SU = sb("SU", [P, 1024], F32, f8_at)
        SW = sb("SW", [P, 1024], F32, f8_at + 4096)

        ZX = sb("ZX", [P, 2, 2, SEQ], F32, cin_at)
        SDA = sb("SDA", [P, HEADS, 384], F32, f8_at)
        ZB = sb("ZB", [P, TT, 256], F32, f8_at + 6144)
        ROW = sb("ROW", [HEADS, 6, SEQ], F32, v_at)
        PW = sb("PW", [P, 256], F32, v_at + 6144)
        assert top[0] <= nc.sbuf_usable_end, (top[0], nc.sbuf_usable_end)

        PS = ctx.enter_context(nc.psum_tensor("PS", [P, 8, 512], F32))
        Y = PS[:, 0:4, :].rearrange("p b n -> p (b n)").rearrange("p (t n) -> p t n", t=TT)

        def bank(b):
            return PS[:, b, :]

        ident = kst[:, K_ID:K_ID + P]
        cmask = kst[:, K_CM:K_CM + 384]
        tri = kst[:, K_TRI:K_TRI + 384]
        iota = kst[:, K_IOTA:K_IOTA + SEQ]

        class Event:

            def __init__(self, name, per, first=0):
                self.sem, self.per, self.first = ctx.enter_context(nc.semaphore(name)), per, first

            def at(self, l, n):
                return l * self.per + (self.first + n)

        raw_loaded = [Event(f"raw_loaded{s}", 32 * PER_SLOT) for s in range(RING)]
        split_hi = Event("split_hi", UNITS)
        split_lo = Event("split_lo", UNITS, RING)
        unit_used = Event("unit_used", UNITS, RING)
        const_in = Event("const_in", 0)
        setup_in = Event("setup_in", 0)
        x_loaded = Event("x_loaded", 0)
        mem_loaded = Event("mem_loaded", 0)
        param_in = Event("param_in", 16)
        gb_in = Event("gb_in", 4 * 32)
        x_ready = Event("x_ready", 4 * TT)
        xT_psum = Event("xT_psum", 4 * 4, 4)
        xT_hi = Event("xT_hi", 4 * 4, 4)
        xT_lo = Event("xT_lo", 4 * 4, 4)
        gu_done = Event("gu_done", 2 * BLOCKS)
        sg_done = Event("sg_done", 2 * BLOCKS * TT)
        h_ready = Event("h_ready", 2 * BLOCKS * TT)
        hT_psum = Event("hT_psum", 2 * BLOCKS)
        hT_hi = Event("hT_hi", 2 * BLOCKS)
        hT_lo = Event("hT_lo", 2 * BLOCKS)
        out_done = Event("out_done", 0)
        rec_ready = Event("rec_ready", 0)
        setup_sin = Event("setup_sin", 0)
        setup_phase = Event("setup_phase", 0)
        cur_ready = Event("cur_ready", 1)
        phase_ready = Event("phase_ready", 1)
        table_ready = Event("table_ready", 1)
        cp_ready = Event("cp_ready", 1)
        cin_zero = Event("cin_zero", 1)
        gw_hi = Event("gw_hi", 1)
        gw_lo = Event("gw_lo", 1)
        ut_ready = Event("ut_ready", 1)
        gate_done = Event("gate_done", 1)
        gate_tok = Event("gate_tok", 1)
        gateT_done = Event("gateT_done", 1)
        gate_read = Event("gate_read", 1)
        gate_abs = Event("gate_abs", 1)
        gate_log = Event("gate_log", 1)
        rows_ready = Event("rows_ready", 1)
        cols_done = Event("cols_done", 1)
        cols_read = Event("cols_read", 1)
        mbc_done = Event("mbc_done", 2)
        mqk_read = Event("mqk_read", 2)
        conv_done = Event("conv_done", 4)
        silu_done = Event("silu_done", 1)
        proj_read = Event("proj_read", 8)
        roped = Event("roped", 2)
        bu_done = Event("bu_done", TILES)
        bu_read = Event("bu_read", TILES)
        z_ready = Event("z_ready", TILES)
        state_ready = Event("state_ready", TILES)
        state_used = Event("state_used", TILES)
        ys_done = Event("ys_done", 1)
        ys_read = Event("ys_read", 1)
        gelu_done = Event("gelu_done", 1)
        glu_done = Event("glu_done", 1)
        glu_sig = Event("glu_sig", 1)
        c_hi_in = Event("c_hi_in", 1)
        c_hi = Event("c_hi", 1)
        c_lo = Event("c_lo", 1)
        kv_read = Event("kv_read", 8)
        tq_done = Event("tq_done", 4)
        tq_read = Event("tq_read", 4)
        decay_in = Event("decay_in", HEADS)
        decay_done = Event("decay_done", HEADS)
        ms_done = Event("ms_done", HEADS)
        msd_ready = Event("msd_ready", HEADS)
        num_done = Event("num_done", TT)
        num_read = Event("num_read", 1)
        ds_done = Event("ds_done", 8)
        ds_masked = Event("ds_masked", 8)
        ds_max = Event("ds_max", 8)
        dp_done = Event("dp_done", 8)
        da_ready = Event("da_ready", HEADS)
        daT_done = Event("daT_done", HEADS)
        daT_read = Event("daT_read", HEADS)
        do_done = Event("do_done", HEADS)
        do_read = Event("do_read", HEADS)
        b_ready = Event("b_ready", 1)
        a_ready = Event("a_ready", 1)
        catT_done = Event("catT_done", 3)
        cat_hi = Event("cat_hi", 3)
        cat_lo = Event("cat_lo", 3)
        qx_read = Event("qx_read", 4)
        xs_done = Event("xs_done", HEADS)
        xs_max = Event("xs_max", HEADS)
        xp_done = Event("xp_done", HEADS)
        xp_norm = Event("xp_norm", HEADS)
        xpT_done = Event("xpT_done", HEADS)
        xpT_read = Event("xpT_read", HEADS)
        xo_done = Event("xo_done", HEADS)
        xo_hi = Event("xo_hi", HEADS)
        xo_lo = Event("xo_lo", HEADS)
        dve_link = Event("dve_link", DVE_LINKS)
        dve_setup = Event("dve_setup", 0)
        pool_link = Event("pool_link", POOL_LINKS)

        act_link = Event("act_link", 2)
        exp_m = Event("exp_m", 1)
        ln_sum = Event("ln_sum", 4 * TT)
        ln_stat = Event("ln_stat", 4 * 2 * TT)
        ln_mid = Event("ln_mid", 4 * TT)
        dc_mid = Event("dc_mid", 2 * HEADS)

        waits_apart = Event("waits_apart", 0)


        block = ctx.enter_context(nc.Block())

        @block.sync
        def _(sp):
            sp.dma_start(kst[:, :], const).then_inc(const_in.sem, 16)
            sp.dma_start(MEMX[:, :, :], mem_in.rearrange("b (t p) d -> p (b t) d", p=P)).then_inc(mem_loaded.sem, 16)
            sp.dma_start(X[:, :, :], x_in.rearrange("b (t p) d -> p (b t) d", p=P)).then_inc(x_loaded.sem, 16)

            def load(l, u, j, first, second):
                sp.wait_ge(split_lo.sem, split_lo.at(l, u - RING + 1 + 3 * j))
                sp.sem_inc(waits_apart.sem, 1)
                s = u % RING
                for dst, src in (first, second):
                    sp.dma_start(dst, src).then_inc(raw_loaded[s].sem, 16)

            def load_gu(l, f, u, j, blk, half):
                r = RAW[u % RING][:, :].rearrange("p (c g n) -> p c g n", c=4, g=2)
                cs = slice(4 * half, 4 * half + 4)
                load(l, u, j, (r[:, :, 0, :], wg_v[f, :, cs, bass.ts(blk, FB)]),
                     (r[:, :, 1, :], wu_v[f, :, cs, bass.ts(blk, FB)]))

            def load_down(l, f, u, j, blk):
                r = RAW[u % RING][:, :].rearrange("p (c n) -> p c n", c=2)
                load(l, u, j, (r[:, 0, :], wd_v[f, blk * 2]), (r[:, 1, :], wd_v[f, blk * 2 + 1]))

            def load_rows(l, u, w, c0, n, cols):
                r = RAW[u % RING][:, 0:n * 512].rearrange("p (c n) -> p c n", c=n)
                h = n // 2
                load(l, u, 0, (r[:, 0:h, :], w[l, :, c0:c0 + h, cols]), (r[:, h:n, :], w[l, :, c0 + h:c0 + n, cols]))

            def load_cols(l, u, w, col):
                r = RAW[u % RING][:, :].rearrange("p (c n) -> p c n", c=KC)
                cols = slice(col, col + 256)
                load(l, u, 0, (r[:, 0:4, :], w[l, :, 0:4, cols]), (r[:, 4:8, :], w[l, :, 4:8, cols]))

            def load_pair(l, u, w, c):
                r = RAW[u % RING][:, :].rearrange("p (c n) -> p c n", c=2)
                load(l, u, 0, (r[:, 0, :], w[l, c]), (r[:, 1, :], w[l, c + 1]))

            def load_single(l, u, w, c):
                r = RAW[u % RING]
                load(l, u, 0, (r[:, 0:512], w[l, c, :, 0:512]), (r[:, 512:1024], w[l, c, :, 512:1024]))

            def load_ffn(l, s):
                b = U_FFN[s]
                f = l * 2 + s
                load_gu(l, f, b, 0, 0, 0)
                load_gu(l, f, b + 1, 0, 0, 1)
                with sp.Fori(0, BLOCKS - 1) as j:
                    load_gu(l, f, b + 2, j, j + 1, 0)
                    load_gu(l, f, b + 3, j, j + 1, 1)
                    load_down(l, f, b + 4, j, j)
                load_down(l, f, b + 32, 0, BLOCKS - 1)

            with sp.Fori(0, DEPTH) as l:
                load_ffn(l, 0)
                load_cols(l, U_SU, win_v, C_SU)
                load_cols(l, U_MQ, win_v, C_MQ)
                load_cols(l, U_MK, win_v, C_MK)
                for u, c in ((U_DQ, C_DQ), (U_DK, C_DK), (U_DV, C_DV), (U_MM, C_MV)):
                    for half in range(2):
                        load_rows(l, u + half, win_v, 4 * half, 4, slice(c, c + 512))
                for i in range(4):
                    load_cols(l, U_K + i, wkv_v, 256 * i)
                for i in range(4):
                    load_rows(l, U_V + i, wkv_v, 4 * (i % 2), 4, slice(D + 512 * (i // 2), D + 512 * (i // 2 + 1)))
                load_single(l, U_WOUT, wout_v, 6)
                load_single(l, U_WOUT + 1, wout_v, 7)
                for i, c in enumerate((4, 0, 2)):
                    load_pair(l, U_WOUT + 2 + i, wout_v, c)
                for i in range(4):
                    load_cols(l, U_WQ + i, wq_v, 256 * i)
                load_single(l, U_WO, wo_v, 0)
                load_single(l, U_WO + 1, wo_v, 1)
                for i in range(3):
                    load_pair(l, U_WO + 2 + i, wo_v, 2 + 2 * i)
                load_ffn(l, 1)
            sp.wait_ge(x_ready.sem, x_ready.at(DEPTH, 0))
            sp.dma_start(out.rearrange("b (t p) d -> p (b t) d", p=P), X[:, :, :]).then_inc(out_done.sem, 16)
            sp.wait_ge(out_done.sem, 16)

        @block.tensor
        def _(pe):
            pe.sem_inc(unit_used.sem, RING)
            pe.wait_ge(const_in.sem, 16)

            def prod(out_ap, sh, sl, mh, ml, first, last):
                nc.tensor.matmul(out_ap, sh, mh, start=first, stop=False)
                nc.tensor.matmul(out_ap, sh, ml, start=False, stop=False)
                return nc.tensor.matmul(out_ap, sl, mh, start=False, stop=last)

            def unit_ready(l, u, j=0):
                pe.wait_ge(split_lo.sem, split_lo.at(l, u + 1 + 3 * j))

            def gate_up(l, s, u, j, half, blk):
                unit_ready(l, u, j)
                wh = WH[u % RING][:, :].rearrange("p (c n) -> p c n", c=4)
                wl = WL[u % RING][:, :].rearrange("p (c n) -> p c n", c=4)
                for t in range(TT):
                    tok = slice(t * P, t * P + P)
                    for c in range(4):
                        k = 4 * half + c
                        mm = prod(bank(4 + t), XH[:, k, tok], XL[:, k, tok], wh[:, c, :], wl[:, c, :],
                                  k == 0, k == KC - 1)
                    if half == 1 and t == 0:
                        mm.then_inc(gu_done.sem, 1)
                    if half == 1 and t == 1:
                        mm.then_inc(unit_used.sem, 1)
                if half == 0:
                    mm.then_inc(unit_used.sem, 1)

            def turn_h(l, s, blk):
                pe.wait_ge(h_ready.sem, h_ready.at(l, 22 * s + 2 * blk + 2))
                for fc in range(2):
                    for t in range(TT):
                        mm = nc.tensor.transpose(PS[:, 6, fc * SEQ + t * P:fc * SEQ + t * P + P],
                                                 HB[:, t, fc * P:fc * P + P], ident)
                mm.then_inc(hT_psum.sem, 1)

            def rows_product(l, u, j, chunks, ah, al, first, last, done=None, single=False):
                unit_ready(l, u, j)
                n = len(chunks)
                wh = WH[u % RING][:, 0:n * D].rearrange("p (c n) -> p c n", c=n)
                wl = WL[u % RING][:, 0:n * D].rearrange("p (c n) -> p c n", c=n)
                for t in range(TT):
                    tok = slice(t * P, t * P + P)
                    for i, c in enumerate(chunks):
                        for half in range(2):
                            cols = slice(512 * half, 512 * half + 512)
                            mm = prod(bank(2 * t + half), ah[:, c, tok], al[:, c, tok], wh[:, i, cols], wl[:, i, cols],
                                      first and i == 0, last and i == n - 1)
                mm.then_inc(unit_used.sem, 1)

            def down(l, s, u, j, blk, first=False, last=False):
                pe.wait_ge(hT_hi.sem, hT_hi.at(l, 11 * s + blk + 1))
                pe.wait_ge(hT_lo.sem, hT_lo.at(l, 11 * s + blk + 1))
                rows_product(l, u, j, [0, 1], HH, HL, first, last)

            def ffn(l, s):
                b = U_FFN[s]
                gate_up(l, s, b, 0, 0, 0)
                gate_up(l, s, b + 1, 0, 1, 0)

                def step(j, jj, first):
                    gate_up(l, s, b + 2, jj, 0, j + 1)
                    turn_h(l, s, j)
                    gate_up(l, s, b + 3, jj, 1, j + 1)
                    down(l, s, b + 4, jj, j, first)

                pe.wait_ge(h_ready.sem, h_ready.at(l, 22 * s + 2))
                step(0, 0, True)
                with pe.Fori(1, BLOCKS - 1) as j:
                    pe.wait_ge(h_ready.sem, h_ready.at(l, j * 2 + (22 * s + 2)))
                    step(j, j, False)
                pe.wait_ge(h_ready.sem, h_ready.at(l, 22 * s + 2 * BLOCKS))
                turn_h(l, s, BLOCKS - 1)
                down(l, s, b + 32, 0, BLOCKS - 1, False, True)

            def turn_x(l, n, src, banks=(4, 5, 6, 7)):
                for t in range(TT):
                    if n > 0:
                        pe.wait_ge(x_ready.sem, x_ready.at(l, TT * (n - 1) + t + 1))
                    for half in range(2):
                        for i in range(4):
                            c = 4 * half + i
                            mm = nc.tensor.transpose(PS[:, banks[2 * t + half], i * P:i * P + P],
                                                     src[:, t, c * P:c * P + P], ident)
                        mm.then_inc(xT_psum.sem, 1)

            def form_b(l, u, b, mh, ml):
                unit_ready(l, u)
                wh = WH[u % RING][:, :].rearrange("p (c n) -> p c n", c=KC)
                wl = WL[u % RING][:, :].rearrange("p (c n) -> p c n", c=KC)
                for f in range(2):
                    for c in range(KC):
                        cols = slice(f * P, f * P + P)
                        mm = prod(PS[:, b, f * SEQ:f * SEQ + SEQ], wh[:, c, cols], wl[:, c, cols],
                                  mh[:, c, :], ml[:, c, :], c == 0, c == KC - 1)
                mm.then_inc(unit_used.sem, 1)

            def form_a(l, u, half, b, ah, al):
                unit_ready(l, u)
                wh = WH[u % RING][:, :].rearrange("p (c n) -> p c n", c=4)
                wl = WL[u % RING][:, :].rearrange("p (c n) -> p c n", c=4)
                for t in range(TT):
                    tok = slice(t * P, t * P + P)
                    for c in range(4):
                        k = 4 * half + c
                        mm = prod(bank(b + t), ah[:, k, tok], al[:, k, tok], wh[:, c, :], wl[:, c, :],
                                  k == 0, k == KC - 1)
                mm.then_inc(unit_used.sem, 1)

            def used(l, u):
                pe.wait_ge(unit_used.sem, unit_used.at(l, u + 1))

            def s5_in(l, i):
                if i == 0:
                    pe.wait_ge(ut_ready.sem, ut_ready.at(l, 1))
                if i == 1:
                    pe.wait_ge(gate_read.sem, gate_read.at(l, 1))
                if i >= 2:
                    pe.wait_ge(bu_read.sem, bu_read.at(l, i - 1))
                r = 32 * (i % 4)
                for part in range(2):
                    o = P_B + part * 256 + (i // 4) * P
                    mm = nc.tensor.matmul(PS[:, 6 + i % 2, part * SEQ:part * SEQ + SEQ], PAR[r:r + 32, o:o + P],
                                          UT[r:r + 32, i // 4, :], start=True, stop=True)
                mm.then_inc(bu_done.sem, 1)

            def s5_out(l, i):
                pe.wait_ge(state_ready.sem, state_ready.at(l, i + 1))
                if i == 0:
                    pe.wait_ge(cp_ready.sem, cp_ready.at(l, 1))
                    pe.wait_ge(proj_read.sem, proj_read.at(l, 3))
                r = 32 * (i % 4)
                for part in range(2):
                    mm = nc.tensor.matmul(PS[r:r + 32, 2, (i // 4) * SEQ:(i // 4 + 1) * SEQ], CP[:, part, i, :],
                                          ZX[:, i % 2, part, :], start=(part == 0), stop=(part == 1))
                mm.then_inc(state_used.sem, 1)

            def mlstm_scores(l, h):
                b = 5 - h % 2
                if h == 0:
                    pe.wait_ge(silu_done.sem, silu_done.at(l, 1))
                pe.wait_ge(decay_in.sem, decay_in.at(l, 2 if h == 0 else 4))
                if h >= 2:
                    pe.wait_ge(msd_ready.sem, msd_ready.at(l, h - 1))
                r = 64 * (h % 2)
                k = COUT[r:r + 64, 2 + h // 2, :]
                q = COUT[r:r + 64, h // 2, :]
                nc.tensor.matmul(PS[:, b, 0:256], k[:, 0:P], q[:, :], start=True, stop=True)
                nc.tensor.matmul(PS[:, b, 256:384], k[:, P:SEQ], q[:, P:SEQ], start=True, stop=True)\
                    .then_inc(ms_done.sem, 1)

            def mlstm_num(l):
                pe.wait_ge(msd_ready.sem, msd_ready.at(l, HEADS))
                for t in range(TT):
                    for h in range(HEADS):
                        o = PS[:, 5 - t, h * 65:h * 65 + 65]
                        if t == 0:
                            mm = nc.tensor.matmul(o, SDA[:, h, 0:P], VA[:, 0, h, :], start=True, stop=True)
                        else:
                            nc.tensor.matmul(o, SDA[:, h, P:2 * P], VA[:, 0, h, :], start=True, stop=False)
                            mm = nc.tensor.matmul(o, SDA[:, h, 2 * P:3 * P], VA[:, 1, h, :], start=False, stop=True)
                    mm.then_inc(num_done.sem, 1)

            def turn_q(l, i):
                if i == 0:
                    pe.wait_ge(roped.sem, roped.at(l, 2))
                if i < 2:
                    pe.wait_ge(bu_read.sem, bu_read.at(l, TILES - 1 + i))
                else:
                    pe.wait_ge(tq_read.sem, tq_read.at(l, i - 1))
                for hh in range(2):
                    for t in range(TT):
                        col = (i // 2) * 512 + (2 * (i % 2) + hh) * P
                        mm = nc.tensor.transpose(PS[:, 6 + i % 2, hh * SEQ + t * P:hh * SEQ + t * P + P],
                                                 RO[:, t, col:col + P], ident)
                mm.then_inc(tq_done.sem, 1)

            def diff_scores(l, h, m):
                i = 2 * h + m
                if i == 0:
                    pe.wait_ge(tq_read.sem, tq_read.at(l, 4))
                if i >= 2:
                    pe.wait_ge(ds_masked.sem, ds_masked.at(l, i - 1))
                r = 64 * m
                nc.tensor.matmul(PS[:, 6 + m, 0:P], DQT[r:r + 64, h, 0:P], DKT[r:r + 64, h, 0:P],
                                 start=True, stop=True)
                nc.tensor.matmul(PS[:, 6 + m, P:384], DQT[r:r + 64, h, P:SEQ], DKT[r:r + 64, h, :],
                                 start=True, stop=True).then_inc(ds_done.sem, 1)

            def diff_out(l, h):
                pe.wait_ge(da_ready.sem, da_ready.at(l, h + 1))
                if h == 0:
                    pe.wait_ge(num_read.sem, num_read.at(l, 1))
                for i in range(3):
                    mm = nc.tensor.transpose(PS[:, 4, i * P:i * P + P], ES[:, 0, i * P:i * P + P], ident)
                mm.then_inc(daT_done.sem, 1)
                pe.wait_ge(daT_read.sem, daT_read.at(l, h + 1))
                if h >= 1:
                    pe.wait_ge(do_read.sem, do_read.at(l, h))
                v = slice(h * P, h * P + P)
                nc.tensor.matmul(PS[:, 5, 0:P], AT[:, 0:P], DV[:, 0, v], start=True, stop=True)
                nc.tensor.matmul(PS[:, 5, P:2 * P], AT[:, P:2 * P], DV[:, 0, v], start=True, stop=False)
                nc.tensor.matmul(PS[:, 5, P:2 * P], AT[:, 2 * P:3 * P], DV[:, 1, v], start=False, stop=True)\
                    .then_inc(do_done.sem, 1)

            def turn_cat(l, i, c0, b):
                for cc in range(2):
                    for t in range(TT):
                        c = c0 + cc
                        mm = nc.tensor.transpose(PS[:, b, cc * SEQ + t * P:cc * SEQ + t * P + P],
                                                 CAT[:, t, c * P:c * P + P], ident)
                mm.then_inc(catT_done.sem, 1)

            def mix(l):
                pe.wait_ge(xT_hi.sem, xT_hi.at(l, 8))
                pe.wait_ge(xT_lo.sem, xT_lo.at(l, 8))
                form_b(l, U_SU, 6, XH, XL)
                pe.wait_ge(gw_lo.sem, gw_lo.at(l, 1))
                for t in range(TT):
                    tok = slice(t * P, t * P + P)
                    for c in range(KC):
                        mm = prod(PS[:, 7, t * 8:t * 8 + 8], XH[:, c, tok], XL[:, c, tok], GWH[:, c, :], GWL[:, c, :],
                                  c == 0, c == KC - 1)
                mm.then_inc(gate_done.sem, 1)
                form_b(l, U_MQ, 4, XH, XL)
                form_b(l, U_MK, 5, XH, XL)
                pe.wait_ge(gate_tok.sem, gate_tok.at(l, 1))
                for g in range(2):
                    for t in range(TT):
                        mm = nc.tensor.transpose(PS[0:4, 7, g * SEQ + t * P:g * SEQ + t * P + P],
                                                 SM[:, 200 + t * 8 + g * 4:200 + t * 8 + g * 4 + 4], ident)
                mm.then_inc(gateT_done.sem, 1)
                form_a(l, U_DQ, 0, 0, XH, XL)
                form_a(l, U_DQ + 1, 1, 0, XH, XL)
                s5_in(l, 0)
                form_a(l, U_DK, 0, 2, XH, XL)
                s5_in(l, 1)
                form_a(l, U_DK + 1, 1, 2, XH, XL)
                s5_in(l, 2)
                pe.wait_ge(mqk_read.sem, mqk_read.at(l, 2))
                form_a(l, U_DV, 0, 4, XH, XL)
                s5_in(l, 3)
                s5_out(l, 0)
                form_a(l, U_DV + 1, 1, 4, XH, XL)
                s5_in(l, 4)
                s5_out(l, 1)
                pe.wait_ge(proj_read.sem, proj_read.at(l, 2))
                form_a(l, U_MM, 0, 0, XH, XL)
                s5_in(l, 5)
                s5_out(l, 2)
                form_a(l, U_MM + 1, 1, 0, XH, XL)
                s5_in(l, 6)
                s5_out(l, 3)
                pe.wait_ge(proj_read.sem, proj_read.at(l, 4))
                form_b(l, U_K, 3, MH, ML)
                s5_in(l, 7)
                s5_out(l, 4)
                pe.wait_ge(proj_read.sem, proj_read.at(l, 6))
                pe.wait_ge(rows_ready.sem, rows_ready.at(l, 1))
                pe.sem_inc(waits_apart.sem, 1)
                for r in range(2):
                    for t in range(TT):
                        mm = nc.tensor.transpose(PS[:, 4, r * 8 + t * 4:r * 8 + t * 4 + 4],
                                                 ROW[:, 1 + 2 * r, t * P:t * P + P], ident[0:4, 0:4])
                mm.then_inc(cols_done.sem, 1)
                pe.wait_ge(proj_read.sem, proj_read.at(l, 8))
                form_b(l, U_K + 1, 0, MH, ML)
                s5_out(l, 5)
                for h in range(2):
                    mm = nc.tensor.matmul(PS[:, 5, h * SEQ:h * SEQ + SEQ],
                                          kst[0:4, K_SEL + h * P:K_SEL + h * P + P], ROW[:, 0, :],
                                          start=True, stop=True)
                mm.then_inc(mbc_done.sem, 1)
                form_b(l, U_K + 2, 1, MH, ML)
                s5_out(l, 6)
                pe.wait_ge(cols_read.sem, cols_read.at(l, 1))
                for h in range(2):
                    mm = nc.tensor.matmul(PS[:, 4, h * SEQ:h * SEQ + SEQ],
                                          kst[0:4, K_SEL + (2 + h) * P:K_SEL + (3 + h) * P], ROW[:, 0, :],
                                          start=True, stop=True)
                mm.then_inc(mbc_done.sem, 1)
                turn_q(l, 0)
                pe.wait_ge(kv_read.sem, kv_read.at(l, 1))
                form_b(l, U_K + 3, 3, MH, ML)
                s5_out(l, 7)
                turn_q(l, 1)
                turn_q(l, 2)
                turn_q(l, 3)
                pe.wait_ge(kv_read.sem, kv_read.at(l, 3))
                form_a(l, U_V, 0, 0, MH, ML)
                mlstm_scores(l, 0)
                mlstm_scores(l, 1)
                diff_scores(l, 0, 0)
                diff_scores(l, 0, 1)
                form_a(l, U_V + 1, 1, 0, MH, ML)
                mlstm_scores(l, 2)
                mlstm_scores(l, 3)
                pe.wait_ge(kv_read.sem, kv_read.at(l, 6))
                form_a(l, U_V + 2, 0, 0, MH, ML)
                pe.wait_ge(gelu_done.sem, gelu_done.at(l, 1))
                pe.wait_ge(kv_read.sem, kv_read.at(l, 4))
                for f in range(2):
                    for c in range(2):
                        o = P_GLU + c * 256 + f * P
                        mm = nc.tensor.matmul(PS[:, 3, f * SEQ:f * SEQ + SEQ], PAR[:, o:o + P], UT[:, c, :],
                                              start=(c == 0), stop=(c == 1))
                mm.then_inc(glu_done.sem, 1)
                mlstm_num(l)
                form_a(l, U_V + 3, 1, 0, MH, ML)
                diff_scores(l, 1, 0)
                diff_scores(l, 1, 1)
                diff_out(l, 0)
                diff_scores(l, 2, 0)
                diff_scores(l, 2, 1)
                diff_out(l, 1)
                pe.wait_ge(b_ready.sem, b_ready.at(l, 1))
                pe.wait_ge(ys_read.sem, ys_read.at(l, 1))
                turn_cat(l, 0, 4, 2)
                diff_scores(l, 3, 0)
                diff_scores(l, 3, 1)
                diff_out(l, 2)
                pe.wait_ge(c_lo.sem, c_lo.at(l, 1))
                pe.wait_ge(cat_lo.sem, cat_lo.at(l, 1))
                pe.wait_ge(kv_read.sem, kv_read.at(l, 8))
                rows_product(l, U_WOUT, 0, [6], CH, CL, True, False)
                diff_out(l, 3)
                rows_product(l, U_WOUT + 1, 0, [7], CH, CL, False, False)
                rows_product(l, U_WOUT + 2, 0, [4, 5], CH, CL, False, False)
                pe.wait_ge(a_ready.sem, a_ready.at(l, 1))
                turn_cat(l, 1, 0, 6)
                turn_cat(l, 2, 2, 7)
                pe.wait_ge(cat_lo.sem, cat_lo.at(l, 2))
                rows_product(l, U_WOUT + 3, 0, [0, 1], CH, CL, False, False)
                pe.wait_ge(cat_lo.sem, cat_lo.at(l, 3))
                rows_product(l, U_WOUT + 4, 0, [2, 3], CH, CL, False, True)

            def xattn(l):
                pe.wait_ge(xT_hi.sem, xT_hi.at(l, 12))
                pe.wait_ge(xT_lo.sem, xT_lo.at(l, 12))
                for i in range(4):
                    form_b(l, U_WQ + i, 4 + i, XH, XL)
                for h in range(HEADS):
                    pe.wait_ge(qx_read.sem, qx_read.at(l, h + 1))
                    for t in range(TT):
                        for c in range(2):
                            mm = nc.tensor.matmul(PS[:, h, t * SEQ:t * SEQ + SEQ],
                                                  QX[:, 2 * h + c, t * P:t * P + P], KT[:, 2 * h + c, :],
                                                  start=(c == 0), stop=(c == 1))
                    mm.then_inc(xs_done.sem, 1)
                for h in range(HEADS):
                    pe.wait_ge(xp_norm.sem, xp_norm.at(l, h + 1))
                    if h >= 2:
                        pe.wait_ge(xpT_read.sem, xpT_read.at(l, h - 1))
                    for mt in range(2):
                        for t in range(TT):
                            mm = nc.tensor.transpose(PS[:, 4 + h % 2, mt * SEQ + t * P:mt * SEQ + t * P + P],
                                                     XP[:, t, mt * P:mt * P + P], ident)
                    mm.then_inc(xpT_done.sem, 1)
                    pe.wait_ge(xpT_read.sem, xpT_read.at(l, h + 1))
                    if h >= 2:
                        pe.wait_ge(xo_lo.sem, xo_lo.at(l, h - 1))
                    for dc in range(2):
                        for mt in range(2):
                            mm = nc.tensor.matmul(PS[:, 6 + h % 2, dc * SEQ:dc * SEQ + SEQ],
                                                  V[:, mt, (2 * h + dc) * P:(2 * h + dc + 1) * P],
                                                  XPT[:, h % 2, mt, :], start=(mt == 0), stop=(mt == 1))
                    mm.then_inc(xo_done.sem, 1)
                pe.wait_ge(xp_done.sem, xp_done.at(l, HEADS))
                pe.wait_ge(xo_lo.sem, xo_lo.at(l, 1))
                rows_product(l, U_WO, 0, [0], CH, CL, True, False)
                rows_product(l, U_WO + 1, 0, [1], CH, CL, False, False)
                for i in range(3):
                    pe.wait_ge(xo_lo.sem, xo_lo.at(l, 2 + i))
                    rows_product(l, U_WO + 2 + i, 0, [2 + 2 * i, 3 + 2 * i], CH, CL, False, i == 2)

            pe.wait_ge(mem_loaded.sem, 16)
            for t in range(TT):
                for half in range(2):
                    for i in range(4):
                        c = 4 * half + i
                        mm = nc.tensor.transpose(PS[:, 2 * t + half, i * P:i * P + P],
                                                 MEMX[:, t, c * P:c * P + P], ident)
                    mm.then_inc(xT_psum.sem, 1)
            pe.wait_ge(x_loaded.sem, 16)
            with pe.Fori(0, DEPTH) as l:
                pe.wait_ge(x_ready.sem, x_ready.at(l, 0))
                turn_x(l, 0, X)
                pe.wait_ge(xT_hi.sem, xT_hi.at(l, 4))
                pe.wait_ge(xT_lo.sem, xT_lo.at(l, 4))
                ffn(l, 0)
                turn_x(l, 1, X)
                mix(l)
                turn_x(l, 2, X)
                xattn(l)
                turn_x(l, 3, X)
                pe.wait_ge(xT_hi.sem, xT_hi.at(l, 16))
                pe.wait_ge(xT_lo.sem, xT_lo.at(l, 16))
                ffn(l, 1)

        @block.scalar
        def _(act):
            def copy(dst, src):
                return nc.scalar.activation(dst, src, ACT.Copy)

            def split(l, u, j=0, half=False):
                s = u % RING
                n = 1024 if half else 2048
                act.wait_ge(raw_loaded[s].sem, raw_loaded[s].at(l, 32 * (u // RING + 1) + 32 * j))
                act.wait_ge(unit_used.sem, unit_used.at(l, u - RING + 1 + 3 * j))
                copy(WH[s][:, 0:n], RAW[s][:, 0:n]).then_inc(split_hi.sem, 1)

            def turned(l, n):
                for t in range(TT):
                    for half in range(2):
                        act.wait_ge(xT_psum.sem, xT_psum.at(l, 4 * n + 2 * t + half + 1))
                        copy(XH[:, 4 * half:4 * half + 4, t * P:t * P + P],
                             PS[:, 4 + 2 * t + half, :].rearrange("p (c n) -> p c n", c=4)).then_inc(xT_hi.sem, 1)

            def h_hi(l, s, blk):
                act.wait_ge(hT_psum.sem, hT_psum.at(l, 11 * s + blk + 1))
                copy(HH[:, :, :], PS[:, 6, :].rearrange("p (c n) -> p c n", c=2)).then_inc(hT_hi.sem, 1)

            def ffn(l, s):
                b = U_FFN[s]
                if s == 0:
                    for u in range(3):
                        split(l, b + u)
                split(l, b + 3)
                split(l, b + 4)
                silu_first(l, s)

                def step(j, jj, last):
                    h_hi(l, s, j)
                    split(l, b + 5, jj)
                    if not last:
                        split(l, b + 6, jj)
                    silu_next(l, s, j)
                    if not last:
                        split(l, b + 7, jj)

                with act.Fori(0, BLOCKS - 2) as j:
                    step(j, j, False)
                step(BLOCKS - 2, BLOCKS - 2, True)
                h_hi(l, s, BLOCKS - 1)

            def silu_at(l, s, blk, value_gu, value_used):
                act.wait_ge(gu_done.sem, gu_done.at(l, value_gu))
                nc.scalar.activation(SG[:, 0, :], PS[:, 4, 0:FB], ACT.Silu).then_inc(sg_done.sem, 1)
                act.wait_ge(unit_used.sem, unit_used.at(l, value_used))
                nc.scalar.activation(SG[:, 1, :], PS[:, 5, 0:FB], ACT.Silu).then_inc(sg_done.sem, 1)

            def silu_first(l, s):
                silu_at(l, s, 0, 11 * s + 1, U_FFN[s] + 2)

            def silu_next(l, s, j):
                silu_at(l, s, j + 1, j + (11 * s + 2), j * 3 + (U_FFN[s] + 4))

            def evac(l, event, n, dst, src, done, wait_used=None):
                if wait_used is None:
                    act.wait_ge(event.sem, event.at(l, n))
                else:
                    act.wait_ge(unit_used.sem, unit_used.at(l, wait_used + 1))
                return copy(dst, src).then_inc(done.sem, 1)

            def kv_out(l, i):
                if i < 4:
                    b = (3, 0, 1, 3)[i]
                    evac(l, None, 0, KT[:, 2 * i:2 * i + 2, :], PS[:, b, :].rearrange("p (f n) -> p f n", f=2),
                         kv_read, U_K + i)
                else:
                    c, t = (i - 4) // 2, i % 2
                    evac(l, None, 0, V[:, t, 512 * c:512 * c + 512], bank(t), kv_read, U_V + 2 * c + 1)

            def tq_out(l, i):
                dst = (DQT, DKT)[i // 2]
                h = 2 * (i % 2)
                evac(l, tq_done, i + 1, dst[:, h:h + 2, :], PS[:, 6 + i % 2, :].rearrange("p (h n) -> p h n", h=2),
                     tq_read)

            def decay(l, h):
                act.wait_ge(decay_in.sem, decay_in.at(l, h + 1))
                nc.scalar.activation(SDA[:, h, :], SDA[:, h, :], ACT.Exp, scale=-1.0).then_inc(decay_done.sem, 1)

            def diff_exp(l, i):
                act.wait_ge(ds_max.sem, ds_max.at(l, i + 1))
                m = i % 2
                for t, (a, b) in enumerate(((0, P), (P, 384))):
                    e = nc.scalar.activation(PR[:, m, a:b], ES[:, m, a:b], ACT.Exp, scale=0.125,
                                             bias=SM[:, 4 * m + t:4 * m + t + 1],
                                             accum_out=SM[:, 8 + 4 * m + t:8 + 4 * m + t + 1])
                e.then_inc(dp_done.sem, 1)

            def diff_evac(l, h):
                act.wait_ge(daT_done.sem, daT_done.at(l, h + 1))
                copy(AT[:, :], PS[:, 4, 0:384]).then_inc(daT_read.sem, 1)
                act.wait_ge(do_done.sem, do_done.at(l, h + 1))
                copy(CAT[:, :, h * P:h * P + P], PS[:, 5, 0:256].rearrange("p (t n) -> p t n", t=2))\
                    .then_inc(do_read.sem, 1)

            def mix(l):
                split(l, U_DQ)
                evac(l, None, 0, UT[:, :, :], PS[:, 6, :].rearrange("p (f n) -> p f n", f=2), ut_ready, U_SU)
                evac(l, gate_done, 1, SM[:, 200:216], PS[:, 7, 0:16], gate_tok)
                split(l, U_DQ + 1)
                act.wait_ge(cin_zero.sem, cin_zero.at(l, 1))
                evac(l, None, 0, CIN[:, 0:2, 3:3 + SEQ], PS[:, 4, :].rearrange("p (f n) -> p f n", f=2), mqk_read, U_MQ)
                split(l, U_DK)
                evac(l, None, 0, CIN[:, 2:4, 3:3 + SEQ], PS[:, 5, :].rearrange("p (f n) -> p f n", f=2), mqk_read, U_MK)
                split(l, U_DK + 1)
                split(l, U_DV)
                for t in range(TT):
                    evac(l, None, 0, QK[:, t, 0:512], bank(t), proj_read, U_DQ + 1)
                act.wait_ge(gate_abs.sem, gate_abs.at(l, 1))
                nc.scalar.activation(ROW[:, 5, :], ROW[:, 5, :], ACT.Exp).then_inc(act_link.sem, 1)
                act.wait_ge(act_link.sem, act_link.at(l, 2))
                nc.scalar.activation(ROW[:, 5, :], ROW[:, 5, :], ACT.Ln, bias=ones_c[0:4, 0:1]).then_inc(gate_log.sem, 1)
                split(l, U_DV + 1)
                split(l, U_MM)
                for t in range(TT):
                    evac(l, None, 0, QK[:, t, 512:1024], bank(2 + t), proj_read, U_DK + 1)
                act.wait_ge(conv_done.sem, conv_done.at(l, 4))
                nc.scalar.activation(COUT[:, :, :], COUT[:, :, :], ACT.Silu).then_inc(silu_done.sem, 1)
                split(l, U_MM + 1)
                split(l, U_K)
                for t in range(TT):
                    evac(l, None, 0, DV[:, t, :], bank(4 + t), proj_read, U_DV + 1)
                split(l, U_K + 1)
                split(l, U_K + 2)
                for t in range(TT):
                    act.wait_ge(unit_used.sem, unit_used.at(l, U_MM + 2))
                    copy(VA[:, t, :, 0:64], PS[:, t, 0:256].rearrange("p (h d) -> p h d", h=HEADS))
                    nc.scalar.activation(SIGO[:, t, :], PS[:, t, 256:512], ACT.Sigmoid).then_inc(proj_read.sem, 1)
                split(l, U_K + 3)
                kv_out(l, 0)
                act.wait_ge(cols_done.sem, cols_done.at(l, 1))
                copy(SM[:, 184:200], PS[:, 4, 0:16]).then_inc(cols_read.sem, 1)
                act.wait_ge(cols_read.sem, cols_read.at(l, 1))
                nc.scalar.activation(SM[:, 192:200], SM[:, 192:200], ACT.Exp).then_inc(exp_m.sem, 1)
                split(l, U_V)
                kv_out(l, 1)
                split(l, U_V + 1)
                kv_out(l, 2)
                decay(l, 0)
                decay(l, 1)
                tq_out(l, 0)
                decay(l, 2)
                decay(l, 3)
                split(l, U_V + 2)
                kv_out(l, 3)
                tq_out(l, 1)
                tq_out(l, 2)
                tq_out(l, 3)
                split(l, U_V + 3)
                act.wait_ge(ys_read.sem, ys_read.at(l, 1))
                nc.scalar.activation(UT[:, :, :], UT[:, :, :], ACT.Gelu_apprx_tanh).then_inc(gelu_done.sem, 1)
                diff_exp(l, 0)
                diff_exp(l, 1)
                split(l, U_WOUT, half=True)
                kv_out(l, 4)
                kv_out(l, 5)
                act.wait_ge(glu_done.sem, glu_done.at(l, 1))
                for f in range(2):
                    g = nc.scalar.activation(COUT[:, f, :], PS[:, 3, f * SEQ:f * SEQ + SEQ], ACT.Sigmoid,
                                             bias=PAR[:, P_GLUB + f:P_GLUB + f + 1])
                g.then_inc(glu_sig.sem, 1)
                split(l, U_WOUT + 1, half=True)
                split(l, U_WOUT + 2)
                kv_out(l, 6)
                kv_out(l, 7)
                act.wait_ge(c_hi_in.sem, c_hi_in.at(l, 1))
                copy(CH[:, 6:8, :], COUT[:, 0:2, :]).then_inc(c_hi.sem, 1)
                diff_exp(l, 2)
                diff_exp(l, 3)
                diff_evac(l, 0)
                diff_exp(l, 4)
                diff_exp(l, 5)
                diff_evac(l, 1)
                act.wait_ge(catT_done.sem, catT_done.at(l, 1))
                copy(CH[:, 4:6, :], PS[:, 2, :].rearrange("p (c n) -> p c n", c=2)).then_inc(cat_hi.sem, 1)
                diff_exp(l, 6)
                diff_exp(l, 7)
                diff_evac(l, 2)
                split(l, U_WOUT + 3)
                diff_evac(l, 3)
                split(l, U_WOUT + 4)
                for i in range(2):
                    act.wait_ge(catT_done.sem, catT_done.at(l, 2 + i))
                    copy(CH[:, 2 * i:2 * i + 2, :], PS[:, 6 + i, :].rearrange("p (c n) -> p c n", c=2))\
                        .then_inc(cat_hi.sem, 1)
                split(l, U_WQ)
                split(l, U_WQ + 1)
                split(l, U_WQ + 2)

            def xattn(l):
                for i in range(4):
                    u = (U_WQ + 3, U_WO, U_WO + 1, U_WO + 2)[i]
                    split(l, u, half=i in (1, 2))
                    evac(l, None, 0, QX[:, 2 * i:2 * i + 2, :], PS[:, 4 + i, :].rearrange("p (f n) -> p f n", f=2),
                         qx_read, U_WQ + i)
                for h in range(HEADS):
                    act.wait_ge(xs_max.sem, xs_max.at(l, h + 1))
                    if h >= 1:
                        act.wait_ge(xpT_done.sem, xpT_done.at(l, h))
                    for t in range(TT):
                        e = nc.scalar.activation(XP[:, t, :], PS[:, h, t * SEQ:t * SEQ + SEQ], ACT.Exp, scale=0.0625,
                                                 bias=SM[:, 2 * h + t:2 * h + t + 1],
                                                 accum_out=SM[:, 8 + 2 * h + t:9 + 2 * h + t])
                    e.then_inc(xp_done.sem, 1)
                    act.wait_ge(xpT_done.sem, xpT_done.at(l, h + 1))
                    copy(XPT[:, h % 2, :, :], PS[:, 4 + h % 2, :].rearrange("p (m n) -> p m n", m=2))\
                        .then_inc(xpT_read.sem, 1)
                    act.wait_ge(xo_done.sem, xo_done.at(l, h + 1))
                    copy(CH[:, 2 * h:2 * h + 2, :], PS[:, 6 + h % 2, :].rearrange("p (m n) -> p m n", m=2))\
                        .then_inc(xo_hi.sem, 1)
                split(l, U_WO + 3)
                split(l, U_WO + 4)
                for u in range(3):
                    split(l, U_FFN[1] + u)

            for i in range(4):
                act.wait_ge(xT_psum.sem, i + 1)
                t, half = i // 2, i % 2
                copy(MH[:, 4 * half:4 * half + 4, t * P:t * P + P], PS[:, i, :].rearrange("p (c n) -> p c n", c=4))\
                    .then_inc(xT_hi.sem, 1)
            act.wait_ge(setup_phase.sem, 1)
            nc.scalar.activation(SW[:, 0:32], SW[:, 0:32], ACT.Sin, scale=TWO_PI).then_inc(setup_sin.sem, 1)
            with act.Fori(0, DEPTH) as l:
                turned(l, 0)
                ffn(l, 0)
                act.wait_ge(phase_ready.sem, phase_ready.at(l, 1))
                nc.scalar.activation(ESN[:, :, :], ESN[:, :, :], ACT.Sin, scale=TWO_PI).then_inc(act_link.sem, 1)
                nc.scalar.activation(EC[:, :, :], EC[:, :, :], ACT.Sin, scale=TWO_PI).then_inc(table_ready.sem, 1)
                act.wait_ge(param_in.sem, param_in.at(l, 16))
                copy(GWH[:, :, :], PAR[:, P_GW:P_GW + 64].rearrange("p (c g) -> p c g", c=KC)).then_inc(gw_hi.sem, 1)
                for u in range(3):
                    split(l, U_SU + u)
                turned(l, 1)
                mix(l)
                turned(l, 2)
                xattn(l)
                turned(l, 3)
                ffn(l, 1)

        @block.vector
        def _(dve):
            v = nc.vector
            count = {"n": 0}
            layer = {}

            def link(ins):
                count["n"] += 1
                if layer:
                    ins.then_inc(dve_link.sem, 1)
                    dve.wait_ge(dve_link.sem, dve_link.at(layer["l"], count["n"]))
                else:
                    ins.then_inc(dve_setup.sem, 1)
                    dve.wait_ge(dve_setup.sem, count["n"])

            def low(dst, full, hi):
                return v.tensor_tensor(dst, full, hi.bitcast(F32), ALU.subtract)

            def split(l, u, j=0, half=False):
                s = u % RING
                n = 1024 if half else 2048
                dve.wait_ge(split_hi.sem, split_hi.at(l, u + 1 + 3 * j))
                low(WL[s][:, 0:n], RAW[s][:, 0:n], WH[s][:, 0:n]).then_inc(split_lo.sem, 1)

            def rsqrt(dst, src, n, work):
                a, b = SM[:, work:work + n], SM[:, work + n:work + 2 * n]
                link(v.tensor_scalar(b.bitcast(I32), src.bitcast(I32), 1, None, ALU.logical_shift_right))
                link(v.tensor_scalar(dst.bitcast(I32), b.bitcast(I32), -1.0, 1597463007.0, ALU.mult, ALU.add))
                for _ in range(3):
                    link(v.scalar_tensor_tensor(a, dst, -0.5, dst, ALU.mult, ALU.mult))
                    link(v.tensor_tensor(a, a, src, ALU.mult))
                    link(v.scalar_tensor_tensor(dst, a, 1.5, dst, ALU.add, ALU.mult))

            def norm(l, n, last_unit):
                c = (0.5 if n in (0, 3) else 1.0) / ALPHA
                dve.wait_ge(unit_used.sem, unit_used.at(l, last_unit + 1))
                for t in range(TT):
                    v.scalar_tensor_tensor(X[:, t, :], Y[:, t, :], c, X[:, t, :], ALU.mult, ALU.add)\
                        .then_inc(ln_sum.sem, 1)
                for t in range(TT):
                    dve.wait_ge(ln_sum.sem, ln_sum.at(l, TT * n + t + 1))
                    for half in range(2):
                        o = 16 + 12 * t + 6 * half
                        v.bn_stats(SM[:, o:o + 6], X[:, t, 512 * half:512 * half + 512]).then_inc(ln_stat.sem, 1)
                for t in range(TT):
                    dve.wait_ge(ln_stat.sem, ln_stat.at(l, 4 * n + 2 * t + 2))
                    dve.sem_inc(waits_apart.sem, 1)
                    link(v.bn_aggr(SM[:, 40 + 2 * t:42 + 2 * t], SM[:, 16 + 12 * t:28 + 12 * t]))
                var = SM[:, 40:44].rearrange("p (t c) -> p t c", t=2)[:, :, 1]
                link(v.tensor_scalar(SM[:, 44:46], var, EPS / ALPHA ** 2, None, ALU.add))
                rsqrt(SM[:, 46:48], SM[:, 44:46], 2, 48)
                dve.wait_ge(gb_in.sem, gb_in.at(l, 32 * (n + 1)))
                for t in range(TT):
                    v.scalar_tensor_tensor(X[:, t, :], X[:, t, :], SM[:, 40 + 2 * t:41 + 2 * t], LNGB[:, 0, :],
                                           ALU.subtract, ALU.mult).then_inc(ln_mid.sem, 1)
                for t in range(TT):
                    dve.wait_ge(ln_mid.sem, ln_mid.at(l, TT * n + t + 1))
                    v.scalar_tensor_tensor(X[:, t, :], X[:, t, :], SM[:, 46 + t:47 + t], LNGB[:, 1, :],
                                           ALU.mult, ALU.add).then_inc(x_ready.sem, 1)

            def turned(l, n):
                for t in range(TT):
                    for half in range(2):
                        dve.wait_ge(xT_hi.sem, xT_hi.at(l, 4 * n + 2 * t + half + 1))
                        cs = slice(4 * half, 4 * half + 4)
                        low(XL[:, cs, t * P:t * P + P], PS[:, 4 + 2 * t + half, :].rearrange("p (c n) -> p c n", c=4),
                            XH[:, cs, t * P:t * P + P]).then_inc(xT_lo.sem, 1)

            def h_mul(l, s, base):
                for t in range(TT):
                    dve.wait_ge(sg_done.sem, sg_done.at(l, base + t))
                    v.tensor_tensor(HB[:, t, :], SG[:, t, :], PS[:, 4 + t, FB:2 * FB], ALU.mult).then_inc(h_ready.sem, 1)

            def ffn(l, s):
                b = U_FFN[s]
                if s == 0:
                    for u in range(3):
                        split(l, b + u)
                split(l, b + 3)
                split(l, b + 4)
                h_mul(l, s, 22 * s + 1)

                def step(j, jj, last):
                    dve.wait_ge(hT_hi.sem, hT_hi.at(l, jj + (11 * s + 1)))
                    low(HL[:, :, :], PS[:, 6, :].rearrange("p (c n) -> p c n", c=2), HH[:, :, :])\
                        .then_inc(hT_lo.sem, 1)
                    split(l, b + 5, jj)
                    if not last:
                        split(l, b + 6, jj)
                    h_mul(l, s, jj * 2 + (22 * s + 3))
                    if not last:
                        split(l, b + 7, jj)

                with dve.Fori(0, BLOCKS - 2) as j:
                    step(j, j, False)
                step(BLOCKS - 2, BLOCKS - 2, True)
                dve.wait_ge(hT_hi.sem, hT_hi.at(l, 11 * s + BLOCKS))
                low(HL[:, :, :], PS[:, 6, :].rearrange("p (c n) -> p c n", c=2), HH[:, :, :]).then_inc(hT_lo.sem, 1)

            def s5_turn_in(l, i):
                dve.wait_ge(bu_done.sem, bu_done.at(l, i + 1))
                if i == 0:
                    dve.wait_ge(table_ready.sem, table_ready.at(l, 1))
                if i >= 2:
                    dve.wait_ge(state_ready.sem, state_ready.at(l, i - 1))
                if i >= 1:
                    dve.wait_ge(z_ready.sem, z_ready.at(l, i))
                both = PS[:, 6 + i % 2, :].rearrange("p (c n) -> p c n", c=2)
                cos = EC[:, i:i + 1, :].to_broadcast([P, 2, SEQ])
                sin = ESN[:, i:i + 1, :].to_broadcast([P, 2, SEQ])
                v.tensor_tensor(ZW[:, :, :], both, cos, ALU.mult)
                v.tensor_tensor(ZT[:, :, :], both, sin, ALU.mult).then_inc(bu_read.sem, 1)
                dve.wait_ge(bu_read.sem, bu_read.at(l, i + 1))
                v.tensor_tensor(ZW[:, 0, :], ZW[:, 0, :], ZT[:, 1, :], ALU.add)
                link(v.tensor_tensor(ZW[:, 1, :], ZW[:, 1, :], ZT[:, 0, :], ALU.subtract))
                rad = CUR[:, R_RAD + i:R_RAD + i + 1].to_broadcast([P, SEQ])
                for part in range(2):
                    z = v.tensor_tensor_scan(ZS[:, i % 2, part, :], rad, ZW[:, part, :], 0.0, ALU.mult, ALU.add)
                z.then_inc(z_ready.sem, 1)

            def conv(l):
                for f in range(4):
                    dve.wait_ge(mqk_read.sem, mqk_read.at(l, f // 2 + 1))
                    w = P_CW + 4 * f
                    link(v.tensor_scalar(COUT[:, f, :], CIN[:, f, 0:SEQ], PAR[:, w:w + 1],
                                         PAR[:, P_CB + f:P_CB + f + 1], ALU.mult, ALU.add))
                    for j in range(1, 4):
                        ins = v.scalar_tensor_tensor(COUT[:, f, :], CIN[:, f, j:j + SEQ], PAR[:, w + j:w + j + 1],
                                                     COUT[:, f, :], ALU.mult, ALU.add)
                        if j < 3:
                            link(ins)
                        else:
                            ins.then_inc(conv_done.sem, 1)

            def gates_in(l):
                dve.wait_ge(gateT_done.sem, gateT_done.at(l, 1))
                v.tensor_scalar(ROW[:, 2, :], PS[0:4, 7, 0:SEQ], PAR[0:4, P_GB:P_GB + 1], None, ALU.add)
                link(v.tensor_scalar(ROW[:, 4, :], PS[0:4, 7, SEQ:2 * SEQ], PAR[0:4, P_GB + 1:P_GB + 2], None, ALU.add))
                v.tensor_scalar(ROW[:, 3, :], ROW[:, 4, :], -1.0, None, ALU.mult).then_inc(gate_read.sem, 1)
                dve.wait_ge(gate_read.sem, gate_read.at(l, 1))
                link(v.tensor_tensor(ROW[:, 5, :], ROW[:, 3, :], ROW[:, 4, :], ALU.min))
                v.tensor_scalar(ROW[:, 4, :], ROW[:, 4, :], 0.0, None, ALU.min).then_inc(gate_abs.sem, 1)

            def gates_out(l):
                dve.wait_ge(gate_log.sem, gate_log.at(l, 1))
                link(v.tensor_tensor(ROW[:, 4, :], ROW[:, 4, :], ROW[:, 5, :], ALU.subtract))
                one = ones_c[0:4, 0:1].to_broadcast([4, SEQ])
                link(v.tensor_tensor_scan(ROW[:, 5, :], one, ROW[:, 4, :], 0.0, ALU.mult, ALU.add))
                link(v.tensor_tensor(ROW[:, 1, :], ROW[:, 2, :], ROW[:, 5, :], ALU.subtract))
                link(v.tensor_scalar(ROW[:, 4, :], ROW[:, 1, :], 0.0, None, ALU.mult))
                link(v.tensor_tensor_scan(ROW[:, 0, :], ROW[:, 1, :], ROW[:, 4, :], 0.0, ALU.max, ALU.max))
                v.scalar_tensor_tensor(ROW[:, 3, :], ROW[:, 0, :], -1.0, ROW[:, 5, :], ALU.mult, ALU.subtract)\
                    .then_inc(rows_ready.sem, 1)

            def decay_args(l, h):
                dve.wait_ge(mbc_done.sem, mbc_done.at(l, h // 2 + 1))
                if h == 0:
                    dve.wait_ge(roped.sem, roped.at(l, 2))
                dve.wait_ge(cols_read.sem, cols_read.at(l, 1))
                m = PS[:, 5 - h // 2, (h % 2) * SEQ:(h % 2 + 1) * SEQ]
                v.scalar_tensor_tensor(SDA[:, h, 0:SEQ], m, SM[:, 184 + h:185 + h], tri[:, 0:SEQ],
                                       ALU.subtract, ALU.add)
                v.scalar_tensor_tensor(SDA[:, h, SEQ:384], m[:, P:SEQ], SM[:, 188 + h:189 + h], tri[:, SEQ:384],
                                       ALU.subtract, ALU.add).then_inc(decay_in.sem, 1)

            def decay_scores(l, h):
                dve.wait_ge(decay_done.sem, decay_done.at(l, h + 1))
                dve.wait_ge(ms_done.sem, ms_done.at(l, h + 1))
                v.scalar_tensor_tensor(SDA[:, h, :], PS[:, 5 - h % 2, 0:384], 0.125, SDA[:, h, :],
                                       ALU.mult, ALU.mult).then_inc(msd_ready.sem, 1)

            def mlstm_out(l):
                dve.wait_ge(num_done.sem, num_done.at(l, 2))
                dve.wait_ge(exp_m.sem, exp_m.at(l, 1))
                for t in range(TT):
                    n4 = PS[:, 5 - t, 0:260].rearrange("p (h d) -> p h d", h=HEADS)
                    den = SM[:, 120 + 4 * t:124 + 4 * t]
                    link(v.tensor_copy(den, n4[:, :, 64]))
                    link(v.scalar_tensor_tensor(den, den, -1.0, den, ALU.mult, ALU.max))
                    link(v.tensor_tensor(den, den, SM[:, 192 + 4 * t:196 + 4 * t], ALU.max))
                    link(v.reciprocal(den, den))
                    hv = CAT[:, t, 512:768].rearrange("p (h d) -> p h d", h=HEADS)
                    ins = v.tensor_tensor(hv, n4[:, :, 0:64], den.unsqueeze(2).to_broadcast([P, HEADS, 64]), ALU.mult)
                    if t == 0:
                        link(ins)
                    else:
                        ins.then_inc(num_read.sem, 1)
                        dve.wait_ge(num_read.sem, num_read.at(l, 1))
                for t in range(TT):
                    link(v.tensor_tensor(ZB[:, t, :], CAT[:, t, 512:768], CAT[:, t, 512:768], ALU.mult))
                link(v.tensor_reduce(SM[:, 128:136].rearrange("p (t h) -> p t h", t=2),
                                     ZB[:, :, :].rearrange("p t (h d) -> p t h d", h=HEADS), AX, ALU.add))
                link(v.tensor_scalar(SM[:, 128:136], SM[:, 128:136], 1.0 / 64, EPS, ALU.mult, ALU.add))
                rsqrt(SM[:, 136:144], SM[:, 128:136], 8, 144)
                for t in range(TT):
                    hv = CAT[:, t, 512:768].rearrange("p (h d) -> p h d", h=HEADS)
                    r = SM[:, 136 + 4 * t:140 + 4 * t].unsqueeze(2).to_broadcast([P, HEADS, 64])
                    link(v.tensor_tensor(hv, hv, r, ALU.mult))
                    link(v.tensor_tensor(CAT[:, t, 512:768], CAT[:, t, 512:768], PAR[:, P_MG:P_MG + 256], ALU.mult))
                    ins = v.tensor_tensor(CAT[:, t, 512:768], CAT[:, t, 512:768], SIGO[:, t, :], ALU.mult)
                    if t == 0:
                        link(ins)
                    else:
                        ins.then_inc(b_ready.sem, 1)

            def diff_max(l, i):
                m = i % 2
                dve.wait_ge(ds_done.sem, ds_done.at(l, i + 1))
                if i > 0 and m == 0:
                    dve.wait_ge(daT_done.sem, daT_done.at(l, i // 2))
                v.tensor_tensor(ES[:, m, :], PS[:, 6 + m, 0:384], cmask, ALU.add).then_inc(ds_masked.sem, 1)
                dve.wait_ge(ds_masked.sem, ds_masked.at(l, i + 1))
                v.tensor_reduce(SM[:, 12 + 4 * m + 4:13 + 4 * m + 4], ES[:, m, 0:P], AX, ALU.max)
                link(v.tensor_reduce(SM[:, 13 + 4 * m + 4:14 + 4 * m + 4], ES[:, m, P:384], AX, ALU.max))
                v.tensor_scalar(SM[:, 4 * m:4 * m + 2], SM[:, 16 + 4 * m:18 + 4 * m], -0.125, None, ALU.mult)\
                    .then_inc(ds_max.sem, 1)

            def diff_combine(l, h):
                dve.wait_ge(dp_done.sem, dp_done.at(l, 2 * h + 2))
                sums = SM[:, 8:16].rearrange("p (m c) -> p m c", m=2)[:, :, 0:2]
                inv = SM[:, 24:28].rearrange("p (m c) -> p m c", m=2)
                link(v.reciprocal(inv, sums))
                link(v.tensor_scalar(SM[:, 26:28], SM[:, 26:28], CUR[:, R_NLAM:R_NLAM + 1], None, ALU.mult))
                for t, (a, b) in enumerate(((0, P), (P, 384))):
                    v.tensor_scalar(ES[:, 0, a:b], PR[:, 0, a:b], SM[:, 24 + t:25 + t], None, ALU.mult)\
                        .then_inc(dc_mid.sem, 1)
                for t, (a, b) in enumerate(((0, P), (P, 384))):
                    dve.wait_ge(dc_mid.sem, dc_mid.at(l, 2 * h + t + 1))
                    ins = v.scalar_tensor_tensor(ES[:, 0, a:b], PR[:, 1, a:b], SM[:, 26 + t:27 + t], ES[:, 0, a:b],
                                                 ALU.mult, ALU.add)
                ins.then_inc(da_ready.sem, 1)

            def diff_norm(l):
                dve.wait_ge(do_read.sem, do_read.at(l, HEADS))
                for h in range(HEADS):
                    for t in range(TT):
                        ins = v.tensor_tensor_reduce(AQ[:, :], CAT[:, t, h * P:h * P + P], CAT[:, t, h * P:h * P + P],
                                                     1.0, 0.0, ALU.mult, ALU.add, SM[:, 160 + 2 * h + t:161 + 2 * h + t])
                        link(ins)
                link(v.tensor_scalar(SM[:, 160:168], SM[:, 160:168], 1.0 / P, EPS, ALU.mult, ALU.add))
                rsqrt(SM[:, 168:176], SM[:, 160:168], 8, 48)
                link(v.tensor_scalar(SM[:, 168:176], SM[:, 168:176], CUR[:, R_OML:R_OML + 1], None, ALU.mult))
                for h in range(HEADS):
                    for t in range(TT):
                        o = CAT[:, t, h * P:h * P + P]
                        ins = v.scalar_tensor_tensor(o, o, SM[:, 168 + 2 * h + t:169 + 2 * h + t],
                                                     PAR[:, P_DG:P_DG + P], ALU.mult, ALU.mult)
                ins.then_inc(a_ready.sem, 1)

            def cat_low(l, i, c, b):
                dve.wait_ge(cat_hi.sem, cat_hi.at(l, i + 1))
                low(CL[:, c:c + 2, :], PS[:, b, :].rearrange("p (c n) -> p c n", c=2), CH[:, c:c + 2, :])\
                    .then_inc(cat_lo.sem, 1)

            def mix(l):
                split(l, U_DQ)
                gates_in(l)
                split(l, U_DQ + 1)
                conv(l)
                split(l, U_DK)
                split(l, U_DK + 1)
                split(l, U_DV)
                s5_turn_in(l, 0)
                gates_out(l)
                split(l, U_DV + 1)
                s5_turn_in(l, 1)
                split(l, U_MM)
                s5_turn_in(l, 2)
                split(l, U_MM + 1)
                s5_turn_in(l, 3)
                split(l, U_K)
                s5_turn_in(l, 4)
                split(l, U_K + 1)
                s5_turn_in(l, 5)
                split(l, U_K + 2)
                s5_turn_in(l, 6)
                split(l, U_K + 3)
                s5_turn_in(l, 7)
                split(l, U_V)
                decay_args(l, 0)
                decay_args(l, 1)
                split(l, U_V + 1)
                decay_args(l, 2)
                decay_args(l, 3)
                dve.wait_ge(state_used.sem, state_used.at(l, TILES))
                for f in range(2):
                    ins = v.scalar_tensor_tensor(UT[:, f, :], UT[:, f, :], PAR[:, P_D + f:P_D + f + 1],
                                                 PS[:, 2, f * SEQ:f * SEQ + SEQ], ALU.mult, ALU.add)
                    if f == 0:
                        link(ins)
                    else:
                        ins.then_inc(ys_read.sem, 1)
                split(l, U_V + 2)
                split(l, U_V + 3)
                decay_scores(l, 0)
                decay_scores(l, 1)
                diff_max(l, 0)
                diff_max(l, 1)
                split(l, U_WOUT, half=True)
                decay_scores(l, 2)
                decay_scores(l, 3)
                dve.wait_ge(glu_sig.sem, glu_sig.at(l, 1))
                v.tensor_tensor(COUT[:, 0:2, :], COUT[:, 0:2, :], UT[:, :, :], ALU.mult).then_inc(c_hi_in.sem, 1)
                mlstm_out(l)
                split(l, U_WOUT + 1, half=True)
                split(l, U_WOUT + 2)
                dve.wait_ge(c_hi.sem, c_hi.at(l, 1))
                low(CL[:, 6:8, :], COUT[:, 0:2, :], CH[:, 6:8, :]).then_inc(c_lo.sem, 1)
                diff_combine(l, 0)
                diff_max(l, 2)
                diff_max(l, 3)
                diff_combine(l, 1)
                diff_max(l, 4)
                diff_max(l, 5)
                cat_low(l, 0, 4, 2)
                diff_combine(l, 2)
                diff_max(l, 6)
                diff_max(l, 7)
                diff_combine(l, 3)
                split(l, U_WOUT + 3)
                diff_norm(l)
                split(l, U_WOUT + 4)
                cat_low(l, 1, 0, 6)
                cat_low(l, 2, 2, 7)
                split(l, U_WQ)
                split(l, U_WQ + 1)
                split(l, U_WQ + 2)

            def xattn(l):
                for i in range(4):
                    split(l, (U_WQ + 3, U_WO, U_WO + 1, U_WO + 2)[i], half=i in (1, 2))
                for h in range(HEADS):
                    dve.wait_ge(xs_done.sem, xs_done.at(l, h + 1))
                    link(v.tensor_reduce(SM[:, 16 + 2 * h:18 + 2 * h],
                                         PS[:, h, :].rearrange("p (t n) -> p t n", t=2), AX, ALU.max))
                    v.tensor_scalar(SM[:, 2 * h:2 * h + 2], SM[:, 16 + 2 * h:18 + 2 * h], -0.0625, None, ALU.mult)\
                        .then_inc(xs_max.sem, 1)
                for h in range(HEADS):
                    dve.wait_ge(xp_done.sem, xp_done.at(l, h + 1))
                    link(v.reciprocal(SM[:, 24:26], SM[:, 8 + 2 * h:10 + 2 * h]))
                    for t in range(TT):
                        ins = v.tensor_scalar(XP[:, t, :], XP[:, t, :], SM[:, 24 + t:25 + t], None, ALU.mult)
                    ins.then_inc(xp_norm.sem, 1)
                    dve.wait_ge(xo_hi.sem, xo_hi.at(l, h + 1))
                    low(CL[:, 2 * h:2 * h + 2, :], PS[:, 6 + h % 2, :].rearrange("p (m n) -> p m n", m=2),
                        CH[:, 2 * h:2 * h + 2, :]).then_inc(xo_lo.sem, 1)
                split(l, U_WO + 3)
                split(l, U_WO + 4)
                for u in range(3):
                    split(l, U_FFN[1] + u)

            def exact_exp(dst, arg, n, w):
                k, r, p, i = (SW[:, w + n * a:w + n * a + n] for a in range(4))
                link(v.tensor_scalar(r, arg, -87.3, 88.7, ALU.max, ALU.min))
                link(v.tensor_scalar(k, r, 1.4426950408889634, MAGIC, ALU.mult, ALU.add))
                link(v.tensor_scalar(k, k, MAGIC, None, ALU.subtract))
                link(v.scalar_tensor_tensor(r, k, -0.693359375, r, ALU.mult, ALU.add))
                link(v.scalar_tensor_tensor(r, k, 2.12194440e-4, r, ALU.mult, ALU.add))
                link(v.tensor_scalar(p, r, 1.0 / 5040, None, ALU.mult))
                for f in (720, 120, 24, 6, 2, 1):
                    link(v.scalar_tensor_tensor(p, p, 1.0 / f, r, ALU.add, ALU.mult))
                link(v.tensor_scalar(p, p, 1.0, None, ALU.add))
                link(v.tensor_scalar(i.bitcast(I32), k, 127.0, None, ALU.add))
                link(v.tensor_scalar(i.bitcast(I32), i.bitcast(I32), 23, None, ALU.logical_shift_left))
                link(v.tensor_tensor(p, p, i, ALU.mult))
                link(v.tensor_scalar(r, arg, -87.3, None, ALU.is_ge))
                link(v.tensor_tensor(dst, p, r, ALU.mult))

            def wrap(x, work):
                link(v.tensor_scalar(work, x, MAGIC, None, ALU.add))
                link(v.tensor_scalar(work, work, MAGIC, None, ALU.subtract))
                link(v.tensor_tensor(x, x, work, ALU.subtract))

            def prepare():
                are, aim, lst = SU[:, 0:16], SU[:, 16:32], SU[:, 32:48]
                step, th, ph, w = SW[:, 64:80], SW[:, 80:96], SW[:, 96:112], SW[:, 112:128]
                exact_exp(step, lst, 16, 256)
                link(v.tensor_tensor(th, aim, step, ALU.mult))
                link(v.tensor_scalar(ph, th, 0.15915494309189535, MAGIC, ALU.mult, ALU.add))
                link(v.tensor_scalar(ph, ph, MAGIC, None, ALU.subtract))
                for part in (6.28125, 0.0019350051879882812, 3.0199159819e-7):
                    link(v.scalar_tensor_tensor(th, ph, -part, th, ALU.mult, ALU.add))
                link(v.tensor_scalar(ph, th, 0.15915494309189535, None, ALU.mult))
                link(v.tensor_copy(SW[:, 0:16], ph))
                link(v.tensor_scalar(SW[:, 16:32], ph, 0.25, None, ALU.add))
                link(v.tensor_scalar(SW[:, 128:160], SW[:, 0:32], MAGIC, None, ALU.add))
                link(v.tensor_scalar(SW[:, 128:160], SW[:, 128:160], MAGIC, None, ALU.subtract))
                v.tensor_tensor(SW[:, 0:32], SW[:, 0:32], SW[:, 128:160], ALU.subtract).then_inc(setup_phase.sem, 1)

                def rec(c, n=8):
                    return REC[:, :, c:c + n]

                def two(ap):
                    return ap.rearrange("p (l i) -> p l i", l=DEPTH)

                link(v.tensor_scalar(w, ph, MAGIC12, None, ALU.add))
                link(v.tensor_scalar(w, w, MAGIC12, None, ALU.subtract))
                link(v.tensor_copy(rec(R_PHI), two(w)))
                link(v.tensor_tensor(rec(R_PLO), two(ph), two(w), ALU.subtract))
                link(v.tensor_tensor(th, are, step, ALU.mult))
                exact_exp(w, th, 16, 256)
                link(v.tensor_copy(rec(R_RAD), two(w)))
                dve.wait_ge(setup_sin.sem, 1)
                nr, ni, den, q = SW[:, 160:176], SW[:, 176:192], SW[:, 192:208], SW[:, 208:224]
                link(v.tensor_tensor(ni, w, SW[:, 0:16], ALU.mult))
                link(v.tensor_tensor(nr, w, SW[:, 16:32], ALU.mult))
                link(v.tensor_scalar(nr, nr, -1.0, None, ALU.add))
                link(v.tensor_tensor(den, are, are, ALU.mult))
                link(v.tensor_tensor(q, aim, aim, ALU.mult))
                link(v.tensor_tensor(den, den, q, ALU.add))
                link(v.reciprocal(den, den))
                link(v.tensor_tensor(q, nr, are, ALU.mult))
                link(v.tensor_tensor(w, ni, aim, ALU.mult))
                link(v.tensor_tensor(q, q, w, ALU.add))
                link(v.tensor_tensor(rec(R_FRE), two(q), two(den), ALU.mult))
                link(v.tensor_tensor(q, ni, are, ALU.mult))
                link(v.tensor_tensor(w, nr, aim, ALU.mult))
                link(v.tensor_tensor(q, q, w, ALU.subtract))
                link(v.tensor_tensor(rec(R_FIM), two(q), two(den), ALU.mult))
                dl = SU[:, 64:64 + DEPTH * 256].rearrange("p (i two d) -> p i two d", two=2, d=64)
                pr = SU[:, 640:640 + 256].rearrange("p (i d) -> p i d", d=64)
                link(v.tensor_tensor(pr, dl[:, :, 0, :], dl[:, :, 1, :], ALU.mult))
                link(v.tensor_reduce(SW[:, 224:228], pr, AX, ALU.add))
                exact_exp(SW[:, 228:232], SW[:, 224:228], 4, 256)
                e = SW[:, 228:232].rearrange("p (l i) -> p l i", l=2)
                link(v.tensor_tensor(rec(R_NLAM, 1), e[:, :, 1:2], e[:, :, 0:1], ALU.subtract))
                li = kst[:, K_LAM:K_LAM + 4].rearrange("p (a l) -> p l a", a=2)
                link(v.tensor_tensor(rec(R_NLAM, 1), rec(R_NLAM, 1), li[:, :, 0:1], ALU.subtract))
                link(v.tensor_copy(rec(R_OML, 1), li[:, :, 1:2]))

            dve.sem_inc(split_lo.sem, RING)
            link(v.memset(ones_c[:, :], 1.0))
            link(v.memset(VA[:, :, :, :], 1.0))
            link(v.memset(REC[:, :, :], 0.0))
            dve.wait_ge(const_in.sem, 16)
            for i in range(4):
                t, half = i // 2, i % 2
                dve.wait_ge(xT_hi.sem, i + 1)
                low(ML[:, 4 * half:4 * half + 4, t * P:t * P + P], PS[:, i, :].rearrange("p (c n) -> p c n", c=4),
                    MH[:, 4 * half:4 * half + 4, t * P:t * P + P]).then_inc(xT_lo.sem, 1)
            dve.wait_ge(setup_in.sem, 16)
            prepare()
            count["n"] = 0
            with dve.Fori(0, DEPTH) as l:
                layer["l"] = l
                v.tensor_copy(CUR[:, :], REC[:, l, :]).then_inc(cur_ready.sem, 1)
                v.memset(CIN[:, :, 0:3], 0.0).then_inc(cin_zero.sem, 1)
                turned(l, 0)
                ffn(l, 0)
                norm(l, 0, U_FFN[0] + 32)
                dve.wait_ge(gw_hi.sem, gw_hi.at(l, 1))
                low(GWL[:, :, :], PAR[:, P_GW:P_GW + 64].rearrange("p (c g) -> p c g", c=KC), GWH[:, :, :])\
                    .then_inc(gw_lo.sem, 1)
                for u in range(3):
                    split(l, U_SU + u)
                turned(l, 1)
                mix(l)
                norm(l, 1, U_WOUT + 4)
                turned(l, 2)
                xattn(l)
                norm(l, 2, U_WO + 4)
                turned(l, 3)
                ffn(l, 1)
                norm(l, 3, U_FFN[1] + 32)
            assert count["n"] == DVE_LINKS, count["n"]

        @block.gpsimd
        def _(pool):
            g = nc.gpsimd
            count = {"n": 0}
            layer = {}

            def link(ins):
                count["n"] += 1
                ins.then_inc(pool_link.sem, 1)
                pool.wait_ge(pool_link.sem, pool_link.at(layer["l"], count["n"]))
                pool.sem_inc(waits_apart.sem, 1)

            def load_gb(l, n):
                f = l * 4 + n
                pool.dma_start(LNGB[:, 0, :], lng_v[f].partition_broadcast(P)).then_inc(gb_in.sem, 16)
                pool.dma_start(LNGB[:, 1, :], lnb_v[f].partition_broadcast(P)).then_inc(gb_in.sem, 16)

            def tables(l):
                pool.wait_ge(cur_ready.sem, cur_ready.at(l, 1))
                pool.sem_inc(waits_apart.sem, 1)
                for i in range(TILES):
                    s, c = ESN[:, i, :], EC[:, i, :]
                    link(g.tensor_scalar(s, iota, CUR[:, R_PHI + i:R_PHI + i + 1], None, ALU.mult))
                    g.tensor_scalar(c, iota, CUR[:, R_PLO + i:R_PLO + i + 1], None, ALU.mult)
                    link(g.tensor_scalar(EF[:, :], s, MAGIC, MAGIC, ALU.add, ALU.subtract))
                    link(g.tensor_tensor(s, s, EF[:, :], ALU.subtract))
                    link(g.tensor_tensor(s, s, c, ALU.add))
                for i in range(TILES):
                    s, c = ESN[:, i, :], EC[:, i, :]
                    link(g.tensor_scalar(c, s, 0.25, None, ALU.add))
                    link(g.tensor_scalar(EF[:, :], c, MAGIC, MAGIC, ALU.add, ALU.subtract))
                    link(g.tensor_tensor(c, c, EF[:, :], ALU.subtract))
                    link(g.tensor_scalar(EF[:, :], s, MAGIC, MAGIC, ALU.add, ALU.subtract))
                    ins = g.tensor_tensor(s, s, EF[:, :], ALU.subtract)
                    if i < TILES - 1:
                        link(ins)
                    else:
                        ins.then_inc(phase_ready.sem, 1)

            def scale_c(l):
                pool.wait_ge(param_in.sem, param_in.at(l, 16))
                cre = PAR[:, P_C:P_C + 256].rearrange("p (i c) -> p i c", i=TILES)
                cim = PAR[:, P_C + 256:P_C + 512].rearrange("p (i c) -> p i c", i=TILES)
                fre = CUR[:, R_FRE:R_FRE + 8].unsqueeze(2).to_broadcast([P, TILES, 32])
                fim = CUR[:, R_FIM:R_FIM + 8].unsqueeze(2).to_broadcast([P, TILES, 32])
                w = EF[:, 0:256].rearrange("p (i c) -> p i c", i=TILES)
                link(g.tensor_tensor(CP[:, 0], cre, fre, ALU.mult))
                link(g.tensor_tensor(w, cim, fim, ALU.mult))
                link(g.tensor_tensor(CP[:, 0], CP[:, 0], w, ALU.subtract))
                link(g.tensor_tensor(CP[:, 1], cre, fim, ALU.mult))
                link(g.tensor_tensor(w, cim, fre, ALU.mult))
                link(g.tensor_tensor(CP[:, 1], CP[:, 1], w, ALU.add))
                g.tensor_scalar(CP[:, 1], CP[:, 1], -1.0, None, ALU.mult).then_inc(cp_ready.sem, 1)

            def rope(l, part):
                pool.wait_ge(proj_read.sem, proj_read.at(l, 2 * part + 2))
                for t in range(TT):
                    src = QK[:, t, 512 * part:512 * part + 512].rearrange("p (g two d) -> p g two d", g=8, two=2)
                    dst = RO[:, t, 512 * part:512 * part + 512].rearrange("p (g two d) -> p g two d", g=8, two=2)
                    w = PW[:, :].rearrange("p (g d) -> p g d", g=8)
                    cos = kst[:, K_COS + 32 * t:K_COS + 32 * t + 32].unsqueeze(1).to_broadcast([P, 8, 32])
                    sin = kst[:, K_SIN + 32 * t:K_SIN + 32 * t + 32].unsqueeze(1).to_broadcast([P, 8, 32])
                    link(g.tensor_tensor(dst[:, :, 0, :], src[:, :, 0, :], cos, ALU.mult))
                    link(g.tensor_tensor(w, src[:, :, 1, :], sin, ALU.mult))
                    link(g.tensor_tensor(dst[:, :, 0, :], dst[:, :, 0, :], w, ALU.subtract))
                    link(g.tensor_tensor(dst[:, :, 1, :], src[:, :, 1, :], cos, ALU.mult))
                    link(g.tensor_tensor(w, src[:, :, 0, :], sin, ALU.mult))
                    ins = g.tensor_tensor(dst[:, :, 1, :], dst[:, :, 1, :], w, ALU.add)
                    if t == 0:
                        link(ins)
                    else:
                        ins.then_inc(roped.sem, 1)

            def turn_back(l, i):
                pool.wait_ge(z_ready.sem, z_ready.at(l, i + 1))
                if i >= 2:
                    pool.wait_ge(state_used.sem, state_used.at(l, i - 1))
                z = ZS[:, i % 2]
                x = ZX[:, i % 2]
                cos = EC[:, i:i + 1, :].to_broadcast([P, 2, SEQ])
                sin = ESN[:, i:i + 1, :].to_broadcast([P, 2, SEQ])
                g.tensor_tensor(x, z, cos, ALU.mult)
                link(g.tensor_tensor(z, z, sin, ALU.mult))
                g.tensor_tensor(x[:, 0, :], x[:, 0, :], z[:, 1, :], ALU.subtract)
                g.tensor_tensor(x[:, 1, :], x[:, 1, :], z[:, 0, :], ALU.add).then_inc(state_ready.sem, 1)

            pool.dma_start(SU[:, 0:576], setup).then_inc(setup_in.sem, 16)
            with pool.Fori(0, DEPTH) as l:
                layer["l"] = l
                pool.wait_ge(x_ready.sem, x_ready.at(l, 0))
                pool.dma_start(PAR[:, :], par[l]).then_inc(param_in.sem, 16)
                load_gb(l, 0)
                pool.wait_ge(xT_psum.sem, 4)
                tables(l)
                scale_c(l)
                rope(l, 0)
                turn_back(l, 0)
                rope(l, 1)
                for i in range(1, TILES):
                    turn_back(l, i)
                pool.wait_ge(state_used.sem, state_used.at(l, TILES))
                load_gb(l, 1)
                pool.wait_ge(x_ready.sem, x_ready.at(l, 4))
                load_gb(l, 2)
                pool.wait_ge(x_ready.sem, x_ready.at(l, 6))
                load_gb(l, 3)
            assert count["n"] == POOL_LINKS, count["n"]


_INS = ["x", "mem", "ffn_w_gate", "ffn_w_up", "ffn_w_down", "ln_g", "ln_b", "w_in", "w_out", "xattn_wq",
        "xattn_wkv", "xattn_wo"]


def constants():
    k = np.zeros((P, K_END), np.float32)
    k[:, K_ID:K_ID + P] = np.eye(P)
    q = np.arange(P)
    k[:, K_CM:K_CM + P] = np.where(q[None, :] // CHUNK <= q[:, None] // CHUNK, 0.0, -1e30)
    k[:, K_CM + 256:K_CM + 384] = k[:, K_CM:K_CM + P]
    k[:, K_TRI:K_TRI + P] = np.where(q[:, None] > q[None, :], 1e30, 0.0)
    k[:, K_TRI + 256:K_TRI + 384] = k[:, K_TRI:K_TRI + P]
    inv = np.float32(10000.0) ** (-np.arange(0, 64, 2, dtype=np.float32) / np.float32(64))
    ang = np.arange(SEQ, dtype=np.float32)[:, None] * inv[None, :].astype(np.float32)
    for t in range(TT):
        k[:, K_COS + 32 * t:K_COS + 32 * t + 32] = np.cos(ang[t * P:t * P + P])
        k[:, K_SIN + 32 * t:K_SIN + 32 * t + 32] = np.sin(ang[t * P:t * P + P])
    k[:, K_IOTA:K_IOTA + SEQ] = np.arange(SEQ)
    k[:, K_LAM:K_LAM + DEPTH] = LAMBDA_INIT
    k[:, K_LAM + DEPTH:K_LAM + 2 * DEPTH] = [1.0 - v for v in LAMBDA_INIT]
    for h in range(HEADS):
        k[h, K_SEL + h * P:K_SEL + h * P + P] = 1.0
    return k


def lay_out(a):
    p = np.zeros((DEPTH, P, P_END), np.float32)
    s = np.zeros((P, 576), np.float32)
    for l in range(DEPTH):
        for g in range(GROUPS):
            tile, par = g // 2, g % 2
            row = (tile % 4) * 32 + par * 16
            for part, (b, c) in enumerate((("s5_b_re", "s5_c_re"), ("s5_b_im", "s5_c_im"))):
                col = P_B + part * 256 + (tile // 4) * P + par * 64
                p[l, row:row + 16, col:col + 64] = a[b][l, g].T
                col = P_C + part * 256 + tile * 32 + par * 16
                p[l, par * 64:par * 64 + 64, col:col + 16] = a[c][l, g].T
            s[par * 64:par * 64 + 64, 32 + l * 8 + tile] = a["s5_log_step"][l, g]
            s[par * 64:par * 64 + 64, l * 8 + tile] = a["s5_a_re"][l, g]
            s[par * 64:par * 64 + 64, 16 + l * 8 + tile] = a["s5_a_im"][l, g]
        p[l, :, P_GLU:P_GLU + 512] = a["s5_glu_w"][l].reshape(2, P, 256).transpose(1, 0, 2).reshape(P, 512)
        p[l, :, P_GLUB:P_GLUB + 2] = a["s5_glu_b"][l].reshape(2, P).T
        p[l, :, P_D:P_D + 2] = a["s5_d"][l].reshape(2, P).T
        p[l, :, P_CW:P_CW + 16] = a["conv_w"][l].reshape(4, 4, P).transpose(2, 1, 0).reshape(P, 16)
        p[l, :, P_CB:P_CB + 4] = a["conv_b"][l].reshape(4, P).T
        p[l, 0:4, P_GB:P_GB + 2] = a["mlstm_gate_b"][l].reshape(2, 4).T
        gw = a["w_in"][l][:, 2560:2568].reshape(KC, P, 8).transpose(1, 0, 2)
        p[l, :, P_GW:P_GW + 64] = gw.reshape(P, 64)
        p[l, :, P_DG:P_DG + P] = a["diff_norm_g"][l][None]
        p[l, :, P_MG:P_MG + 256] = a["mlstm_norm_g"][l][None]
        s[:, 64 + 256 * l:64 + 256 * l + 256] = a["diff_lambda"][l].reshape(1, 256)
    return p, s


def kernel(**inputs):
    import concourse.bacc as bacc
    from concourse.bass_utils import run_bass_kernel_spmd

    a = {k: np.asarray(v) for k, v in inputs.items()}
    par, setup = lay_out(a)
    arrays = {n: np.ascontiguousarray(a[n]) for n in _INS}
    arrays.update(params=par, setup=setup, constants=constants())
    nc = bacc.Bacc("TRN2", target_bir_lowering=False, num_devices=1)
    args = [nc.dram_tensor(f"in_{n}", v.shape, mybir.dt.from_np(v.dtype), kind="ExternalInput").ap()
            for n, v in arrays.items()]
    out = nc.dram_tensor("out", (1, SEQ, D), F32, kind="ExternalOutput").ap()
    build(nc, *args, out)
    r = run_bass_kernel_spmd(nc, [{f"in_{n}": v for n, v in arrays.items()}], core_ids=[0])
    return r.results[0]["out"]
```

```python
import math
from contextlib import ExitStack

import numpy as np

import concourse.bass as bass
from concourse import mybir

F32 = mybir.dt.float32
F32R = mybir.dt.float32r
I32 = mybir.dt.int32
ACT = mybir.ActivationFunctionType
ALU = mybir.AluOpType
AX = mybir.AxisListType.X

D = 1024
SEQ = 256
DEPTH = 2
FF = 2816
P = 128
KC = D // P
TT = SEQ // P
FB = 256
BLOCKS = FF // FB
HEADS = 4
CHUNK = 64
GROUPS = 16
TILES = GROUPS * 64 // P
ALPHA = (2 * DEPTH) ** 0.25
EPS = 1e-5
LAMBDA_INIT = [0.8 - 0.6 * math.exp(-0.3 * l) for l in range(DEPTH)]

U_FFN = (0, 66)
U_DQ, U_SU, U_MQ, U_MK, U_DK, U_DV, U_MM = 34, 36, 37, 38, 39, 41, 43
U_K = (33, 45, 46, 53)
U_V = 47
U_WOUT = (51, 52, 54, 55, 56)
U_WQ, U_WO = 57, 61
UNITS = 99
RING = 3
PER_SLOT = UNITS // RING

C_DQ, C_DK, C_DV, C_MQ, C_MK, C_MV, C_SU = 0, 512, 1024, 1536, 1792, 2048, 2568

K_ID, K_CM, K_TRI, K_COS, K_SIN, K_IOTA, K_LAM, K_SEL, K_END = 0, 128, 512, 896, 960, 1024, 1280, 1284, 1796

P_B, P_C, P_GLU, P_GLUB, P_D, P_CW, P_CB, P_GB, P_GW, P_DG, P_MG, P_ARE, P_AIM, P_LST, P_DL, P_END = (
    0, 512, 1024, 1536, 1538, 1540, 1556, 1560, 1562, 1626, 1754, 2010, 2018, 2026, 2034, 2290)

R_RAD, R_PHI, R_PLO, R_FRE, R_FIM, R_NLAM, R_END = 0, 8, 16, 24, 32, 40, 41

MAGIC = 12582912.0
MAGIC12 = 3072.0
TWO_PI = 6.2831850

DVE_LINKS, POOL_LINKS = 236, 112


def build(nc, x_in, mem_in, wg, wu, wd, ln_g, ln_b, w_in, w_out, wq, wkv, wo, par, const, out):
    wg_v = wg.rearrange("l s (c p) f -> (l s) p c f", p=P)
    wu_v = wu.rearrange("l s (c p) f -> (l s) p c f", p=P)
    wd_v = wd.rearrange("l s (c p) n -> (l s) c p n", p=P)
    win_v = w_in.rearrange("l (c p) n -> l p c n", p=P)
    wout_v = w_out.rearrange("l (c p) n -> l c p n", p=P)
    wq_v = wq.rearrange("l (c p) n -> l p c n", p=P)
    wkv_v = wkv.rearrange("l (c p) n -> l p c n", p=P)
    wo_v = wo.rearrange("l (c p) n -> l c p n", p=P)
    lng_v = ln_g.rearrange("l n d -> (l n) d")
    lnb_v = ln_b.rearrange("l n d -> (l n) d")

    ctx = ExitStack()
    with ctx:
        top = [(nc.sbuf_base + 31) // 32 * 32]

        def place(name, shape, dt, at=None):
            size = 4 * int(np.prod(shape[1:]))
            if at is None:
                at = top[0]
                top[0] += (size + 31) // 32 * 32
            return nc.alloc_sbuf_tensor_at(name, shape, dt, offset=at), at

        def sb(name, shape, dt=F32, at=None):
            return place(name, shape, dt, at)[0]

        kst = sb("kst", [P, K_END])
        X = sb("X", [P, TT, D])
        XH, xh_at = place("XH", [P, KC, SEQ], F32R)
        XL, xl_at = place("XL", [P, KC, SEQ], F32R)
        MH = sb("MH", [P, KC, SEQ], F32R)
        ML = sb("ML", [P, KC, SEQ], F32R)
        RAW = [sb(f"RAW{s}", [P, 2048]) for s in range(RING)]
        WH = [sb(f"WH{s}", [P, 2048], F32R) for s in range(RING)]
        WL = [sb(f"WL{s}", [P, 2048], F32R) for s in range(RING)]
        LNGB, gb_at = place("LNGB", [P, 2, D], F32)
        F8, f8_at = place("F8", [P, 2048], F32)
        KT = sb("KT", [P, KC, SEQ])
        V, v_at = place("V", [P, TT, D], F32)
        CH, ch_at = place("CH", [P, KC, SEQ], F32R)
        CL, cl_at = place("CL", [P, KC, SEQ], F32R)
        RQ, rq_at = place("RQ", [P, 2048], F32)
        DV = sb("DV", [P, TT, 512])
        VA = sb("VA", [P, TT, HEADS, 65])
        SIGO = sb("SIGO", [P, TT, 256])
        CIN, cin_at = place("CIN", [P, 4, SEQ + 3], F32)
        COUT, cout_at = place("COUT", [P, 4, SEQ], F32)
        UT = sb("UT", [P, 2, SEQ])
        PAR = sb("PAR", [P, P_END])
        CUR = sb("CUR", [P, R_END])
        GWH = sb("GWH", [P, KC, 8], F32R)
        GWL = sb("GWL", [P, KC, 8], F32R)
        CP = sb("CP", [P, 2, TILES, 32])
        SM = sb("SM", [P, 224])
        ones_c = sb("ones_c", [P, 1])

        HB = sb("HB", [P, TT, FB], F32, f8_at)
        SG = sb("SG", [P, TT, FB], F32, f8_at + 2048)
        HH = sb("HH", [P, 2, SEQ], F32R, f8_at + 4096)
        HL = sb("HL", [P, 2, SEQ], F32R, f8_at + 6144)
        QK = sb("QK", [P, TT, 1024], F32, f8_at)
        RO = sb("RO", [P, TT, 1024], F32, rq_at)
        CAT = sb("CAT", [P, TT, 768], F32, rq_at)
        QX = sb("QX", [P, KC, SEQ], F32, rq_at)
        MEMX = sb("MEMX", [P, TT, D], F32, rq_at)
        DQT = sb("DQT", [P, HEADS, SEQ], F32, xh_at)
        DKT = sb("DKT", [P, HEADS, SEQ], F32, xh_at + 4096)
        ES = sb("ES", [P, 2, 384], F32, xl_at)
        PR = sb("PR", [P, 2, 384], F32, xl_at + 3072)
        AT = sb("AT", [P, 384], F32, xl_at + 6144)
        DG = sb("DG", [P, P])
        AQ = sb("AQ", [P, 4, P], F32, f8_at + 6144)
        XP = sb("XP", [P, 2, 2, 256], F32, f8_at)
        XPT = sb("XPT", [P, 2, 2, 256], F32, f8_at + 4096)
        ZW = sb("ZW", [P, 2, SEQ], F32, gb_at)
        ZT = sb("ZT", [P, 2, SEQ], F32, gb_at + 2048)
        ZS = sb("ZS", [P, 2, 2, SEQ], F32, gb_at + 4096)
        EC = sb("EC", [P, TILES, SEQ], F32, ch_at)
        ESN = sb("ESN", [P, TILES, SEQ], F32, cl_at)
        EF = sb("EF", [P, SEQ], F32, rq_at)
        SW = sb("SW", [P, 512], F32, v_at)
        XG = sb("XG", [P, TT, D], F32, f8_at)
        HH2 = sb("HH2", [P, 2, SEQ], F32R, rq_at + 2048)
        HL2 = sb("HL2", [P, 2, SEQ], F32R, rq_at + 4096)

        ZX = sb("ZX", [P, 2, 2, SEQ], F32, cin_at)
        SDA = sb("SDA", [P, HEADS, 384], F32, f8_at)
        ZB = sb("ZB", [P, TT, 256], F32, f8_at + 6144)
        ROW = sb("ROW", [HEADS, 6, SEQ], F32, v_at)
        PW = sb("PW", [P, 256], F32, v_at + 6144)
        GATES = sb("GATES", [8, SEQ], F32, v_at + 7168)
        assert top[0] <= nc.sbuf_usable_end, (top[0], nc.sbuf_usable_end)

        PS = ctx.enter_context(nc.psum_tensor("PS", [P, 8, 512], F32))
        Y = PS[:, 0:4, :].rearrange("p b n -> p (b n)").rearrange("p (t n) -> p t n", t=TT)

        def bank(b):
            return PS[:, b, :]

        ident = kst[:, K_ID:K_ID + P]
        cmask = kst[:, K_CM:K_CM + 384]
        tri = kst[:, K_TRI:K_TRI + 384]
        iota = kst[:, K_IOTA:K_IOTA + SEQ]

        class Event:

            def __init__(self, name, per, first=0):
                self.sem, self.per, self.first = ctx.enter_context(nc.semaphore(name)), per, first

            def at(self, l, n):
                return l * self.per + (self.first + n)

        raw_loaded = [Event(f"raw_loaded{s}", 32 * PER_SLOT) for s in range(RING)]
        split_hi = Event("split_hi", UNITS)
        split_lo = Event("split_lo", UNITS, RING)
        unit_used = Event("unit_used", UNITS, RING)
        const_in = Event("const_in", 0)
        const_rest = Event("const_rest", 0)
        x_loaded = Event("x_loaded", 0)
        mem_loaded = Event("mem_loaded", 0)
        param_in = Event("param_in", 16)
        gb_in = Event("gb_in", 4 * 32)
        x_ready = Event("x_ready", 4 * TT, TT)
        xT_psum = Event("xT_psum", 4 * 4, 4)
        xT_hi = Event("xT_hi", 4 * 4, 4)
        xT_lo = Event("xT_lo", 4 * 4, 4)
        gu_done = Event("gu_done", 2 * BLOCKS)
        sg_done = Event("sg_done", 2 * BLOCKS * TT)
        h_ready = Event("h_ready", 2 * BLOCKS * TT)
        hT_psum = Event("hT_psum", 2 * BLOCKS)
        hT_hi = Event("hT_hi", 2 * BLOCKS)
        hT_lo = Event("hT_lo", 2 * BLOCKS)
        out_done = Event("out_done", 0)
        prep_sin = Event("prep_sin", 1)
        prep_phase = Event("prep_phase", 1)
        y_half = Event("y_half", 4)
        cur_ready = Event("cur_ready", 1)
        phase_ready = Event("phase_ready", 1)
        table_ready = Event("table_ready", 1)
        cp_ready = Event("cp_ready", 1)
        cin_zero = Event("cin_zero", 1)
        gw_hi = Event("gw_hi", 1)
        gw_lo = Event("gw_lo", 1)
        ut_ready = Event("ut_ready", 1)
        gate_done = Event("gate_done", 1)
        gate_tok = Event("gate_tok", 1)
        gateT_done = Event("gateT_done", 1)
        gate_read = Event("gate_read", 1)
        gate_abs = Event("gate_abs", 1)
        gate_log = Event("gate_log", 1)
        rows_ready = Event("rows_ready", 1)
        cols_done = Event("cols_done", 1)
        cols_read = Event("cols_read", 1)
        mbc_done = Event("mbc_done", 2)
        mqk_read = Event("mqk_read", 2)
        conv_done = Event("conv_done", 4)
        silu_done = Event("silu_done", 1)
        proj_read = Event("proj_read", 8)
        roped = Event("roped", 2)
        bu_done = Event("bu_done", TILES)
        bu_read = Event("bu_read", TILES)
        z_ready = Event("z_ready", TILES)
        state_ready = Event("state_ready", TILES)
        state_used = Event("state_used", TILES)
        ys_done = Event("ys_done", 1)
        ys_read = Event("ys_read", 1)
        gelu_done = Event("gelu_done", 1)
        glu_done = Event("glu_done", 1)
        glu_sig = Event("glu_sig", 1)
        c_hi_in = Event("c_hi_in", 1)
        c_hi = Event("c_hi", 1)
        c_lo = Event("c_lo", 1)
        kv_read = Event("kv_read", 8)
        tq_done = Event("tq_done", 4)
        tq_read = Event("tq_read", 4)
        decay_in = Event("decay_in", HEADS)
        decay_done = Event("decay_done", HEADS)
        ms_done = Event("ms_done", HEADS)
        msd_ready = Event("msd_ready", HEADS)
        num_done = Event("num_done", TT)
        num_read = Event("num_read", 1)
        ds_done = Event("ds_done", 8)
        ds_masked = Event("ds_masked", 8)
        ds_max = Event("ds_max", 8)
        dp_done = Event("dp_done", 8)
        da_ready = Event("da_ready", HEADS)
        daT_done = Event("daT_done", HEADS)
        daT_read = Event("daT_read", HEADS)
        do_done = Event("do_done", HEADS)
        do_read = Event("do_read", HEADS)
        ml_scale = Event("ml_scale", 1)
        b_ready = Event("b_ready", 1)
        a_ready = Event("a_ready", 2)
        catT_done = Event("catT_done", 3)
        cat_hi = Event("cat_hi", 3)
        cat_lo = Event("cat_lo", 3)
        qx_read = Event("qx_read", 4)
        xs_done = Event("xs_done", HEADS)
        xs_max = Event("xs_max", HEADS)
        xp_done = Event("xp_done", HEADS)
        xp_norm = Event("xp_norm", HEADS)
        xpT_done = Event("xpT_done", HEADS)
        xpT_read = Event("xpT_read", HEADS)
        xo_done = Event("xo_done", HEADS)
        xo_hi = Event("xo_hi", HEADS)
        xo_lo = Event("xo_lo", HEADS)
        dve_link = Event("dve_link", DVE_LINKS)
        pool_link = Event("pool_link", POOL_LINKS)

        act_link = Event("act_link", 2)
        exp_m = Event("exp_m", 1)
        ln_sum = Event("ln_sum", 4 * TT)
        ln_mean = Event("ln_mean", 4 * TT)
        ln_square = Event("ln_square", 4 * TT)
        ln_center = Event("ln_center", 4 * TT)
        dc_mid = Event("dc_mid", 2 * HEADS)

        waits_apart = Event("waits_apart", 0)


        block = ctx.enter_context(nc.Block())

        @block.sync
        def _(sp):
            sp.dma_start(ident, const[:, K_ID:K_ID + P]).then_inc(const_in.sem, 16)
            sp.dma_start(X[:, :, :], x_in.rearrange("b (t p) d -> p (b t) d", p=P)).then_inc(x_loaded.sem, 16)

            def load(l, u, j, first, second):
                sp.wait_ge(split_lo.sem, split_lo.at(l, u - RING + 1 + 3 * j))
                sp.sem_inc(waits_apart.sem, 1)
                s = u % RING
                for dst, src in (first, second):
                    sp.dma_start(dst, src).then_inc(raw_loaded[s].sem, 16)

            def load_gu(l, f, u, j, blk, half):
                r = RAW[u % RING][:, :].rearrange("p (c g n) -> p c g n", c=4, g=2)
                cs = slice(4 * half, 4 * half + 4)
                load(l, u, j, (r[:, :, 0, :], wg_v[f, :, cs, bass.ts(blk, FB)]),
                     (r[:, :, 1, :], wu_v[f, :, cs, bass.ts(blk, FB)]))

            def load_down(l, f, u, j, blk):
                r = RAW[u % RING][:, :].rearrange("p (c n) -> p c n", c=2)
                load(l, u, j, (r[:, 0, :], wd_v[f, blk * 2]), (r[:, 1, :], wd_v[f, blk * 2 + 1]))

            def load_rows(l, u, w, c0, n, cols):
                r = RAW[u % RING][:, 0:n * 512].rearrange("p (c n) -> p c n", c=n)
                h = n // 2
                load(l, u, 0, (r[:, 0:h, :], w[l, :, c0:c0 + h, cols]), (r[:, h:n, :], w[l, :, c0 + h:c0 + n, cols]))

            def load_cols(l, u, w, col):
                r = RAW[u % RING][:, :].rearrange("p (c n) -> p c n", c=KC)
                cols = slice(col, col + 256)
                load(l, u, 0, (r[:, 0:4, :], w[l, :, 0:4, cols]), (r[:, 4:8, :], w[l, :, 4:8, cols]))

            def load_pair(l, u, w, c):
                r = RAW[u % RING][:, :].rearrange("p (c n) -> p c n", c=2)
                load(l, u, 0, (r[:, 0, :], w[l, c]), (r[:, 1, :], w[l, c + 1]))

            def load_single(l, u, w, c):
                r = RAW[u % RING]
                load(l, u, 0, (r[:, 0:512], w[l, c, :, 0:512]), (r[:, 512:1024], w[l, c, :, 512:1024]))

            def load_ffn(l, s):
                b = U_FFN[s]
                f = l * 2 + s
                load_gu(l, f, b, 0, 0, 0)
                load_gu(l, f, b + 1, 0, 0, 1)
                with sp.Fori(0, BLOCKS - 1) as j:
                    load_gu(l, f, b + 2, j, j + 1, 0)
                    load_gu(l, f, b + 3, j, j + 1, 1)
                    load_down(l, f, b + 4, j, j)
                load_down(l, f, b + 32, 0, BLOCKS - 1)

            with sp.Fori(0, DEPTH) as l:
                load_ffn(l, 0)
                load_cols(l, U_K[0], wkv_v, 0)
                for half in range(2):
                    load_rows(l, U_DQ + half, win_v, 4 * half, 4, slice(C_DQ, C_DQ + 512))
                load_cols(l, U_SU, win_v, C_SU)
                load_cols(l, U_MQ, win_v, C_MQ)
                load_cols(l, U_MK, win_v, C_MK)
                for u, c in ((U_DK, C_DK), (U_DV, C_DV), (U_MM, C_MV)):
                    for half in range(2):
                        load_rows(l, u + half, win_v, 4 * half, 4, slice(c, c + 512))
                load_cols(l, U_K[1], wkv_v, 256)
                load_cols(l, U_K[2], wkv_v, 512)
                for i in range(4):
                    load_rows(l, U_V + i, wkv_v, 4 * (i % 2), 4, slice(D + 512 * (i // 2), D + 512 * (i // 2 + 1)))
                load_single(l, U_WOUT[0], wout_v, 6)
                load_single(l, U_WOUT[1], wout_v, 7)
                load_cols(l, U_K[3], wkv_v, 768)
                load_pair(l, U_WOUT[2], wout_v, 4)
                load_pair(l, U_WOUT[3], wout_v, 0)
                load_pair(l, U_WOUT[4], wout_v, 2)
                for i in range(4):
                    load_cols(l, U_WQ + i, wq_v, 256 * i)
                load_single(l, U_WO, wo_v, 0)
                load_single(l, U_WO + 1, wo_v, 1)
                for i in range(3):
                    load_pair(l, U_WO + 2 + i, wo_v, 2 + 2 * i)
                load_ffn(l, 1)
            sp.wait_ge(x_ready.sem, x_ready.at(DEPTH, 0))
            sp.dma_start(out.rearrange("b (t p) d -> p (b t) d", p=P), X[:, :, :]).then_inc(out_done.sem, 16)
            sp.wait_ge(out_done.sem, 16)

        @block.tensor
        def _(pe):
            pe.sem_inc(unit_used.sem, RING)
            pe.wait_ge(const_in.sem, 16)

            def prod(out_ap, sh, sl, mh, ml, first, last):
                nc.tensor.matmul(out_ap, sh, mh, start=first, stop=False)
                nc.tensor.matmul(out_ap, sh, ml, start=False, stop=False)
                return nc.tensor.matmul(out_ap, sl, mh, start=False, stop=last)

            def unit_ready(l, u, j=0):
                pe.wait_ge(split_lo.sem, split_lo.at(l, u + 1 + 3 * j))

            def gate_up_tile(u, half, t):
                wh = WH[u % RING][:, :].rearrange("p (c n) -> p c n", c=4)
                wl = WL[u % RING][:, :].rearrange("p (c n) -> p c n", c=4)
                tok = slice(t * P, t * P + P)
                for c in range(4):
                    k = 4 * half + c
                    mm = prod(bank(4 + t), XH[:, k, tok], XL[:, k, tok], wh[:, c, :], wl[:, c, :],
                              k == 0, k == KC - 1)
                return mm

            def gate_up(l, u, j, half):
                unit_ready(l, u, j)
                mm = gate_up_tile(u, half, 0)
                if half == 1:
                    mm.then_inc(gu_done.sem, 1)
                gate_up_tile(u, half, 1).then_inc(unit_used.sem, 1)

            def turn_h(l, s, blk):
                pe.wait_ge(h_ready.sem, h_ready.at(l, 22 * s + 2 * blk + 2))
                for fc in range(2):
                    for t in range(TT):
                        mm = nc.tensor.transpose(PS[:, 6, fc * SEQ + t * P:fc * SEQ + t * P + P],
                                                 HB[:, t, fc * P:fc * P + P], ident)
                mm.then_inc(hT_psum.sem, 1)

            def rows_tile(u, chunks, ah, al, t, first, last):
                n = len(chunks)
                wh = WH[u % RING][:, 0:n * D].rearrange("p (c n) -> p c n", c=n)
                wl = WL[u % RING][:, 0:n * D].rearrange("p (c n) -> p c n", c=n)
                tok = slice(t * P, t * P + P)
                for i, c in enumerate(chunks):
                    for half in range(2):
                        cols = slice(512 * half, 512 * half + 512)
                        mm = prod(bank(2 * t + half), ah[:, c, tok], al[:, c, tok], wh[:, i, cols], wl[:, i, cols],
                                  first and i == 0, last and i == n - 1)
                return mm

            def rows_product(l, u, j, chunks, ah, al, first, last):
                unit_ready(l, u, j)
                mm = rows_tile(u, chunks, ah, al, 0, first, last)
                if last:
                    mm.then_inc(y_half.sem, 1)
                rows_tile(u, chunks, ah, al, 1, first, last).then_inc(unit_used.sem, 1)

            def h_turned(l, s, blk):
                pe.wait_ge(hT_hi.sem, hT_hi.at(l, 11 * s + blk + 1))
                pe.wait_ge(hT_lo.sem, hT_lo.at(l, 11 * s + blk + 1))

            def turn_x(l, n, t):
                pe.wait_ge(x_ready.sem, x_ready.at(l, TT * (n - 1) + t + 1))
                for half in range(2):
                    if n == 1 and t == 1 and half == 1:
                        pe.wait_ge(kv_read.sem, kv_read.at(l, 1))
                    for i in range(4):
                        c = 4 * half + i
                        mm = nc.tensor.transpose(PS[:, 4 + 2 * t + half, i * P:i * P + P],
                                                 X[:, t, c * P:c * P + P], ident)
                    mm.then_inc(xT_psum.sem, 1)

            def turned(l, n, t):
                pe.wait_ge(xT_hi.sem, xT_hi.at(l, 4 * n + 2 * t + 2))
                pe.wait_ge(xT_lo.sem, xT_lo.at(l, 4 * n + 2 * t + 2))

            def ffn(l, s):
                b = U_FFN[s]
                n = 3 * s
                turn_x(l, n, 0)
                turned(l, n, 0)
                unit_ready(l, b)
                gate_up_tile(b, 0, 0)
                turn_x(l, n, 1)
                unit_ready(l, b + 1)
                gate_up_tile(b + 1, 1, 0).then_inc(gu_done.sem, 1)
                turned(l, n, 1)
                gate_up_tile(b, 0, 1).then_inc(unit_used.sem, 1)
                gate_up_tile(b + 1, 1, 1).then_inc(unit_used.sem, 1)

                unit_ready(l, b + 2)
                pe.wait_ge(h_ready.sem, h_ready.at(l, 22 * s + 1))
                gate_up_tile(b + 2, 0, 0)
                pe.wait_ge(h_ready.sem, h_ready.at(l, 22 * s + 2))
                gate_up_tile(b + 2, 0, 1).then_inc(unit_used.sem, 1)
                turn_h(l, s, 0)
                gate_up(l, b + 3, 0, 1)
                h_turned(l, s, 0)
                rows_product(l, b + 4, 0, [0, 1], HH, HL, True, False)
                with pe.Fori(1, BLOCKS - 2) as j:
                    pe.wait_ge(h_ready.sem, h_ready.at(l, j * 2 + (22 * s + 2)))
                    gate_up(l, b + 2, j, 0)
                    turn_h(l, s, j)
                    gate_up(l, b + 3, j, 1)
                    h_turned(l, s, j)
                    rows_product(l, b + 4, j, [0, 1], HH, HL, False, False)
                j = BLOCKS - 2
                pe.wait_ge(h_ready.sem, h_ready.at(l, j * 2 + (22 * s + 2)))
                gate_up(l, b + 2, j, 0)
                turn_h(l, s, j)
                gate_up(l, b + 3, j, 1)
                h_turned(l, s, j)
                unit_ready(l, b + 4, j)
                rows_tile(b + 4, [0, 1], HH, HL, 0, False, False)
                turn_h(l, s, j + 1)
                rows_tile(b + 4, [0, 1], HH, HL, 1, False, False).then_inc(unit_used.sem, 1)
                h_turned(l, s, j + 1)
                rows_product(l, b + 32, 0, [0, 1], HH2, HL2, False, True)

            def form_b_half(u, b, mh, ml, f):
                wh = WH[u % RING][:, :].rearrange("p (c n) -> p c n", c=KC)
                wl = WL[u % RING][:, :].rearrange("p (c n) -> p c n", c=KC)
                for c in range(KC):
                    cols = slice(f * P, f * P + P)
                    mm = prod(PS[:, b, f * SEQ:f * SEQ + SEQ], wh[:, c, cols], wl[:, c, cols],
                              mh[:, c, :], ml[:, c, :], c == 0, c == KC - 1)
                return mm

            def form_b(l, u, b, mh, ml):
                unit_ready(l, u)
                form_b_half(u, b, mh, ml, 0)
                form_b_half(u, b, mh, ml, 1).then_inc(unit_used.sem, 1)

            def form_a_tile(u, half, b, ah, al, t):
                wh = WH[u % RING][:, :].rearrange("p (c n) -> p c n", c=4)
                wl = WL[u % RING][:, :].rearrange("p (c n) -> p c n", c=4)
                tok = slice(t * P, t * P + P)
                for c in range(4):
                    k = 4 * half + c
                    mm = prod(bank(b + t), ah[:, k, tok], al[:, k, tok], wh[:, c, :], wl[:, c, :],
                              k == 0, k == KC - 1)
                return mm

            def form_a(l, u, half, b, ah, al):
                unit_ready(l, u)
                form_a_tile(u, half, b, ah, al, 0)
                form_a_tile(u, half, b, ah, al, 1).then_inc(unit_used.sem, 1)

            def s5_in(l, i):
                if i == 0:
                    pe.wait_ge(ut_ready.sem, ut_ready.at(l, 1))
                if i == 1:
                    pe.wait_ge(gate_read.sem, gate_read.at(l, 1))
                if i >= 2:
                    pe.wait_ge(bu_read.sem, bu_read.at(l, i - 1))
                r = 32 * (i % 4)
                for part in range(2):
                    o = P_B + part * 256 + (i // 4) * P
                    mm = nc.tensor.matmul(PS[:, 6 + i % 2, part * SEQ:part * SEQ + SEQ], PAR[r:r + 32, o:o + P],
                                          UT[r:r + 32, i // 4, :], start=True, stop=True)
                mm.then_inc(bu_done.sem, 1)

            def s5_out(l, i):
                pe.wait_ge(state_ready.sem, state_ready.at(l, i + 1))
                if i == 0:
                    pe.wait_ge(cp_ready.sem, cp_ready.at(l, 1))
                    pe.wait_ge(proj_read.sem, proj_read.at(l, 3))
                r = 32 * (i % 4)
                for part in range(2):
                    mm = nc.tensor.matmul(PS[r:r + 32, 2, (i // 4) * SEQ:(i // 4 + 1) * SEQ], CP[:, part, i, :],
                                          ZX[:, i % 2, part, :], start=(part == 0), stop=(part == 1))
                mm.then_inc(state_used.sem, 1)

            def mlstm_scores(l, h):
                b = 3 - h % 2
                if h == 0:
                    pe.wait_ge(silu_done.sem, silu_done.at(l, 1))
                    pe.wait_ge(kv_read.sem, kv_read.at(l, 2))
                if h == 1:
                    pe.wait_ge(ys_read.sem, ys_read.at(l, 1))
                if h >= 2:
                    pe.wait_ge(msd_ready.sem, msd_ready.at(l, h - 1))
                r = 64 * (h % 2)
                k = COUT[r:r + 64, 2 + h // 2, :]
                q = COUT[r:r + 64, h // 2, :]
                nc.tensor.matmul(PS[:, b, 0:256], k[:, 0:P], q[:, :], start=True, stop=True)
                nc.tensor.matmul(PS[:, b, 256:384], k[:, P:SEQ], q[:, P:SEQ], start=True, stop=True)\
                    .then_inc(ms_done.sem, 1)

            def mlstm_num(l):
                pe.wait_ge(msd_ready.sem, msd_ready.at(l, HEADS))
                for t in range(TT):
                    for h in range(HEADS):
                        o = PS[:, 3 - t, h * 65:h * 65 + 65]
                        if t == 0:
                            mm = nc.tensor.matmul(o, SDA[:, h, 0:P], VA[:, 0, h, :], start=True, stop=True)
                        else:
                            nc.tensor.matmul(o, SDA[:, h, P:2 * P], VA[:, 0, h, :], start=True, stop=False)
                            mm = nc.tensor.matmul(o, SDA[:, h, 2 * P:3 * P], VA[:, 1, h, :], start=False, stop=True)
                    mm.then_inc(num_done.sem, 1)

            def turn_q(l, i):
                if i == 0:
                    pe.wait_ge(roped.sem, roped.at(l, 2))
                if i < 2:
                    pe.wait_ge(bu_read.sem, bu_read.at(l, TILES - 1 + i))
                else:
                    pe.wait_ge(tq_read.sem, tq_read.at(l, i - 1))
                for hh in range(2):
                    for t in range(TT):
                        col = (i % 2) * 512 + (2 * (i // 2) + hh) * P
                        mm = nc.tensor.transpose(PS[:, 6 + i % 2, hh * SEQ + t * P:hh * SEQ + t * P + P],
                                                 RO[:, t, col:col + P], ident)
                mm.then_inc(tq_done.sem, 1)

            def diff_scores(l, h, m):
                i = 2 * h + m
                if i == 0:
                    pe.wait_ge(tq_read.sem, tq_read.at(l, 4))
                if i >= 2:
                    pe.wait_ge(ds_masked.sem, ds_masked.at(l, i - 1))
                r = 64 * m
                nc.tensor.matmul(PS[:, 6 + m, 0:P], DQT[r:r + 64, h, 0:P], DKT[r:r + 64, h, 0:P],
                                 start=True, stop=True)
                nc.tensor.matmul(PS[:, 6 + m, P:384], DQT[r:r + 64, h, P:SEQ], DKT[r:r + 64, h, :],
                                 start=True, stop=True).then_inc(ds_done.sem, 1)

            def diff_turn(l, h):
                pe.wait_ge(da_ready.sem, da_ready.at(l, h + 1))
                if h == 0:
                    pe.wait_ge(decay_in.sem, decay_in.at(l, HEADS))
                else:
                    pe.wait_ge(daT_read.sem, daT_read.at(l, h))
                for i in range(3):
                    mm = nc.tensor.transpose(PS[:, 4, i * P:i * P + P], ES[:, 0, i * P:i * P + P], ident)
                mm.then_inc(daT_done.sem, 1)

            def diff_out(l, h):
                pe.wait_ge(daT_read.sem, daT_read.at(l, h + 1))
                if h == 0:
                    pe.wait_ge(glu_sig.sem, glu_sig.at(l, 1))
                else:
                    pe.wait_ge(do_read.sem, do_read.at(l, h))
                v = slice(h * P, h * P + P)
                nc.tensor.matmul(PS[:, 5, 0:P], AT[:, 0:P], DV[:, 0, v], start=True, stop=True)
                nc.tensor.matmul(PS[:, 5, P:2 * P], AT[:, P:2 * P], DV[:, 0, v], start=True, stop=False)
                nc.tensor.matmul(PS[:, 5, P:2 * P], AT[:, 2 * P:3 * P], DV[:, 1, v], start=False, stop=True)\
                    .then_inc(do_done.sem, 1)

            def turn_cat(l, i, c0, b):
                for cc in range(2):
                    for t in range(TT):
                        c = c0 + cc
                        mm = nc.tensor.transpose(PS[:, b, cc * SEQ + t * P:cc * SEQ + t * P + P],
                                                 CAT[:, t, c * P:c * P + P], ident)
                mm.then_inc(catT_done.sem, 1)

            def cols(l):
                pe.wait_ge(proj_read.sem, proj_read.at(l, 6))
                pe.wait_ge(rows_ready.sem, rows_ready.at(l, 1))
                pe.sem_inc(waits_apart.sem, 1)
                for r in range(2):
                    for t in range(TT):
                        mm = nc.tensor.transpose(PS[:, 4, r * 8 + t * 4:r * 8 + t * 4 + 4],
                                                 ROW[:, 1 + 2 * r, t * P:t * P + P], ident[0:4, 0:4])
                mm.then_inc(cols_done.sem, 1)

            def spread(l, i):
                if i == 1:
                    pe.wait_ge(cols_read.sem, cols_read.at(l, 1))
                for h in range(2):
                    o = K_SEL + (2 * i + h) * P
                    mm = nc.tensor.matmul(PS[:, 5 - i, h * SEQ:h * SEQ + SEQ], kst[0:4, o:o + P], ROW[:, 0, :],
                                          start=True, stop=True)
                mm.then_inc(mbc_done.sem, 1)

            def mix(l):
                form_b(l, U_K[0], 7, MH, ML)
                turn_x(l, 1, 0)
                turned(l, 1, 0)
                unit_ready(l, U_DQ)
                form_a_tile(U_DQ, 0, 0, XH, XL, 0)
                turn_x(l, 1, 1)
                unit_ready(l, U_DQ + 1)
                form_a_tile(U_DQ + 1, 1, 0, XH, XL, 0)
                turned(l, 1, 1)
                form_a_tile(U_DQ, 0, 0, XH, XL, 1).then_inc(unit_used.sem, 1)
                form_a_tile(U_DQ + 1, 1, 0, XH, XL, 1).then_inc(unit_used.sem, 1)
                form_b(l, U_SU, 6, XH, XL)
                pe.wait_ge(gw_lo.sem, gw_lo.at(l, 1))
                for c in range(KC):
                    mm = prod(PS[0:8, 7, 0:SEQ], GWH[:, c, :], GWL[:, c, :], XH[:, c, :], XL[:, c, :],
                              c == 0, c == KC - 1)
                mm.then_inc(gate_done.sem, 1)
                form_b(l, U_MQ, 4, XH, XL)
                s5_in(l, 0)
                pe.wait_ge(gate_tok.sem, gate_tok.at(l, 1))
                pe.sem_inc(waits_apart.sem, 1)
                for g in range(2):
                    mm = nc.tensor.matmul(PS[0:4, 7, g * SEQ:g * SEQ + SEQ], ident[0:8, 4 * g:4 * g + 4],
                                          GATES[:, :], start=True, stop=True)
                mm.then_inc(gateT_done.sem, 1)
                form_b(l, U_MK, 5, XH, XL)
                form_a(l, U_DK, 0, 2, XH, XL)
                s5_in(l, 1)
                form_a(l, U_DK + 1, 1, 2, XH, XL)
                s5_in(l, 2)
                pe.wait_ge(mqk_read.sem, mqk_read.at(l, 2))
                form_a(l, U_DV, 0, 4, XH, XL)
                s5_out(l, 0)
                s5_in(l, 3)
                form_a(l, U_DV + 1, 1, 4, XH, XL)
                s5_out(l, 1)
                s5_in(l, 4)
                pe.wait_ge(proj_read.sem, proj_read.at(l, 2))
                form_a(l, U_MM, 0, 0, XH, XL)
                s5_out(l, 2)
                s5_in(l, 5)
                form_a(l, U_MM + 1, 1, 0, XH, XL)
                s5_out(l, 3)
                s5_in(l, 6)
                cols(l)
                pe.wait_ge(proj_read.sem, proj_read.at(l, 4))
                form_b(l, U_K[1], 3, MH, ML)
                s5_out(l, 4)
                s5_in(l, 7)
                turn_q(l, 0)
                spread(l, 0)
                spread(l, 1)
                pe.wait_ge(proj_read.sem, proj_read.at(l, 8))
                form_b(l, U_K[2], 0, MH, ML)
                s5_out(l, 5)
                turn_q(l, 1)
                turn_q(l, 2)
                pe.wait_ge(kv_read.sem, kv_read.at(l, 3))
                form_a(l, U_V, 0, 0, MH, ML)
                turn_q(l, 3)
                s5_out(l, 6)
                s5_out(l, 7)
                diff_scores(l, 0, 0)
                diff_scores(l, 0, 1)
                form_a(l, U_V + 1, 1, 0, MH, ML)
                mlstm_scores(l, 0)
                mlstm_scores(l, 1)
                diff_scores(l, 1, 0)
                diff_scores(l, 1, 1)
                diff_turn(l, 0)
                pe.wait_ge(gelu_done.sem, gelu_done.at(l, 1))
                for f in range(2):
                    for c in range(2):
                        o = P_GLU + c * 256 + f * P
                        mm = nc.tensor.matmul(PS[:, 5, f * SEQ:f * SEQ + SEQ], PAR[:, o:o + P], UT[:, c, :],
                                              start=(c == 0), stop=(c == 1))
                mm.then_inc(glu_done.sem, 1)
                pe.wait_ge(kv_read.sem, kv_read.at(l, 5))
                form_a(l, U_V + 2, 0, 0, MH, ML)
                diff_out(l, 0)
                mlstm_scores(l, 2)
                mlstm_scores(l, 3)
                diff_turn(l, 1)
                diff_scores(l, 2, 0)
                diff_scores(l, 2, 1)
                form_a(l, U_V + 3, 1, 0, MH, ML)
                mlstm_num(l)
                diff_out(l, 1)
                diff_turn(l, 2)
                diff_scores(l, 3, 0)
                diff_scores(l, 3, 1)
                pe.wait_ge(c_lo.sem, c_lo.at(l, 1))
                pe.wait_ge(num_read.sem, num_read.at(l, 1))
                pe.wait_ge(kv_read.sem, kv_read.at(l, 7))
                rows_product(l, U_WOUT[0], 0, [6], CH, CL, True, False)
                rows_product(l, U_WOUT[1], 0, [7], CH, CL, False, False)
                diff_out(l, 2)
                diff_turn(l, 3)
                pe.wait_ge(ds_masked.sem, ds_masked.at(l, 7))
                unit_ready(l, U_K[3])
                form_b_half(U_K[3], 6, MH, ML, 0)
                diff_out(l, 3)
                form_b_half(U_K[3], 6, MH, ML, 1).then_inc(unit_used.sem, 1)
                pe.wait_ge(b_ready.sem, b_ready.at(l, 1))
                pe.wait_ge(ds_masked.sem, ds_masked.at(l, 8))
                turn_cat(l, 0, 4, 7)
                pe.wait_ge(a_ready.sem, a_ready.at(l, 1))
                turn_cat(l, 1, 0, 4)
                pe.wait_ge(cat_lo.sem, cat_lo.at(l, 1))
                rows_product(l, U_WOUT[2], 0, [4, 5], CH, CL, False, False)
                pe.wait_ge(a_ready.sem, a_ready.at(l, 2))
                turn_cat(l, 2, 2, 5)
                pe.wait_ge(cat_lo.sem, cat_lo.at(l, 2))
                rows_product(l, U_WOUT[3], 0, [0, 1], CH, CL, False, False)
                pe.wait_ge(cat_lo.sem, cat_lo.at(l, 3))
                rows_product(l, U_WOUT[4], 0, [2, 3], CH, CL, False, True)

            def xattn(l):
                pe.wait_ge(kv_read.sem, kv_read.at(l, 8))
                turn_x(l, 2, 0)
                turn_x(l, 2, 1)
                turned(l, 2, 1)

                def scores(h):
                    pe.wait_ge(qx_read.sem, qx_read.at(l, h + 1))
                    for t in range(TT):
                        for c in range(2):
                            mm = nc.tensor.matmul(PS[:, h, t * SEQ:t * SEQ + SEQ],
                                                  QX[:, 2 * h + c, t * P:t * P + P], KT[:, 2 * h + c, :],
                                                  start=(c == 0), stop=(c == 1))
                    mm.then_inc(xs_done.sem, 1)

                def turn(h):
                    pe.wait_ge(xp_norm.sem, xp_norm.at(l, h + 1))
                    if h >= 2:
                        pe.wait_ge(xpT_read.sem, xpT_read.at(l, h - 1))
                    for mt in range(2):
                        for t in range(TT):
                            mm = nc.tensor.transpose(PS[:, 4 + h % 2, mt * SEQ + t * P:mt * SEQ + t * P + P],
                                                     XP[:, h % 2, t, mt * P:mt * P + P], ident)
                    mm.then_inc(xpT_done.sem, 1)

                def read(h):
                    pe.wait_ge(xpT_read.sem, xpT_read.at(l, h + 1))
                    if h < 2:
                        pe.wait_ge(qx_read.sem, qx_read.at(l, 4))
                    if h >= 2:
                        pe.wait_ge(xo_lo.sem, xo_lo.at(l, h - 1))
                    for dc in range(2):
                        for mt in range(2):
                            mm = nc.tensor.matmul(PS[:, 6 + h % 2, dc * SEQ:dc * SEQ + SEQ],
                                                  V[:, mt, (2 * h + dc) * P:(2 * h + dc + 1) * P],
                                                  XPT[:, h % 2, mt, :], start=(mt == 0), stop=(mt == 1))
                    mm.then_inc(xo_done.sem, 1)

                for i in range(4):
                    form_b(l, U_WQ + i, 4 + i, XH, XL)
                    if i > 0:
                        scores(i - 1)
                turn(0)
                scores(3)
                turn(1)
                read(0)
                turn(2)
                read(1)
                turn(3)
                read(2)
                pe.wait_ge(xp_done.sem, xp_done.at(l, HEADS))
                pe.wait_ge(xo_lo.sem, xo_lo.at(l, 1))
                rows_product(l, U_WO, 0, [0], CH, CL, True, False)
                read(3)
                rows_product(l, U_WO + 1, 0, [1], CH, CL, False, False)
                for i in range(3):
                    pe.wait_ge(xo_lo.sem, xo_lo.at(l, 2 + i))
                    rows_product(l, U_WO + 2 + i, 0, [2 + 2 * i, 3 + 2 * i], CH, CL, False, i == 2)

            pe.wait_ge(mem_loaded.sem, 16)
            for t in range(TT):
                for half in range(2):
                    for i in range(4):
                        c = 4 * half + i
                        mm = nc.tensor.transpose(PS[:, 2 * t + half, i * P:i * P + P],
                                                 MEMX[:, t, c * P:c * P + P], ident)
                    mm.then_inc(xT_psum.sem, 1)
            with pe.Fori(0, DEPTH) as l:
                ffn(l, 0)
                mix(l)
                xattn(l)
                ffn(l, 1)

        @block.scalar
        def _(act):
            def copy(dst, src):
                return nc.scalar.activation(dst, src, ACT.Copy)

            def split(l, u, j=0, half=False):
                s = u % RING
                n = 1024 if half else 2048
                act.wait_ge(raw_loaded[s].sem, raw_loaded[s].at(l, 32 * (u // RING + 1) + 32 * j))
                act.wait_ge(unit_used.sem, unit_used.at(l, u - RING + 1 + 3 * j))
                copy(WH[s][:, 0:n], RAW[s][:, 0:n]).then_inc(split_hi.sem, 1)

            def turned(l, n, t):
                for half in range(2):
                    act.wait_ge(xT_psum.sem, xT_psum.at(l, 4 * n + 2 * t + half + 1))
                    copy(XH[:, 4 * half:4 * half + 4, t * P:t * P + P],
                         PS[:, 4 + 2 * t + half, :].rearrange("p (c n) -> p c n", c=4)).then_inc(xT_hi.sem, 1)

            def square(l, n, t):
                act.wait_ge(ln_mean.sem, ln_mean.at(l, TT * n + t + 1))
                nc.scalar.activation(Y[:, t, :], X[:, t, :], ACT.Square, bias=SM[:, 18 + t:19 + t],
                                     accum_out=SM[:, 20 + t:21 + t]).then_inc(ln_square.sem, 1)

            def h_hi(l, s, blk, dst=HH):
                act.wait_ge(hT_psum.sem, hT_psum.at(l, 11 * s + blk + 1))
                copy(dst[:, :, :], PS[:, 6, :].rearrange("p (c n) -> p c n", c=2)).then_inc(hT_hi.sem, 1)

            def ffn(l, s):
                b = U_FFN[s]
                if s == 0:
                    split(l, b)
                    turned(l, 0, 0)
                    split(l, b + 1)
                    turned(l, 0, 1)
                    split(l, b + 2)
                act.wait_ge(gu_done.sem, gu_done.at(l, 11 * s + 1))
                silu(0)
                split(l, b + 3)
                act.wait_ge(unit_used.sem, unit_used.at(l, b + 2))
                silu(1)
                split(l, b + 4)

                def step(j, jj, last):
                    h_hi(l, s, j)
                    split(l, b + 5, jj)
                    silu_next(l, s, j)
                    if not last:
                        split(l, b + 6, jj)
                        split(l, b + 7, jj)

                step(0, 0, False)
                step(1, 1, False)
                if s == 0:
                    act.wait_ge(prep_phase.sem, prep_phase.at(l, 1))
                    nc.scalar.activation(SW[:, 0:16], SW[:, 0:16], ACT.Sin, scale=TWO_PI).then_inc(prep_sin.sem, 1)
                with act.Fori(2, BLOCKS - 2) as j:
                    step(j, j, False)
                step(BLOCKS - 2, BLOCKS - 2, True)
                if s == 0:
                    split(l, U_K[0])
                h_hi(l, s, BLOCKS - 1, HH2)
                if s == 0:
                    copy(GWH[:, :, :], PAR[:, P_GW:P_GW + 64].rearrange("p (c g) -> p c g", c=KC)).then_inc(gw_hi.sem, 1)

            def silu(t):
                nc.scalar.activation(SG[:, t, :], PS[:, 4 + t, 0:FB], ACT.Silu).then_inc(sg_done.sem, 1)

            def silu_next(l, s, j):
                act.wait_ge(gu_done.sem, gu_done.at(l, j + (11 * s + 2)))
                silu(0)
                act.wait_ge(unit_used.sem, unit_used.at(l, j * 3 + (U_FFN[s] + 4)))
                silu(1)

            def evac(l, event, n, dst, src, done, wait_used=None):
                if wait_used is None:
                    act.wait_ge(event.sem, event.at(l, n))
                else:
                    act.wait_ge(unit_used.sem, unit_used.at(l, wait_used + 1))
                return copy(dst, src).then_inc(done.sem, 1)

            def kv_out(l, i):
                if i < 4:
                    b = (7, 3, 0, 6)[i]
                    evac(l, None, 0, KT[:, 2 * i:2 * i + 2, :], PS[:, b, :].rearrange("p (f n) -> p f n", f=2),
                         kv_read, U_K[i])
                else:
                    c, t = (i - 4) // 2, i % 2
                    evac(l, None, 0, V[:, t, 512 * c:512 * c + 512], bank(t), kv_read, U_V + 2 * c + 1)

            def tq_out(l, i):
                dst = (DQT, DKT)[i % 2]
                h = 2 * (i // 2)
                evac(l, tq_done, i + 1, dst[:, h:h + 2, :], PS[:, 6 + i % 2, :].rearrange("p (h n) -> p h n", h=2),
                     tq_read)

            def decay(l, h):
                act.wait_ge(decay_in.sem, decay_in.at(l, h + 1))
                nc.scalar.activation(SDA[:, h, :], SDA[:, h, :], ACT.Exp, scale=-1.0).then_inc(decay_done.sem, 1)

            def diff_exp(l, i):
                act.wait_ge(ds_max.sem, ds_max.at(l, i + 1))
                m = i % 2
                for t, (a, b) in enumerate(((0, P), (P, 384))):
                    e = nc.scalar.activation(PR[:, m, a:b], ES[:, m, a:b], ACT.Exp, scale=0.125,
                                             bias=SM[:, 4 * m + t:4 * m + t + 1],
                                             accum_out=SM[:, 8 + 4 * m + t:8 + 4 * m + t + 1])
                e.then_inc(dp_done.sem, 1)

            def diff_turned(l, h):
                act.wait_ge(daT_done.sem, daT_done.at(l, h + 1))
                copy(AT[:, :], PS[:, 4, 0:384]).then_inc(daT_read.sem, 1)

            def diff_evac(l, h):
                act.wait_ge(do_done.sem, do_done.at(l, h + 1))
                copy(CAT[:, :, h * P:h * P + P], PS[:, 5, 0:256].rearrange("p (t n) -> p t n", t=2))\
                    .then_inc(do_read.sem, 1)

            def cat_high(l, i, c, b):
                act.wait_ge(catT_done.sem, catT_done.at(l, i + 1))
                copy(CH[:, c:c + 2, :], PS[:, b, :].rearrange("p (c n) -> p c n", c=2)).then_inc(cat_hi.sem, 1)

            def boundary(l, n, last_u):
                square(l, n, 0)
                square(l, n, 1)
                if n == 0:
                    split(l, last_u + 3)
                    kv_out(l, 0)
                turned(l, n + 1, 0)
                turned(l, n + 1, 1)
                if n > 0:
                    split(l, last_u + 3)

            def mix(l):
                split(l, U_SU)
                act.wait_ge(phase_ready.sem, phase_ready.at(l, 1))
                nc.scalar.activation(ESN[:, :, :], ESN[:, :, :], ACT.Sin, scale=TWO_PI).then_inc(act_link.sem, 1)
                nc.scalar.activation(EC[:, :, :], EC[:, :, :], ACT.Sin, scale=TWO_PI).then_inc(table_ready.sem, 1)
                split(l, U_MQ)
                for t in range(TT):
                    evac(l, None, 0, QK[:, t, 0:512], bank(t), proj_read, U_DQ + 1)
                split(l, U_MK)
                evac(l, None, 0, UT[:, :, :], PS[:, 6, :].rearrange("p (f n) -> p f n", f=2), ut_ready, U_SU)
                evac(l, gate_done, 1, GATES[:, :], PS[0:8, 7, 0:SEQ], gate_tok)
                act.wait_ge(cin_zero.sem, cin_zero.at(l, 1))
                split(l, U_DK)
                evac(l, None, 0, CIN[:, 0:2, 3:3 + SEQ], PS[:, 4, :].rearrange("p (f n) -> p f n", f=2), mqk_read, U_MQ)
                split(l, U_DK + 1)
                evac(l, None, 0, CIN[:, 2:4, 3:3 + SEQ], PS[:, 5, :].rearrange("p (f n) -> p f n", f=2), mqk_read, U_MK)
                act.wait_ge(gate_abs.sem, gate_abs.at(l, 1))
                nc.scalar.activation(ROW[:, 5, :], ROW[:, 5, :], ACT.Exp).then_inc(act_link.sem, 1)
                act.wait_ge(act_link.sem, act_link.at(l, 2))
                nc.scalar.activation(ROW[:, 5, :], ROW[:, 5, :], ACT.Ln, bias=ones_c[0:4, 0:1]).then_inc(gate_log.sem, 1)
                split(l, U_DV)
                split(l, U_DV + 1)
                for t in range(TT):
                    evac(l, None, 0, QK[:, t, 512:1024], bank(2 + t), proj_read, U_DK + 1)
                act.wait_ge(conv_done.sem, conv_done.at(l, 4))
                nc.scalar.activation(COUT[:, :, :], COUT[:, :, :], ACT.Silu).then_inc(silu_done.sem, 1)
                split(l, U_MM)
                split(l, U_MM + 1)
                for t in range(TT):
                    evac(l, None, 0, DV[:, t, :], bank(4 + t), proj_read, U_DV + 1)
                split(l, U_K[1])
                split(l, U_K[2])
                for t in range(TT):
                    act.wait_ge(unit_used.sem, unit_used.at(l, U_MM + 2))
                    copy(VA[:, t, :, 0:64], PS[:, t, 0:256].rearrange("p (h d) -> p h d", h=HEADS))
                    nc.scalar.activation(SIGO[:, t, :], PS[:, t, 256:512], ACT.Sigmoid).then_inc(proj_read.sem, 1)
                act.wait_ge(cols_done.sem, cols_done.at(l, 1))
                copy(SM[:, 184:200], PS[:, 4, 0:16]).then_inc(cols_read.sem, 1)
                act.wait_ge(cols_read.sem, cols_read.at(l, 1))
                nc.scalar.activation(SM[:, 192:200], SM[:, 192:200], ACT.Exp).then_inc(exp_m.sem, 1)
                split(l, U_V)
                kv_out(l, 1)
                tq_out(l, 0)
                decay(l, 0)
                decay(l, 1)
                split(l, U_V + 1)
                decay(l, 2)
                decay(l, 3)
                kv_out(l, 2)
                tq_out(l, 1)
                tq_out(l, 2)
                split(l, U_V + 2)
                tq_out(l, 3)
                act.wait_ge(ys_read.sem, ys_read.at(l, 1))
                nc.scalar.activation(UT[:, :, :], UT[:, :, :], ACT.Gelu_apprx_tanh).then_inc(gelu_done.sem, 1)
                diff_exp(l, 0)
                diff_exp(l, 1)
                split(l, U_V + 3)
                kv_out(l, 4)
                kv_out(l, 5)
                diff_turned(l, 0)
                diff_exp(l, 2)
                diff_exp(l, 3)
                act.wait_ge(glu_done.sem, glu_done.at(l, 1))
                for f in range(2):
                    g = nc.scalar.activation(ZX[:, 0, f, :], PS[:, 5, f * SEQ:f * SEQ + SEQ], ACT.Sigmoid,
                                             bias=PAR[:, P_GLUB + f:P_GLUB + f + 1])
                g.then_inc(glu_sig.sem, 1)
                split(l, U_WOUT[0], half=True)
                diff_evac(l, 0)
                act.wait_ge(c_hi_in.sem, c_hi_in.at(l, 1))
                copy(CH[:, 6:8, :], UT[:, :, :]).then_inc(c_hi.sem, 1)
                diff_turned(l, 1)
                diff_exp(l, 4)
                diff_exp(l, 5)
                split(l, U_WOUT[1], half=True)
                kv_out(l, 6)
                kv_out(l, 7)
                diff_evac(l, 1)
                diff_turned(l, 2)
                diff_exp(l, 6)
                diff_exp(l, 7)
                split(l, U_K[3])
                split(l, U_WOUT[2])
                diff_evac(l, 2)
                diff_turned(l, 3)
                diff_evac(l, 3)
                kv_out(l, 3)
                cat_high(l, 0, 4, 7)
                cat_high(l, 1, 0, 4)
                split(l, U_WOUT[3])
                split(l, U_WOUT[4])
                cat_high(l, 2, 2, 5)
                split(l, U_WQ)
                split(l, U_WQ + 1)

            def xattn(l):
                def probabilities(h):
                    act.wait_ge(xs_max.sem, xs_max.at(l, h + 1))
                    if h >= 2:
                        act.wait_ge(xpT_done.sem, xpT_done.at(l, h - 1))
                    for t in range(TT):
                        e = nc.scalar.activation(XP[:, h % 2, t, :], PS[:, h, t * SEQ:t * SEQ + SEQ], ACT.Exp,
                                                 scale=0.0625, bias=SM[:, 24 + 2 * h + t:25 + 2 * h + t],
                                                 accum_out=SM[:, 8 + 2 * h + t:9 + 2 * h + t])
                    e.then_inc(xp_done.sem, 1)

                def turned_p(h):
                    act.wait_ge(xpT_done.sem, xpT_done.at(l, h + 1))
                    if h >= 2:
                        act.wait_ge(xo_done.sem, xo_done.at(l, h - 1))
                    copy(XPT[:, h % 2, :, :], PS[:, 4 + h % 2, :].rearrange("p (m n) -> p m n", m=2))\
                        .then_inc(xpT_read.sem, 1)

                def high(h):
                    act.wait_ge(xo_done.sem, xo_done.at(l, h + 1))
                    copy(CH[:, 2 * h:2 * h + 2, :], PS[:, 6 + h % 2, :].rearrange("p (m n) -> p m n", m=2))\
                        .then_inc(xo_hi.sem, 1)

                for i in range(4):
                    evac(l, None, 0, QX[:, 2 * i:2 * i + 2, :], PS[:, 4 + i, :].rearrange("p (f n) -> p f n", f=2),
                         qx_read, U_WQ + i)
                    split(l, (U_WQ + 3, U_WO, U_WO + 1, U_WO + 2)[i], half=i in (1, 2))
                    if i > 1:
                        probabilities(i - 2)
                probabilities(2)
                turned_p(0)
                turned_p(1)
                probabilities(3)
                high(0)
                turned_p(2)
                high(1)
                turned_p(3)
                high(2)
                split(l, U_WO + 3)
                high(3)
                split(l, U_WO + 4)
                split(l, U_FFN[1])
                split(l, U_FFN[1] + 1)

            act.dma_start(MEMX[:, :, :], mem_in.rearrange("b (t p) d -> p (b t) d", p=P)).then_inc(mem_loaded.sem, 16)
            for i in range(4):
                act.wait_ge(xT_psum.sem, i + 1)
                t, half = i // 2, i % 2
                copy(MH[:, 4 * half:4 * half + 4, t * P:t * P + P], PS[:, i, :].rearrange("p (c n) -> p c n", c=4))\
                    .then_inc(xT_hi.sem, 1)
            with act.Fori(0, DEPTH) as l:
                ffn(l, 0)
                split(l, U_DQ)
                boundary(l, 0, U_FFN[0] + 32)
                mix(l)
                boundary(l, 1, U_WOUT[4])
                xattn(l)
                boundary(l, 2, U_WO + 4)
                ffn(l, 1)
                square(l, 3, 0)
                square(l, 3, 1)

        @block.vector
        def _(dve):
            v = nc.vector
            count = {"n": 0}
            layer = {}

            def link(ins):
                count["n"] += 1
                ins.then_inc(dve_link.sem, 1)
                dve.wait_ge(dve_link.sem, dve_link.at(layer["l"], count["n"]))

            def low(dst, full, hi):
                return v.tensor_tensor(dst, full, hi.bitcast(F32), ALU.subtract)

            def split(l, u, j=0, half=False):
                s = u % RING
                n = 1024 if half else 2048
                dve.wait_ge(split_hi.sem, split_hi.at(l, u + 1 + 3 * j))
                low(WL[s][:, 0:n], RAW[s][:, 0:n], WH[s][:, 0:n]).then_inc(split_lo.sem, 1)

            def rsqrt(dst, src, n, work, done=None):
                a, b = SM[:, work:work + n], SM[:, work + n:work + 2 * n]
                link(v.tensor_scalar(b.bitcast(I32), src.bitcast(I32), 1, None, ALU.logical_shift_right))
                link(v.tensor_scalar(dst.bitcast(I32), b.bitcast(I32), -1.0, 1597463007.0, ALU.mult, ALU.add))
                for i in range(3):
                    link(v.scalar_tensor_tensor(a, dst, -0.5, dst, ALU.mult, ALU.mult))
                    link(v.tensor_tensor(a, a, src, ALU.mult))
                    ins = v.scalar_tensor_tensor(dst, a, 1.5, dst, ALU.add, ALU.mult)
                    if i < 2 or done is None:
                        link(ins)
                    else:
                        ins.then_inc(done.sem, 1)

            def norm_sum(l, n, t, last_unit):
                c = (0.5 if n in (0, 3) else 1.0) / ALPHA
                if t == 0:
                    dve.wait_ge(y_half.sem, y_half.at(l, n + 1))
                else:
                    dve.wait_ge(unit_used.sem, unit_used.at(l, last_unit + 1))
                v.scalar_tensor_tensor(X[:, t, :], Y[:, t, :], c, X[:, t, :], ALU.mult, ALU.add,
                                       accum_out=SM[:, 16 + t:17 + t]).then_inc(ln_sum.sem, 1)
                dve.wait_ge(ln_sum.sem, ln_sum.at(l, TT * n + t + 1))
                v.tensor_scalar(SM[:, 18 + t:19 + t], SM[:, 16 + t:17 + t], -1.0 / D, None, ALU.mult)\
                    .then_inc(ln_mean.sem, 1)

            def norm_center(l, n, t):
                dve.wait_ge(ln_mean.sem, ln_mean.at(l, TT * n + t + 1))
                dve.wait_ge(gb_in.sem, gb_in.at(l, 32 * (n + 1)))
                v.scalar_tensor_tensor(XG[:, t, :], X[:, t, :], SM[:, 18 + t:19 + t], LNGB[:, 0, :],
                                       ALU.add, ALU.mult).then_inc(ln_center.sem, 1)

            def norm_scale(l, n, t):
                dve.wait_ge(ln_square.sem, ln_square.at(l, TT * n + t + 1))
                var, m, b = SM[:, 20 + t:21 + t], SM[:, 48 + t:49 + t], SM[:, 50 + t:51 + t]
                y, a = SM[:, 22 + t:23 + t], SM[:, 52 + t:53 + t]
                link(v.tensor_scalar(var, var, 1.0 / D, EPS / ALPHA ** 2, ALU.mult, ALU.add))
                v.tensor_scalar(m, var, -0.5, None, ALU.mult)
                link(v.tensor_scalar(b.bitcast(I32), var.bitcast(I32), 1, None, ALU.logical_shift_right))
                link(v.tensor_scalar(y.bitcast(I32), b.bitcast(I32), -1.0, 1597463007.0, ALU.mult, ALU.add))
                for _ in range(3):
                    link(v.scalar_tensor_tensor(a, y, y, m, ALU.mult, ALU.mult))
                    link(v.scalar_tensor_tensor(y, a, 1.5, y, ALU.add, ALU.mult))
                dve.wait_ge(ln_center.sem, ln_center.at(l, TT * n + t + 1))
                v.scalar_tensor_tensor(X[:, t, :], XG[:, t, :], y, LNGB[:, 1, :],
                                       ALU.mult, ALU.add).then_inc(x_ready.sem, 1)

            def turned(l, n, t):
                for half in range(2):
                    dve.wait_ge(xT_hi.sem, xT_hi.at(l, 4 * n + 2 * t + half + 1))
                    cs = slice(4 * half, 4 * half + 4)
                    low(XL[:, cs, t * P:t * P + P], PS[:, 4 + 2 * t + half, :].rearrange("p (c n) -> p c n", c=4),
                        XH[:, cs, t * P:t * P + P]).then_inc(xT_lo.sem, 1)

            def boundary(l, n, last_u):
                norm_sum(l, n, 0, last_u)
                norm_center(l, n, 0)
                norm_sum(l, n, 1, last_u)
                norm_scale(l, n, 0)
                norm_center(l, n, 1)
                if n == 0:
                    split(l, last_u + 3)
                turned(l, n + 1, 0)
                norm_scale(l, n, 1)
                turned(l, n + 1, 1)
                if n > 0:
                    split(l, last_u + 3)

            def h_mul(l, base, t):
                dve.wait_ge(sg_done.sem, sg_done.at(l, base + t))
                v.tensor_tensor(HB[:, t, :], SG[:, t, :], PS[:, 4 + t, FB:2 * FB], ALU.mult).then_inc(h_ready.sem, 1)

            def ffn(l, s):
                b = U_FFN[s]
                if s == 0:
                    split(l, b)
                    turned(l, 0, 0)
                    split(l, b + 1)
                    turned(l, 0, 1)
                    split(l, b + 2)
                h_mul(l, 22 * s + 1, 0)
                split(l, b + 3)
                h_mul(l, 22 * s + 1, 1)
                split(l, b + 4)

                def step(j, jj, last):
                    dve.wait_ge(hT_hi.sem, hT_hi.at(l, jj + (11 * s + 1)))
                    low(HL[:, :, :], PS[:, 6, :].rearrange("p (c n) -> p c n", c=2), HH[:, :, :])\
                        .then_inc(hT_lo.sem, 1)
                    split(l, b + 5, jj)
                    h_mul(l, jj * 2 + (22 * s + 3), 0)
                    h_mul(l, jj * 2 + (22 * s + 3), 1)
                    if not last:
                        split(l, b + 6, jj)
                        split(l, b + 7, jj)

                step(0, 0, False)
                if s == 0:
                    prepare_first(l)
                step(1, 1, False)
                if s == 0:
                    prepare_rest(l)
                with dve.Fori(2, BLOCKS - 2) as j:
                    step(j, j, False)
                step(BLOCKS - 2, BLOCKS - 2, True)
                if s == 0:
                    split(l, U_K[0])
                dve.wait_ge(hT_hi.sem, hT_hi.at(l, 11 * s + BLOCKS))
                low(HL2[:, :, :], PS[:, 6, :].rearrange("p (c n) -> p c n", c=2), HH2[:, :, :]).then_inc(hT_lo.sem, 1)

            def s5_turn_in(l, i):
                dve.wait_ge(bu_done.sem, bu_done.at(l, i + 1))
                if i == 0:
                    dve.wait_ge(table_ready.sem, table_ready.at(l, 1))
                if i >= 2:
                    dve.wait_ge(state_ready.sem, state_ready.at(l, i - 1))
                if i >= 1:
                    dve.wait_ge(z_ready.sem, z_ready.at(l, i))
                both = PS[:, 6 + i % 2, :].rearrange("p (c n) -> p c n", c=2)
                cos = EC[:, i:i + 1, :].to_broadcast([P, 2, SEQ])
                sin = ESN[:, i:i + 1, :].to_broadcast([P, 2, SEQ])
                v.tensor_tensor(ZW[:, :, :], both, cos, ALU.mult)
                v.tensor_tensor(ZT[:, :, :], both, sin, ALU.mult).then_inc(bu_read.sem, 1)
                dve.wait_ge(bu_read.sem, bu_read.at(l, i + 1))
                v.tensor_tensor(ZW[:, 0, :], ZW[:, 0, :], ZT[:, 1, :], ALU.add)
                link(v.tensor_tensor(ZW[:, 1, :], ZW[:, 1, :], ZT[:, 0, :], ALU.subtract))
                rad = CUR[:, R_RAD + i:R_RAD + i + 1].to_broadcast([P, SEQ])
                for part in range(2):
                    z = v.tensor_tensor_scan(ZS[:, i % 2, part, :], rad, ZW[:, part, :], 0.0, ALU.mult, ALU.add)
                z.then_inc(z_ready.sem, 1)

            def conv(l, half):
                dve.wait_ge(mqk_read.sem, mqk_read.at(l, half + 1))
                for f in range(2 * half, 2 * half + 2):
                    w = P_CW + 4 * f
                    link(v.tensor_scalar(COUT[:, f, :], CIN[:, f, 0:SEQ], PAR[:, w:w + 1],
                                         PAR[:, P_CB + f:P_CB + f + 1], ALU.mult, ALU.add))
                    for j in range(1, 4):
                        ins = v.scalar_tensor_tensor(COUT[:, f, :], CIN[:, f, j:j + SEQ], PAR[:, w + j:w + j + 1],
                                                     COUT[:, f, :], ALU.mult, ALU.add)
                        if j < 3:
                            link(ins)
                        else:
                            ins.then_inc(conv_done.sem, 1)

            def gates_in(l):
                dve.wait_ge(gateT_done.sem, gateT_done.at(l, 1))
                v.tensor_scalar(ROW[:, 2, :], PS[0:4, 7, 0:SEQ], PAR[0:4, P_GB:P_GB + 1], None, ALU.add)
                link(v.tensor_scalar(ROW[:, 4, :], PS[0:4, 7, SEQ:2 * SEQ], PAR[0:4, P_GB + 1:P_GB + 2], None, ALU.add))
                v.tensor_scalar(ROW[:, 3, :], ROW[:, 4, :], -1.0, None, ALU.mult).then_inc(gate_read.sem, 1)
                dve.wait_ge(gate_read.sem, gate_read.at(l, 1))
                link(v.tensor_tensor(ROW[:, 5, :], ROW[:, 3, :], ROW[:, 4, :], ALU.min))
                v.tensor_scalar(ROW[:, 4, :], ROW[:, 4, :], 0.0, None, ALU.min).then_inc(gate_abs.sem, 1)

            def gates_out(l):
                dve.wait_ge(gate_log.sem, gate_log.at(l, 1))
                link(v.tensor_tensor(ROW[:, 4, :], ROW[:, 4, :], ROW[:, 5, :], ALU.subtract))
                one = ones_c[0:4, 0:1].to_broadcast([4, SEQ])
                link(v.tensor_tensor_scan(ROW[:, 5, :], one, ROW[:, 4, :], 0.0, ALU.mult, ALU.add))
                link(v.tensor_tensor(ROW[:, 1, :], ROW[:, 2, :], ROW[:, 5, :], ALU.subtract))
                link(v.tensor_scalar(ROW[:, 4, :], ROW[:, 1, :], 0.0, None, ALU.mult))
                link(v.tensor_tensor_scan(ROW[:, 0, :], ROW[:, 1, :], ROW[:, 4, :], 0.0, ALU.max, ALU.max))
                v.scalar_tensor_tensor(ROW[:, 3, :], ROW[:, 0, :], -1.0, ROW[:, 5, :], ALU.mult, ALU.subtract)\
                    .then_inc(rows_ready.sem, 1)

            def decay_args(l, h):
                dve.wait_ge(mbc_done.sem, mbc_done.at(l, h // 2 + 1))
                if h == 0:
                    dve.wait_ge(roped.sem, roped.at(l, 2))
                dve.wait_ge(cols_read.sem, cols_read.at(l, 1))
                m = PS[:, 5 - h // 2, (h % 2) * SEQ:(h % 2 + 1) * SEQ]
                v.scalar_tensor_tensor(SDA[:, h, 0:SEQ], m, SM[:, 184 + h:185 + h], tri[:, 0:SEQ],
                                       ALU.subtract, ALU.add)
                v.scalar_tensor_tensor(SDA[:, h, SEQ:384], m[:, P:SEQ], SM[:, 188 + h:189 + h], tri[:, SEQ:384],
                                       ALU.subtract, ALU.add).then_inc(decay_in.sem, 1)

            def decay_scores(l, h):
                dve.wait_ge(decay_done.sem, decay_done.at(l, h + 1))
                dve.wait_ge(ms_done.sem, ms_done.at(l, h + 1))
                v.scalar_tensor_tensor(SDA[:, h, :], PS[:, 3 - h % 2, 0:384], 0.125, SDA[:, h, :],
                                       ALU.mult, ALU.mult).then_inc(msd_ready.sem, 1)

            def mlstm_sums(l):
                dve.wait_ge(num_done.sem, num_done.at(l, 2))
                dve.wait_ge(exp_m.sem, exp_m.at(l, 1))
                for t in range(TT):
                    n4 = PS[:, 3 - t, 0:260].rearrange("p (h d) -> p h d", h=HEADS)
                    den = SM[:, 120 + 4 * t:124 + 4 * t]
                    link(v.tensor_copy(den, n4[:, :, 64]))
                    link(v.scalar_tensor_tensor(den, den, -1.0, den, ALU.mult, ALU.max))
                    link(v.tensor_tensor(den, den, SM[:, 192 + 4 * t:196 + 4 * t], ALU.max))
                    link(v.reciprocal(den, den))
                    hv = CAT[:, t, 512:768].rearrange("p (h d) -> p h d", h=HEADS)
                    ins = v.tensor_tensor(hv, n4[:, :, 0:64], den.unsqueeze(2).to_broadcast([P, HEADS, 64]), ALU.mult)
                    if t == 0:
                        link(ins)
                    else:
                        ins.then_inc(num_read.sem, 1)
                        dve.wait_ge(num_read.sem, num_read.at(l, 1))

            def mlstm_stats(l):
                for t in range(TT):
                    link(v.tensor_tensor(ZB[:, t, :], CAT[:, t, 512:768], CAT[:, t, 512:768], ALU.mult))
                link(v.tensor_reduce(SM[:, 128:136].rearrange("p (t h) -> p t h", t=2),
                                     ZB[:, :, :].rearrange("p t (h d) -> p t h d", h=HEADS), AX, ALU.add))
                link(v.tensor_scalar(SM[:, 128:136], SM[:, 128:136], 1.0 / 64, EPS, ALU.mult, ALU.add))
                rsqrt(SM[:, 136:144], SM[:, 128:136], 8, 144, ml_scale)

            def diff_max(l, i):
                m = i % 2
                dve.wait_ge(ds_done.sem, ds_done.at(l, i + 1))
                if i > 0 and m == 0:
                    dve.wait_ge(daT_done.sem, daT_done.at(l, i // 2))
                v.tensor_tensor(ES[:, m, :], PS[:, 6 + m, 0:384], cmask, ALU.add).then_inc(ds_masked.sem, 1)
                dve.wait_ge(ds_masked.sem, ds_masked.at(l, i + 1))
                v.tensor_reduce(SM[:, 12 + 4 * m + 4:13 + 4 * m + 4], ES[:, m, 0:P], AX, ALU.max)
                link(v.tensor_reduce(SM[:, 13 + 4 * m + 4:14 + 4 * m + 4], ES[:, m, P:384], AX, ALU.max))
                v.tensor_scalar(SM[:, 4 * m:4 * m + 2], SM[:, 16 + 4 * m:18 + 4 * m], -0.125, None, ALU.mult)\
                    .then_inc(ds_max.sem, 1)

            def diff_combine(l, h):
                dve.wait_ge(dp_done.sem, dp_done.at(l, 2 * h + 2))
                sums = SM[:, 8:16].rearrange("p (m c) -> p m c", m=2)[:, :, 0:2]
                inv = SM[:, 24:28].rearrange("p (m c) -> p m c", m=2)
                link(v.reciprocal(inv, sums))
                link(v.tensor_scalar(SM[:, 26:28], SM[:, 26:28], CUR[:, R_NLAM:R_NLAM + 1], None, ALU.mult))
                for t, (a, b) in enumerate(((0, P), (P, 384))):
                    v.tensor_scalar(ES[:, 0, a:b], PR[:, 0, a:b], SM[:, 24 + t:25 + t], None, ALU.mult)\
                        .then_inc(dc_mid.sem, 1)
                for t, (a, b) in enumerate(((0, P), (P, 384))):
                    dve.wait_ge(dc_mid.sem, dc_mid.at(l, 2 * h + t + 1))
                    ins = v.scalar_tensor_tensor(ES[:, 0, a:b], PR[:, 1, a:b], SM[:, 26 + t:27 + t], ES[:, 0, a:b],
                                                 ALU.mult, ALU.add)
                ins.then_inc(da_ready.sem, 1)

            def diff_norm(l, i):
                dve.wait_ge(do_read.sem, do_read.at(l, 2 * i + 2))
                for h in range(2 * i, 2 * i + 2):
                    for t in range(TT):
                        ins = v.tensor_tensor_reduce(AQ[:, 2 * (h % 2) + t, :], CAT[:, t, h * P:h * P + P],
                                                     CAT[:, t, h * P:h * P + P], 1.0, 0.0, ALU.mult, ALU.add,
                                                     SM[:, 160 + 2 * h + t:161 + 2 * h + t])
                link(ins)
                m, q = SM[:, 160 + 4 * i:164 + 4 * i], SM[:, 168 + 4 * i:172 + 4 * i]
                link(v.tensor_scalar(m, m, 1.0 / P, EPS, ALU.mult, ALU.add))
                rsqrt(q, m, 4, 48)
                for h in range(2 * i, 2 * i + 2):
                    for t in range(TT):
                        o = CAT[:, t, h * P:h * P + P]
                        ins = v.scalar_tensor_tensor(o, o, SM[:, 168 + 2 * h + t:169 + 2 * h + t],
                                                     DG[:, :], ALU.mult, ALU.mult)
                ins.then_inc(a_ready.sem, 1)

            def cat_low(l, i, c, b):
                dve.wait_ge(cat_hi.sem, cat_hi.at(l, i + 1))
                low(CL[:, c:c + 2, :], PS[:, b, :].rearrange("p (c n) -> p c n", c=2), CH[:, c:c + 2, :])\
                    .then_inc(cat_lo.sem, 1)

            def mix(l):
                split(l, U_SU)
                dve.wait_ge(gw_hi.sem, gw_hi.at(l, 1))
                low(GWL[:, :, :], PAR[:, P_GW:P_GW + 64].rearrange("p (c g) -> p c g", c=KC), GWH[:, :, :])\
                    .then_inc(gw_lo.sem, 1)
                split(l, U_MQ)
                split(l, U_MK)
                gates_in(l)
                split(l, U_DK)
                conv(l, 0)
                split(l, U_DK + 1)
                s5_turn_in(l, 0)
                split(l, U_DV)
                conv(l, 1)
                gates_out(l)
                s5_turn_in(l, 1)
                split(l, U_DV + 1)
                s5_turn_in(l, 2)
                split(l, U_MM)
                s5_turn_in(l, 3)
                split(l, U_MM + 1)
                s5_turn_in(l, 4)
                split(l, U_K[1])
                s5_turn_in(l, 5)
                split(l, U_K[2])
                s5_turn_in(l, 6)
                split(l, U_V)
                s5_turn_in(l, 7)
                decay_args(l, 0)
                decay_args(l, 1)
                split(l, U_V + 1)
                decay_args(l, 2)
                decay_args(l, 3)
                split(l, U_V + 2)
                dve.wait_ge(state_used.sem, state_used.at(l, TILES))
                for f in range(2):
                    ins = v.scalar_tensor_tensor(UT[:, f, :], UT[:, f, :], PAR[:, P_D + f:P_D + f + 1],
                                                 PS[:, 2, f * SEQ:f * SEQ + SEQ], ALU.mult, ALU.add)
                    if f == 0:
                        link(ins)
                    else:
                        ins.then_inc(ys_read.sem, 1)
                diff_max(l, 0)
                diff_max(l, 1)
                split(l, U_V + 3)
                diff_combine(l, 0)
                decay_scores(l, 0)
                decay_scores(l, 1)
                diff_max(l, 2)
                diff_max(l, 3)
                split(l, U_WOUT[0], half=True)
                diff_combine(l, 1)
                dve.wait_ge(glu_sig.sem, glu_sig.at(l, 1))
                v.tensor_tensor(UT[:, :, :], ZX[:, 0, :, :], UT[:, :, :], ALU.mult).then_inc(c_hi_in.sem, 1)
                decay_scores(l, 2)
                decay_scores(l, 3)
                diff_max(l, 4)
                diff_max(l, 5)
                dve.wait_ge(c_hi.sem, c_hi.at(l, 1))
                low(CL[:, 6:8, :], UT[:, :, :], CH[:, 6:8, :]).then_inc(c_lo.sem, 1)
                split(l, U_WOUT[1], half=True)
                diff_combine(l, 2)
                mlstm_sums(l)
                diff_max(l, 6)
                diff_max(l, 7)
                mlstm_stats(l)
                diff_combine(l, 3)
                split(l, U_K[3])
                diff_norm(l, 0)
                split(l, U_WOUT[2])
                cat_low(l, 0, 4, 7)
                cat_low(l, 1, 0, 4)
                diff_norm(l, 1)
                split(l, U_WOUT[3])
                split(l, U_WOUT[4])
                cat_low(l, 2, 2, 5)
                split(l, U_WQ)
                split(l, U_WQ + 1)

            def xattn(l):
                def maximum(h):
                    dve.wait_ge(xs_done.sem, xs_done.at(l, h + 1))
                    link(v.tensor_reduce(SM[:, 32 + 2 * h:34 + 2 * h],
                                         PS[:, h, :].rearrange("p (t n) -> p t n", t=2), AX, ALU.max))
                    v.tensor_scalar(SM[:, 24 + 2 * h:26 + 2 * h], SM[:, 32 + 2 * h:34 + 2 * h], -0.0625, None,
                                    ALU.mult).then_inc(xs_max.sem, 1)

                def divide(h):
                    dve.wait_ge(xp_done.sem, xp_done.at(l, h + 1))
                    link(v.reciprocal(SM[:, 40 + 2 * h:42 + 2 * h], SM[:, 8 + 2 * h:10 + 2 * h]))
                    for t in range(TT):
                        ins = v.tensor_scalar(XP[:, h % 2, t, :], XP[:, h % 2, t, :],
                                              SM[:, 40 + 2 * h + t:41 + 2 * h + t], None, ALU.mult)
                    ins.then_inc(xp_norm.sem, 1)

                def output(h):
                    dve.wait_ge(xo_hi.sem, xo_hi.at(l, h + 1))
                    low(CL[:, 2 * h:2 * h + 2, :], PS[:, 6 + h % 2, :].rearrange("p (m n) -> p m n", m=2),
                        CH[:, 2 * h:2 * h + 2, :]).then_inc(xo_lo.sem, 1)

                for i in range(4):
                    split(l, (U_WQ + 3, U_WO, U_WO + 1, U_WO + 2)[i], half=i in (1, 2))
                    if i > 0:
                        maximum(i - 1)
                    if i > 1:
                        divide(i - 2)
                maximum(3)
                divide(2)
                divide(3)
                output(0)
                output(1)
                output(2)
                split(l, U_WO + 3)
                output(3)
                split(l, U_WO + 4)
                split(l, U_FFN[1])
                split(l, U_FFN[1] + 1)

            def exact_exp(dst, arg, n, w):
                k, r, p, i = (SW[:, w + n * a:w + n * a + n] for a in range(4))
                link(v.tensor_scalar(r, arg, -87.3, 88.7, ALU.max, ALU.min))
                link(v.tensor_scalar(k, r, 1.4426950408889634, MAGIC, ALU.mult, ALU.add))
                link(v.tensor_scalar(k, k, MAGIC, None, ALU.subtract))
                link(v.scalar_tensor_tensor(r, k, -0.693359375, r, ALU.mult, ALU.add))
                link(v.scalar_tensor_tensor(r, k, 2.12194440e-4, r, ALU.mult, ALU.add))
                link(v.tensor_scalar(p, r, 1.0 / 5040, None, ALU.mult))
                for f in (720, 120, 24, 6, 2, 1):
                    link(v.scalar_tensor_tensor(p, p, 1.0 / f, r, ALU.add, ALU.mult))
                link(v.tensor_scalar(p, p, 1.0, None, ALU.add))
                link(v.tensor_scalar(i.bitcast(I32), k, 127.0, None, ALU.add))
                link(v.tensor_scalar(i.bitcast(I32), i.bitcast(I32), 23, None, ALU.logical_shift_left))
                link(v.tensor_tensor(p, p, i, ALU.mult))
                link(v.tensor_scalar(r, arg, -87.3, None, ALU.is_ge))
                link(v.tensor_tensor(dst, p, r, ALU.mult))

            def prepare_first(l):
                dve.wait_ge(param_in.sem, param_in.at(l, 16))
                aim = PAR[:, P_AIM:P_AIM + 8]
                th, ph, w = SW[:, 48:56], SW[:, 56:64], SW[:, 64:72]
                v.tensor_copy(SW[:, 16:24], PAR[:, P_LST:P_LST + 8])
                dl = PAR[:, P_DL:P_DL + 256].rearrange("p (i two d) -> p i two d", two=2, d=64)
                pr = SW[:, 144:272].rearrange("p (i d) -> p i d", d=64)
                link(v.tensor_tensor(pr, dl[:, :, 0, :], dl[:, :, 1, :], ALU.mult))
                link(v.tensor_reduce(SW[:, 24:26], pr, AX, ALU.add))
                exact_exp(SW[:, 32:42], SW[:, 16:26], 10, 96)
                link(v.tensor_tensor(th, aim, SW[:, 32:40], ALU.mult))
                link(v.tensor_scalar(ph, th, 0.15915494309189535, MAGIC, ALU.mult, ALU.add))
                link(v.tensor_scalar(ph, ph, MAGIC, None, ALU.subtract))
                for part in (6.28125, 0.0019350051879882812, 3.0199159819e-7):
                    link(v.scalar_tensor_tensor(th, ph, -part, th, ALU.mult, ALU.add))
                link(v.tensor_scalar(ph, th, 0.15915494309189535, None, ALU.mult))
                v.tensor_copy(SW[:, 0:8], ph)
                link(v.tensor_scalar(SW[:, 8:16], ph, 0.25, None, ALU.add))
                link(v.tensor_scalar(SW[:, 72:88], SW[:, 0:16], MAGIC, None, ALU.add))
                link(v.tensor_scalar(SW[:, 72:88], SW[:, 72:88], MAGIC, None, ALU.subtract))
                v.tensor_tensor(SW[:, 0:16], SW[:, 0:16], SW[:, 72:88], ALU.subtract).then_inc(prep_phase.sem, 1)
                link(v.tensor_scalar(w, ph, MAGIC12, None, ALU.add))
                link(v.tensor_scalar(w, w, MAGIC12, None, ALU.subtract))
                v.tensor_copy(CUR[:, R_PHI:R_PHI + 8], w)
                v.tensor_tensor(CUR[:, R_PLO:R_PLO + 8], ph, w, ALU.subtract)

            def prepare_rest(l):
                are, aim = PAR[:, P_ARE:P_ARE + 8], PAR[:, P_AIM:P_AIM + 8]
                th, w = SW[:, 304:312], SW[:, 312:320]
                link(v.tensor_tensor(th, are, SW[:, 32:40], ALU.mult))
                exact_exp(w, th, 8, 96)
                v.tensor_copy(CUR[:, R_RAD:R_RAD + 8], w)
                dve.wait_ge(prep_sin.sem, prep_sin.at(l, 1))
                nr, ni, den, q, q2 = (SW[:, 272 + 8 * i:280 + 8 * i] for i in (0, 1, 2, 3, 6))
                v.tensor_tensor(ni, w, SW[:, 0:8], ALU.mult)
                link(v.tensor_tensor(nr, w, SW[:, 8:16], ALU.mult))
                link(v.tensor_scalar(nr, nr, -1.0, None, ALU.add))
                v.tensor_tensor(den, are, are, ALU.mult)
                link(v.tensor_tensor(q, aim, aim, ALU.mult))
                link(v.tensor_tensor(den, den, q, ALU.add))
                link(v.reciprocal(den, den))
                v.tensor_tensor(q, nr, are, ALU.mult)
                link(v.tensor_tensor(q2, ni, aim, ALU.mult))
                link(v.tensor_tensor(q, q, q2, ALU.add))
                link(v.tensor_tensor(CUR[:, R_FRE:R_FRE + 8], q, den, ALU.mult))
                v.tensor_tensor(q, ni, are, ALU.mult)
                link(v.tensor_tensor(q2, nr, aim, ALU.mult))
                link(v.tensor_tensor(q, q, q2, ALU.subtract))
                v.tensor_tensor(CUR[:, R_FIM:R_FIM + 8], q, den, ALU.mult)
                dve.wait_ge(const_rest.sem, 16)
                li = kst[:, K_LAM:K_LAM + 2 * DEPTH].rearrange("p (a l) -> p l a", a=2)
                link(v.tensor_copy(SW[:, 328:330], li[:, l, :]))
                link(v.tensor_tensor(w[:, 0:1], SW[:, 41:42], SW[:, 40:41], ALU.subtract))
                v.tensor_tensor(CUR[:, R_NLAM:R_NLAM + 1], w[:, 0:1], SW[:, 328:329], ALU.subtract)
                v.tensor_scalar(DG[:, :], PAR[:, P_DG:P_DG + P], SW[:, 329:330], None, ALU.mult)\
                    .then_inc(cur_ready.sem, 1)

            dve.sem_inc(split_lo.sem, RING)
            v.memset(ones_c[:, :], 1.0)
            v.memset(VA[:, :, :, :], 1.0)
            dve.wait_ge(x_loaded.sem, 16)
            dve.sem_inc(x_ready.sem, TT)
            for i in range(4):
                t, half = i // 2, i % 2
                dve.wait_ge(xT_hi.sem, i + 1)
                low(ML[:, 4 * half:4 * half + 4, t * P:t * P + P], PS[:, i, :].rearrange("p (c n) -> p c n", c=4),
                    MH[:, 4 * half:4 * half + 4, t * P:t * P + P]).then_inc(xT_lo.sem, 1)
            with dve.Fori(0, DEPTH) as l:
                layer["l"] = l
                v.memset(CIN[:, :, 0:3], 0.0).then_inc(cin_zero.sem, 1)
                ffn(l, 0)
                split(l, U_DQ)
                boundary(l, 0, U_FFN[0] + 32)
                mix(l)
                boundary(l, 1, U_WOUT[4])
                xattn(l)
                boundary(l, 2, U_WO + 4)
                ffn(l, 1)
                norm_sum(l, 3, 0, U_FFN[1] + 32)
                norm_center(l, 3, 0)
                norm_sum(l, 3, 1, U_FFN[1] + 32)
                norm_scale(l, 3, 0)
                norm_center(l, 3, 1)
                norm_scale(l, 3, 1)
            assert count["n"] == DVE_LINKS, count["n"]

        @block.gpsimd
        def _(pool):
            g = nc.gpsimd
            count = {"n": 0}
            layer = {}

            def link(ins):
                count["n"] += 1
                ins.then_inc(pool_link.sem, 1)
                pool.wait_ge(pool_link.sem, pool_link.at(layer["l"], count["n"]))
                pool.sem_inc(waits_apart.sem, 1)

            def load_gb(l, n):
                f = l * 4 + n
                pool.dma_start(LNGB[:, 0, :], lng_v[f].partition_broadcast(P)).then_inc(gb_in.sem, 16)
                pool.dma_start(LNGB[:, 1, :], lnb_v[f].partition_broadcast(P)).then_inc(gb_in.sem, 16)

            def tables(l):
                pool.wait_ge(const_rest.sem, 16)
                pool.wait_ge(cur_ready.sem, cur_ready.at(l, 1))
                pool.sem_inc(waits_apart.sem, 1)
                for i in range(TILES):
                    s, c = ESN[:, i, :], EC[:, i, :]
                    link(g.tensor_scalar(s, iota, CUR[:, R_PHI + i:R_PHI + i + 1], None, ALU.mult))
                    g.tensor_scalar(c, iota, CUR[:, R_PLO + i:R_PLO + i + 1], None, ALU.mult)
                    link(g.tensor_scalar(EF[:, :], s, MAGIC, MAGIC, ALU.add, ALU.subtract))
                    link(g.tensor_tensor(s, s, EF[:, :], ALU.subtract))
                    link(g.tensor_tensor(s, s, c, ALU.add))
                for i in range(TILES):
                    s, c = ESN[:, i, :], EC[:, i, :]
                    link(g.tensor_scalar(c, s, 0.25, None, ALU.add))
                    link(g.tensor_scalar(EF[:, :], c, MAGIC, MAGIC, ALU.add, ALU.subtract))
                    link(g.tensor_tensor(c, c, EF[:, :], ALU.subtract))
                    link(g.tensor_scalar(EF[:, :], s, MAGIC, MAGIC, ALU.add, ALU.subtract))
                    ins = g.tensor_tensor(s, s, EF[:, :], ALU.subtract)
                    if i < TILES - 1:
                        link(ins)
                    else:
                        ins.then_inc(phase_ready.sem, 1)

            def scale_c(l):
                pool.wait_ge(param_in.sem, param_in.at(l, 16))
                cre = PAR[:, P_C:P_C + 256].rearrange("p (i c) -> p i c", i=TILES)
                cim = PAR[:, P_C + 256:P_C + 512].rearrange("p (i c) -> p i c", i=TILES)
                fre = CUR[:, R_FRE:R_FRE + 8].unsqueeze(2).to_broadcast([P, TILES, 32])
                fim = CUR[:, R_FIM:R_FIM + 8].unsqueeze(2).to_broadcast([P, TILES, 32])
                w = EF[:, 0:256].rearrange("p (i c) -> p i c", i=TILES)
                link(g.tensor_tensor(CP[:, 0], cre, fre, ALU.mult))
                link(g.tensor_tensor(w, cim, fim, ALU.mult))
                link(g.tensor_tensor(CP[:, 0], CP[:, 0], w, ALU.subtract))
                link(g.tensor_tensor(CP[:, 1], cre, fim, ALU.mult))
                link(g.tensor_tensor(w, cim, fre, ALU.mult))
                link(g.tensor_tensor(CP[:, 1], CP[:, 1], w, ALU.add))
                g.tensor_scalar(CP[:, 1], CP[:, 1], -1.0, None, ALU.mult).then_inc(cp_ready.sem, 1)

            def rope(l, part):
                pool.wait_ge(proj_read.sem, proj_read.at(l, 2 * part + 2))
                for t in range(TT):
                    src = QK[:, t, 512 * part:512 * part + 512].rearrange("p (g two d) -> p g two d", g=8, two=2)
                    dst = RO[:, t, 512 * part:512 * part + 512].rearrange("p (g two d) -> p g two d", g=8, two=2)
                    w = PW[:, :].rearrange("p (g d) -> p g d", g=8)
                    cos = kst[:, K_COS + 32 * t:K_COS + 32 * t + 32].unsqueeze(1).to_broadcast([P, 8, 32])
                    sin = kst[:, K_SIN + 32 * t:K_SIN + 32 * t + 32].unsqueeze(1).to_broadcast([P, 8, 32])
                    link(g.tensor_tensor(dst[:, :, 0, :], src[:, :, 0, :], cos, ALU.mult))
                    link(g.tensor_tensor(w, src[:, :, 1, :], sin, ALU.mult))
                    link(g.tensor_tensor(dst[:, :, 0, :], dst[:, :, 0, :], w, ALU.subtract))
                    link(g.tensor_tensor(dst[:, :, 1, :], src[:, :, 1, :], cos, ALU.mult))
                    link(g.tensor_tensor(w, src[:, :, 0, :], sin, ALU.mult))
                    ins = g.tensor_tensor(dst[:, :, 1, :], dst[:, :, 1, :], w, ALU.add)
                    if t == 0:
                        link(ins)
                    else:
                        ins.then_inc(roped.sem, 1)

            def turn_back(l, i):
                pool.wait_ge(z_ready.sem, z_ready.at(l, i + 1))
                if i >= 2:
                    pool.wait_ge(state_used.sem, state_used.at(l, i - 1))
                z = ZS[:, i % 2]
                x = ZX[:, i % 2]
                cos = EC[:, i:i + 1, :].to_broadcast([P, 2, SEQ])
                sin = ESN[:, i:i + 1, :].to_broadcast([P, 2, SEQ])
                g.tensor_tensor(x, z, cos, ALU.mult)
                link(g.tensor_tensor(z, z, sin, ALU.mult))
                g.tensor_tensor(x[:, 0, :], x[:, 0, :], z[:, 1, :], ALU.subtract)
                g.tensor_tensor(x[:, 1, :], x[:, 1, :], z[:, 0, :], ALU.add).then_inc(state_ready.sem, 1)

            def mlstm_scale(l):
                pool.wait_ge(ml_scale.sem, ml_scale.at(l, 1))
                pool.sem_inc(waits_apart.sem, 1)
                for t in range(TT):
                    o = CAT[:, t, 512:768]
                    hv = o.rearrange("p (h d) -> p h d", h=HEADS)
                    scale = SM[:, 136 + 4 * t:140 + 4 * t].unsqueeze(2).to_broadcast([P, HEADS, 64])
                    link(g.tensor_tensor(hv, hv, scale, ALU.mult))
                    link(g.tensor_tensor(o, o, PAR[:, P_MG:P_MG + 256], ALU.mult))
                    ins = g.tensor_tensor(o, o, SIGO[:, t, :], ALU.mult)
                    if t == 0:
                        link(ins)
                    else:
                        ins.then_inc(b_ready.sem, 1)

            pool.dma_start(kst[:, P:K_END], const[:, P:K_END]).then_inc(const_rest.sem, 16)
            with pool.Fori(0, DEPTH) as l:
                layer["l"] = l
                pool.wait_ge(x_ready.sem, x_ready.at(l, 0))
                pool.dma_start(PAR[:, :], par[l]).then_inc(param_in.sem, 16)
                load_gb(l, 0)
                pool.wait_ge(xT_psum.sem, 4)
                tables(l)
                scale_c(l)
                rope(l, 0)
                turn_back(l, 0)
                rope(l, 1)
                for i in range(1, TILES):
                    turn_back(l, i)
                pool.wait_ge(state_used.sem, state_used.at(l, TILES))
                load_gb(l, 1)
                mlstm_scale(l)
                pool.wait_ge(x_ready.sem, x_ready.at(l, 4))
                load_gb(l, 2)
                pool.wait_ge(x_ready.sem, x_ready.at(l, 6))
                load_gb(l, 3)
            assert count["n"] == POOL_LINKS, count["n"]


_INS = ["x", "mem", "ffn_w_gate", "ffn_w_up", "ffn_w_down", "ln_g", "ln_b", "w_in", "w_out", "xattn_wq",
        "xattn_wkv", "xattn_wo"]


def constants():
    k = np.zeros((P, K_END), np.float32)
    k[:, K_ID:K_ID + P] = np.eye(P)
    q = np.arange(P)
    k[:, K_CM:K_CM + P] = np.where(q[None, :] // CHUNK <= q[:, None] // CHUNK, 0.0, -1e30)
    k[:, K_CM + 256:K_CM + 384] = k[:, K_CM:K_CM + P]
    k[:, K_TRI:K_TRI + P] = np.where(q[:, None] > q[None, :], 1e30, 0.0)
    k[:, K_TRI + 256:K_TRI + 384] = k[:, K_TRI:K_TRI + P]
    inv = np.float32(10000.0) ** (-np.arange(0, 64, 2, dtype=np.float32) / np.float32(64))
    ang = np.arange(SEQ, dtype=np.float32)[:, None] * inv[None, :].astype(np.float32)
    for t in range(TT):
        k[:, K_COS + 32 * t:K_COS + 32 * t + 32] = np.cos(ang[t * P:t * P + P])
        k[:, K_SIN + 32 * t:K_SIN + 32 * t + 32] = np.sin(ang[t * P:t * P + P])
    k[:, K_IOTA:K_IOTA + SEQ] = np.arange(SEQ)
    k[:, K_LAM:K_LAM + DEPTH] = LAMBDA_INIT
    k[:, K_LAM + DEPTH:K_LAM + 2 * DEPTH] = [1.0 - v for v in LAMBDA_INIT]
    for h in range(HEADS):
        k[h, K_SEL + h * P:K_SEL + h * P + P] = 1.0
    return k


def lay_out(a):
    p = np.zeros((DEPTH, P, P_END), np.float32)
    for l in range(DEPTH):
        for g in range(GROUPS):
            tile, par = g // 2, g % 2
            row = (tile % 4) * 32 + par * 16
            for part, (b, c) in enumerate((("s5_b_re", "s5_c_re"), ("s5_b_im", "s5_c_im"))):
                col = P_B + part * 256 + (tile // 4) * P + par * 64
                p[l, row:row + 16, col:col + 64] = a[b][l, g].T
                col = P_C + part * 256 + tile * 32 + par * 16
                p[l, par * 64:par * 64 + 64, col:col + 16] = a[c][l, g].T
            for col, name in ((P_ARE, "s5_a_re"), (P_AIM, "s5_a_im"), (P_LST, "s5_log_step")):
                p[l, par * 64:par * 64 + 64, col + tile] = a[name][l, g]
        p[l, :, P_GLU:P_GLU + 512] = a["s5_glu_w"][l].reshape(2, P, 256).transpose(1, 0, 2).reshape(P, 512)
        p[l, :, P_GLUB:P_GLUB + 2] = a["s5_glu_b"][l].reshape(2, P).T
        p[l, :, P_D:P_D + 2] = a["s5_d"][l].reshape(2, P).T
        p[l, :, P_CW:P_CW + 16] = a["conv_w"][l].reshape(4, 4, P).transpose(2, 1, 0).reshape(P, 16)
        p[l, :, P_CB:P_CB + 4] = a["conv_b"][l].reshape(4, P).T
        p[l, 0:4, P_GB:P_GB + 2] = a["mlstm_gate_b"][l].reshape(2, 4).T
        gw = a["w_in"][l][:, 2560:2568].reshape(KC, P, 8).transpose(1, 0, 2)
        p[l, :, P_GW:P_GW + 64] = gw.reshape(P, 64)
        p[l, :, P_DG:P_DG + P] = a["diff_norm_g"][l][None]
        p[l, :, P_MG:P_MG + 256] = a["mlstm_norm_g"][l][None]
        p[l, :, P_DL:P_DL + 256] = a["diff_lambda"][l].reshape(1, 256)
    return p


def kernel(**inputs):
    import concourse.bacc as bacc
    from concourse.bass_utils import run_bass_kernel_spmd

    a = {k: np.asarray(v) for k, v in inputs.items()}
    arrays = {n: np.ascontiguousarray(a[n]) for n in _INS}
    arrays.update(params=lay_out(a), constants=constants())
    nc = bacc.Bacc("TRN2", target_bir_lowering=False, num_devices=1)
    args = [nc.dram_tensor(f"in_{n}", v.shape, mybir.dt.from_np(v.dtype), kind="ExternalInput").ap()
            for n, v in arrays.items()]
    out = nc.dram_tensor("out", (1, SEQ, D), F32, kind="ExternalOutput").ap()
    build(nc, *args, out)
    r = run_bass_kernel_spmd(nc, [{f"in_{n}": v for n, v in arrays.items()}], core_ids=[0])
    return r.results[0]["out"]
```
